# Optimizing a Trainium2 kernel written in Bass

```python
import jax, jax.numpy as jnp
from jax import lax
import numpy as np
import jax
import jax.numpy as jnp

D_MODEL = 1024
BATCH = 1
SEQ = 256
DEPTH = 2

GRID_W = 64
CTX_LEN = 256
N_MOD = 9
NA_HEADS = 8
HEAD_DIM = 64
NA_WIDTH = NA_HEADS * HEAD_DIM
NA_KH = 8
NA_KW = 16
POOL_GROUPS = 4
POOL_CH = 128
POOL_WIDTH = POOL_GROUPS * POOL_CH
POOL_WINDOWS = (2, 4, 8, 16)
MIX_WIDTH = NA_WIDTH + POOL_WIDTH
IN_WIDTH = 3 * NA_WIDTH + POOL_WIDTH
D_FF = 2816
ROPE_THETA = 10000.0
ROPE_PAIRS = HEAD_DIM // 4
RMS_EPS = 1e-6
NEG_INF = -1e30


def rms_norm(x, g):
    xf = x.astype(jnp.float32)
    y = xf * lax.rsqrt(jnp.mean(xf * xf, axis=-1, keepdims=True) + RMS_EPS)
    return (y * g.astype(jnp.float32)).astype(x.dtype)

def modulate(h, shift, scale):
    return h * (1.0 + scale) + shift

def mod_vectors(cvec, w_mod, b_mod):
    m = jax.nn.silu(cvec) @ w_mod + b_mod
    return jnp.split(m, N_MOD, axis=-1)

def swiglu(h, w_gate_up, w_down):
    gate, up = jnp.split(h @ w_gate_up, 2, axis=-1)
    return (jax.nn.silu(gate) * up) @ w_down

def sandwich_ffn(x, w_gate_up, w_down, g_pre, g_post, shift, scale, gate):
    h = modulate(rms_norm(x, g_pre), shift, scale)
    return x + 0.5 * gate * rms_norm(swiglu(h, w_gate_up, w_down), g_post)

def axial_rope(x, rows):
    seq = rows * GRID_W
    t = jnp.arange(seq)
    inv = ROPE_THETA ** (-jnp.arange(ROPE_PAIRS, dtype=jnp.float32) / ROPE_PAIRS)

    def rot(xa, pos):
        ang = pos.astype(jnp.float32)[:, None] * inv
        cos = jnp.cos(ang)[:, None, :]
        sin = jnp.sin(ang)[:, None, :]
        x1, x2 = jnp.split(xa, 2, axis=-1)
        return jnp.concatenate([x1 * cos - x2 * sin, x2 * cos + x1 * sin], axis=-1)

    xr, xc = jnp.split(x.astype(jnp.float32), 2, axis=-1)
    return jnp.concatenate([rot(xr, t // GRID_W), rot(xc, t % GRID_W)], axis=-1).astype(x.dtype)

def neighbourhood_attention(q, k, v, kc, vc, rpb, rows):
    b, s, h, dh = q.shape
    kh = min(NA_KH, rows)
    scale = dh ** -0.5
    q = q.reshape(b, rows, GRID_W, h, dh)
    k = k.reshape(b, rows, GRID_W, h, dh)
    v = v.reshape(b, rows, GRID_W, h, dh)
    r = np.arange(rows)
    row_start = np.clip(r - kh // 2, 0, rows - kh)
    row_idx = row_start[:, None] + np.arange(kh)[None, :]
    k_blk = k[:, row_idx]
    v_blk = v[:, row_idx]
    j = np.arange(GRID_W)
    col_start = np.clip(j - NA_KW // 2, 0, GRID_W - NA_KW)
    col_valid = (j[None, :] >= col_start[:, None]) & (j[None, :] < col_start[:, None] + NA_KW)
    dr = row_idx - r[:, None]
    dc = np.clip(j[None, :] - j[:, None] + NA_KW - 1, 0, 2 * NA_KW - 2)
    bias = rpb[:, dr + NA_KH - 1]
    bias = bias[..., dc]
    bias = jnp.transpose(bias, (0, 1, 3, 2, 4)).astype(jnp.float32)
    s_loc = jnp.einsum('brqhd,brkchd->bhrqkc', q, k_blk, preferred_element_type=jnp.float32) * scale
    s_loc = jnp.where(col_valid[:, None, :], s_loc + bias, NEG_INF)
    s_ctx = jnp.einsum('brqhd,bkhd->bhrqk', q, kc, preferred_element_type=jnp.float32) * scale
    n_loc = kh * GRID_W
    scores = jnp.concatenate([s_loc.reshape(b, h, rows, GRID_W, n_loc), s_ctx], axis=-1)
    p = jax.nn.softmax(scores, axis=-1).astype(v.dtype)
    p_loc = p[..., :n_loc].reshape(b, h, rows, GRID_W, kh, GRID_W)
    p_ctx = p[..., n_loc:]
    o = jnp.einsum('bhrqkc,brkchd->brqhd', p_loc, v_blk) + jnp.einsum('bhrqk,bkhd->brqhd', p_ctx, vc)
    return o.reshape(b, s, h * dh)

def context_attention(q, k, v):
    b, l, h, dh = q.shape
    sc = jnp.einsum('bqhd,bkhd->bhqk', q, k, preferred_element_type=jnp.float32) * dh ** -0.5
    p = jax.nn.softmax(sc, axis=-1).astype(v.dtype)
    return jnp.einsum('bhqk,bkhd->bqhd', p, v).reshape(b, l, h * dh)

def pool_mix(u, w_pool, pool_scale):
    length = u.shape[-2]
    ug = u.reshape(u.shape[:-1] + (POOL_GROUPS, POOL_CH))
    uf = ug.astype(jnp.float32)
    cs = jnp.cumsum(uf, axis=-3)
    pad = [(0, 0)] * cs.ndim
    pad[-3] = (1, 0)
    cs = jnp.pad(cs, pad)
    t = np.arange(length)
    outs = []
    for g, w in enumerate(POOL_WINDOWS):
        lo = np.clip(t - w // 2, 0, length)
        hi = np.clip(t - w // 2 + w, 0, length)
        cnt = (hi - lo).astype(np.float32)[:, None]
        csg = cs[..., g, :]
        outs.append((jnp.take(csg, hi, axis=-2) - jnp.take(csg, lo, axis=-2)) / cnt)
    pooled = jnp.stack(outs, axis=-2)
    d = (pooled - uf).astype(u.dtype)
    y = jnp.einsum('...gc,gcd->...gd', d, w_pool) * pool_scale.reshape(POOL_GROUPS, POOL_CH)
    return y.reshape(u.shape)

def token_mix(hx, hc, w_in, w_out, rpb, w_pool, pool_scale, with_ctx_out):
    b, s, _ = hx.shape
    rows = s // GRID_W
    l = hc.shape[1]
    qx, kx, vx, ux = jnp.split(hx @ w_in, [NA_WIDTH, 2 * NA_WIDTH, 3 * NA_WIDTH], axis=-1)
    if with_ctx_out:
        qc, kc, vc, uc = jnp.split(hc @ w_in, [NA_WIDTH, 2 * NA_WIDTH, 3 * NA_WIDTH], axis=-1)
    else:
        kc, vc = jnp.split(hc @ w_in[:, NA_WIDTH:3 * NA_WIDTH], 2, axis=-1)
    heads = lambda t, n: t.reshape(b, n, NA_HEADS, HEAD_DIM)
    qx = axial_rope(heads(qx, s), rows)
    kx = axial_rope(heads(kx, s), rows)
    kc_h, vc_h = heads(kc, l), heads(vc, l)
    na_x = neighbourhood_attention(qx, kx, heads(vx, s), kc_h, vc_h, rpb, rows)
    pool_x = pool_mix(ux.reshape(b, rows, GRID_W, POOL_WIDTH), w_pool, pool_scale).reshape(b, s, POOL_WIDTH)
    out_x = jnp.concatenate([na_x, pool_x], axis=-1) @ w_out
    if with_ctx_out:
        na_c = context_attention(heads(qc, l), kc_h, vc_h)
        pool_c = pool_mix(uc, w_pool, pool_scale)
        out_c = jnp.concatenate([na_c, pool_c], axis=-1) @ w_out
        return out_x, out_c
    return out_x, None

def first_inputs(seed: int = 0) -> dict:
    key = jax.random.key(seed)
    ks = jax.random.split(key, 14)
    nrm = jax.random.normal
    f32 = jnp.float32
    return {
        'x': nrm(ks[0], (BATCH, SEQ, D_MODEL), f32),
        'c': nrm(ks[1], (BATCH, D_MODEL), f32),
        'ctx': nrm(ks[2], (BATCH, CTX_LEN, D_MODEL), f32),
        'c_ctx': nrm(ks[3], (D_MODEL,), f32),
        'w_mod': nrm(ks[4], (DEPTH, D_MODEL, N_MOD * D_MODEL), f32) * (0.5 * D_MODEL ** -0.5),
        'b_mod': nrm(ks[5], (DEPTH, N_MOD * D_MODEL), f32) * 0.01,
        'norm_g': 1.0 + 0.05 * nrm(ks[6], (DEPTH, 6, D_MODEL), f32),
        'w_ffn_gate_up': nrm(ks[7], (DEPTH, 2, D_MODEL, 2 * D_FF), f32) * D_MODEL ** -0.5,
        'w_ffn_down': nrm(ks[8], (DEPTH, 2, D_FF, D_MODEL), f32) * D_FF ** -0.5,
        'w_in': nrm(ks[9], (DEPTH, D_MODEL, IN_WIDTH), f32) * D_MODEL ** -0.5,
        'w_out': nrm(ks[10], (DEPTH, MIX_WIDTH, D_MODEL), f32) * MIX_WIDTH ** -0.5,
        'na_rpb': nrm(ks[11], (DEPTH, NA_HEADS, 2 * NA_KH - 1, 2 * NA_KW - 1), f32) * 0.1,
        'w_pool': nrm(ks[12], (DEPTH, POOL_GROUPS, POOL_CH, POOL_CH), f32) * POOL_CH ** -0.5,
        'pool_scale': 1.0 + 0.05 * nrm(ks[13], (DEPTH, POOL_WIDTH), f32),
    }

def first_block(x, c, ctx, c_ctx, w_mod, b_mod, norm_g, w_ffn_gate_up, w_ffn_down, w_in, w_out, na_rpb, w_pool, pool_scale):
    for l in range(DEPTH):
        last = l == DEPTH - 1
        mx = [m[:, None, :] for m in mod_vectors(c, w_mod[l], b_mod[l])]
        mc = mod_vectors(c_ctx, w_mod[l], b_mod[l])
        g = norm_g[l]
        x = sandwich_ffn(x, w_ffn_gate_up[l, 0], w_ffn_down[l, 0], g[0], g[1], mx[0], mx[1], mx[2])
        ctx = sandwich_ffn(ctx, w_ffn_gate_up[l, 0], w_ffn_down[l, 0], g[0], g[1], mc[0], mc[1], mc[2])
        hx = modulate(rms_norm(x, g[2]), mx[3], mx[4])
        hc = modulate(rms_norm(ctx, g[2]), mc[3], mc[4])
        out_x, out_c = token_mix(hx, hc, w_in[l], w_out[l], na_rpb[l], w_pool[l], pool_scale[l], not last)
        x = x + mx[5] * rms_norm(out_x, g[3])
        x = sandwich_ffn(x, w_ffn_gate_up[l, 1], w_ffn_down[l, 1], g[4], g[5], mx[6], mx[7], mx[8])
        if not last:
            ctx = ctx + mc[5] * rms_norm(out_c, g[3])
            ctx = sandwich_ffn(ctx, w_ffn_gate_up[l, 1], w_ffn_down[l, 1], g[4], g[5], mc[6], mc[7], mc[8])
    return x


N_MIXERS = 2
N_ATTN_LAYERS = (DEPTH + 1) // 2
N_MLSTM_LAYERS = DEPTH // 2

DIL_CONFIGS = ((128, 1), (512, 4), (2048, 16))
N_GROUPS = len(DIL_CONFIGS)
ATTN_HEADS = 8
ATTN_HEAD_DIM = 128
ATTN_WIDTH = ATTN_HEADS * ATTN_HEAD_DIM
ATTN_IN_WIDTH = N_GROUPS * 3 * ATTN_WIDTH
ROT_DIM = ATTN_HEAD_DIM // 4
ROPE_THETA_2 = 500000.0
BLOCK = 128

MLSTM_HEADS = 8
MLSTM_QK_DIM = D_MODEL // 2 // MLSTM_HEADS
MLSTM_V_DIM = D_MODEL // MLSTM_HEADS
QK_WIDTH = MLSTM_HEADS * MLSTM_QK_DIM
MLSTM_IN_WIDTH = 2 * QK_WIDTH + 2 * D_MODEL + 2 * MLSTM_HEADS
MLSTM_CHUNK = 64
CONV_WIDTH = 4

D_FF_2 = -(-8 * D_MODEL // (3 * 256)) * 256


def rms_norm_2(x, g):
    xf = x.astype(jnp.float32)
    y = xf * lax.rsqrt(jnp.mean(xf * xf, axis=-1, keepdims=True) + RMS_EPS)
    return y.astype(x.dtype) * g.astype(x.dtype)

def apply_partial_rope(t, positions):
    half = ROT_DIM // 2
    inv_freq = ROPE_THETA_2 ** (-jnp.arange(half, dtype=jnp.float32) * 2.0 / ROT_DIM)
    ang = positions.astype(jnp.float32)[..., None] * inv_freq
    cos = jnp.cos(ang)[:, :, None, :]
    sin = jnp.sin(ang)[:, :, None, :]
    tf = t.astype(jnp.float32)
    x1 = tf[..., :half]
    x2 = tf[..., half:ROT_DIM]
    out = jnp.concatenate([x1 * cos - x2 * sin, x2 * cos + x1 * sin, tf[..., ROT_DIM:]], axis=-1)
    return out.astype(t.dtype)

def banded_window_attention(q, k, v, window):
    *lead, L, hd = q.shape
    nb = -(-L // BLOCK)
    Lp = nb * BLOCK
    pad = [(0, 0)] * len(lead) + [(0, Lp - L), (0, 0)]

    def blocks(t):
        return jnp.pad(t, pad).reshape(*lead, nb, BLOCK, hd)

    def with_prev(t):
        prev = jnp.concatenate([jnp.zeros_like(t[..., :1, :, :]), t[..., :-1, :, :]], axis=-3)
        return jnp.concatenate([prev, t], axis=-2)

    qb = blocks(q)
    kk = with_prev(blocks(k))
    vv = with_prev(blocks(v))
    s = jnp.einsum('...iqd,...ikd->...iqk', qb, kk).astype(jnp.float32)
    blk = jnp.arange(nb)[:, None, None]
    a = jnp.arange(BLOCK)[None, :, None]
    c = jnp.arange(2 * BLOCK)[None, None, :]
    dist = a + BLOCK - c
    valid = (dist >= 0) & (dist <= window) & ((blk - 1) * BLOCK + c >= 0)
    s = jnp.where(valid, s, -jnp.inf)
    m = jnp.max(s, axis=-1, keepdims=True)
    p = jnp.exp(s - m)
    den = jnp.sum(p, axis=-1, keepdims=True)
    o = jnp.einsum('...iqk,...ikd->...iqd', (p / den).astype(v.dtype), vv)
    lse = (m + jnp.log(den))[..., 0]
    o = o.reshape(*lead, Lp, hd)[..., :L, :]
    lse = lse.reshape(*lead, Lp)[..., :L]
    return o, lse

def dilated_window_attention(q, k, v, window, dilation):
    B, S, H, hd = q.shape
    L = S // dilation

    def to_sub(t):
        return t.reshape(B, L, dilation, H, hd).transpose(0, 2, 3, 1, 4)

    o, lse = banded_window_attention(to_sub(q), to_sub(k), to_sub(v), window // dilation)
    o = o.transpose(0, 3, 1, 2, 4).reshape(B, S, H, hd)
    lse = lse.transpose(0, 3, 1, 2).reshape(B, S, H)
    return o, lse

def dilated_attention_mixer(xn, positions, w_in, w_out):
    B, S, _ = xn.shape
    proj = (xn @ w_in).reshape(B, S, N_GROUPS, 3, ATTN_HEADS, ATTN_HEAD_DIM)
    scale = ATTN_HEAD_DIM ** -0.5
    outs = []
    lses = []
    for g, (window, dilation) in enumerate(DIL_CONFIGS):
        q = apply_partial_rope(proj[:, :, g, 0], positions) * scale
        k = apply_partial_rope(proj[:, :, g, 1], positions)
        v = proj[:, :, g, 2]
        o, lse = dilated_window_attention(q, k, v, window, dilation)
        outs.append(o)
        lses.append(lse)
    wts = jax.nn.softmax(jnp.stack(lses), axis=0)
    o = jnp.einsum('gbsh,gbshd->bshd', wts.astype(xn.dtype), jnp.stack(outs))
    return o.reshape(B, S, ATTN_WIDTH) @ w_out

def causal_depthwise_conv(t, w, b):
    out = lax.conv_general_dilated(
        t, w[:, None, :].astype(t.dtype), window_strides=(1,),
        padding=[(CONV_WIDTH - 1, 0)], dimension_numbers=('NWC', 'WIO', 'NWC'),
        feature_group_count=t.shape[-1])
    return out + b.astype(t.dtype)

def mlstm_chunk_step(carry, xs):
    C, n, m = carry
    q, k, v, ig, lf = xs
    L = q.shape[2]
    b = jnp.cumsum(lf, axis=-1)
    causal = jnp.tril(jnp.ones((L, L), dtype=bool))
    dmat = jnp.where(causal, b[..., :, None] - b[..., None, :] + ig[..., None, :], -jnp.inf)
    inter = b + m[..., None]
    m_t = jnp.maximum(inter, jnp.max(dmat, axis=-1))
    w_intra = jnp.exp(dmat - m_t[..., None])
    w_inter = jnp.exp(inter - m_t)
    sm = w_intra * jnp.einsum('bhtd,bhsd->bhts', q, k)
    num = jnp.einsum('bhts,bhsv->bhtv', sm, v) + w_inter[..., None] * jnp.einsum('bhtd,bhdv->bhtv', q, C)
    den = jnp.sum(sm, axis=-1) + w_inter * jnp.einsum('bhtd,bhd->bht', q, n)
    h = num / jnp.maximum(jnp.abs(den), jnp.exp(-m_t))[..., None]
    b_last = b[..., -1]
    decay = b_last[..., None] - b + ig
    m_new = jnp.maximum(b_last + m, jnp.max(decay, axis=-1))
    ws = jnp.exp(decay - m_new[..., None])
    carry_scale = jnp.exp(b_last + m - m_new)
    C_new = carry_scale[..., None, None] * C + jnp.einsum('bhs,bhsd,bhsv->bhdv', ws, k, v)
    n_new = carry_scale[..., None] * n + jnp.einsum('bhs,bhsd->bhd', ws, k)
    return (C_new, n_new, m_new), h

def mlstm_chunkwise(q, k, v, ig, lf):
    B, H, S, dk = q.shape
    dv = v.shape[-1]
    nc = S // MLSTM_CHUNK

    def to_chunks(t):
        return jnp.moveaxis(t.reshape(B, H, nc, MLSTM_CHUNK, *t.shape[3:]), 2, 0)

    init = (jnp.zeros((B, H, dk, dv), jnp.float32), jnp.zeros((B, H, dk), jnp.float32),
            jnp.zeros((B, H), jnp.float32))
    _, h = lax.scan(mlstm_chunk_step, init,
                    (to_chunks(q), to_chunks(k), to_chunks(v), to_chunks(ig), to_chunks(lf)))
    return jnp.moveaxis(h, 0, 2).reshape(B, H, S, dv)

def mlstm_mixer(xn, w_in, conv_w, conv_b, ig_bias, fg_bias, head_gain, w_out):
    B, S, _ = xn.shape
    proj = xn @ w_in
    qk_pre = proj[..., :2 * QK_WIDTH]
    v = proj[..., 2 * QK_WIDTH:2 * QK_WIDTH + D_MODEL]
    o_pre = proj[..., 2 * QK_WIDTH + D_MODEL:2 * QK_WIDTH + 2 * D_MODEL]
    gates = proj[..., 2 * QK_WIDTH + 2 * D_MODEL:].astype(jnp.float32)
    qk = jax.nn.silu(causal_depthwise_conv(qk_pre, conv_w, conv_b))
    ig = gates[..., :MLSTM_HEADS] + ig_bias.astype(jnp.float32)
    lf = jax.nn.log_sigmoid(gates[..., MLSTM_HEADS:] + fg_bias.astype(jnp.float32))

    def heads(t, d):
        return t.reshape(B, S, MLSTM_HEADS, d).transpose(0, 2, 1, 3).astype(jnp.float32)

    q = heads(qk[..., :QK_WIDTH], MLSTM_QK_DIM)
    k = heads(qk[..., QK_WIDTH:], MLSTM_QK_DIM) * (MLSTM_QK_DIM ** -0.5)
    vh = heads(v, MLSTM_V_DIM)
    h = mlstm_chunkwise(q, k, vh, ig.transpose(0, 2, 1), lf.transpose(0, 2, 1))
    h = h.transpose(0, 2, 1, 3)
    h = h * lax.rsqrt(jnp.mean(h * h, axis=-1, keepdims=True) + RMS_EPS)
    h = h.reshape(B, S, D_MODEL).astype(xn.dtype) * head_gain.astype(xn.dtype)
    return (h * jax.nn.sigmoid(o_pre)) @ w_out

def swiglu_2(xn, w_in, w_out):
    gu = xn @ w_in
    return (jax.nn.silu(gu[..., :D_FF_2]) * gu[..., D_FF_2:]) @ w_out

def second_inputs(seed: int = 0) -> dict:
    key = jax.random.key(seed)
    ks = jax.random.split(key, 20)

    def dense(k, shape, fan_in):
        return jax.random.normal(k, shape, jnp.float32) * (fan_in ** -0.5)

    def gain(k, shape):
        return 1.0 + 0.05 * jax.random.normal(k, shape, jnp.float32)

    x = jax.random.normal(ks[0], (BATCH, SEQ, D_MODEL), jnp.float32)
    offset = jax.random.randint(ks[1], (BATCH, 1), 0, 4096, dtype=jnp.int32)
    positions = offset + jnp.arange(SEQ, dtype=jnp.int32)[None, :]
    return {
        'x': x,
        'positions': positions,
        'attn_norm': gain(ks[2], (N_ATTN_LAYERS, D_MODEL)),
        'attn_w_in': dense(ks[3], (N_ATTN_LAYERS, D_MODEL, ATTN_IN_WIDTH), D_MODEL),
        'attn_w_out': dense(ks[4], (N_ATTN_LAYERS, ATTN_WIDTH, D_MODEL), ATTN_WIDTH),
        'mlstm_norm': gain(ks[5], (N_MLSTM_LAYERS, D_MODEL)),
        'mlstm_w_in': dense(ks[6], (N_MLSTM_LAYERS, D_MODEL, MLSTM_IN_WIDTH), D_MODEL),
        'mlstm_conv_w': dense(ks[7], (N_MLSTM_LAYERS, CONV_WIDTH, 2 * QK_WIDTH), CONV_WIDTH),
        'mlstm_conv_b': 0.02 * jax.random.normal(ks[8], (N_MLSTM_LAYERS, 2 * QK_WIDTH), jnp.float32),
        'mlstm_ig_bias': 0.1 * jax.random.normal(ks[9], (N_MLSTM_LAYERS, MLSTM_HEADS), jnp.float32),
        'mlstm_fg_bias': 3.0 + 0.1 * jax.random.normal(ks[10], (N_MLSTM_LAYERS, MLSTM_HEADS), jnp.float32),
        'mlstm_head_gain': gain(ks[11], (N_MLSTM_LAYERS, D_MODEL)),
        'mlstm_w_out': dense(ks[12], (N_MLSTM_LAYERS, D_MODEL, D_MODEL), D_MODEL),
        'ffn_norm': gain(ks[13], (DEPTH, D_MODEL)),
        'ffn_w_in': dense(ks[14], (DEPTH, D_MODEL, 2 * D_FF_2), D_MODEL),
        'ffn_w_out': dense(ks[15], (DEPTH, D_FF_2, D_MODEL), D_FF_2),
        'final_norm': gain(ks[16], (D_MODEL,)),
    }

def second_block(x, positions, attn_norm, attn_w_in, attn_w_out, mlstm_norm, mlstm_w_in,
              mlstm_conv_w, mlstm_conv_b, mlstm_ig_bias, mlstm_fg_bias, mlstm_head_gain,
              mlstm_w_out, ffn_norm, ffn_w_in, ffn_w_out, final_norm):
    h = x
    for i in range(DEPTH):
        j = i // N_MIXERS
        if i % N_MIXERS == 0:
            h = h + dilated_attention_mixer(rms_norm_2(h, attn_norm[j]), positions,
                                            attn_w_in[j], attn_w_out[j])
        else:
            h = h + mlstm_mixer(rms_norm_2(h, mlstm_norm[j]), mlstm_w_in[j], mlstm_conv_w[j],
                                mlstm_conv_b[j], mlstm_ig_bias[j], mlstm_fg_bias[j],
                                mlstm_head_gain[j], mlstm_w_out[j])
        h = h + swiglu_2(rms_norm_2(h, ffn_norm[i]), ffn_w_in[i], ffn_w_out[i])
    return rms_norm_2(h, final_norm)


def setup_inputs(seed=0):
    out = dict(first_inputs(seed))
    for name, value in second_inputs(seed + 1).items():
        if name != "x":
            out[name + "_2"] = value
    return out


def reference(
    x, c, ctx, c_ctx, w_mod, b_mod, norm_g, w_ffn_gate_up, w_ffn_down, w_in, w_out, na_rpb,
    w_pool, pool_scale, positions_2, attn_norm_2, attn_w_in_2, attn_w_out_2, mlstm_norm_2,
    mlstm_w_in_2, mlstm_conv_w_2, mlstm_conv_b_2, mlstm_ig_bias_2, mlstm_fg_bias_2,
    mlstm_head_gain_2, mlstm_w_out_2, ffn_norm_2, ffn_w_in_2, ffn_w_out_2, final_norm_2,
):
    x = first_block(
        x, c, ctx, c_ctx, w_mod, b_mod, norm_g, w_ffn_gate_up, w_ffn_down, w_in, w_out, na_rpb,
        w_pool, pool_scale,
    )
    return second_block(
        x, positions_2, attn_norm_2, attn_w_in_2, attn_w_out_2, mlstm_norm_2, mlstm_w_in_2,
        mlstm_conv_w_2, mlstm_conv_b_2, mlstm_ig_bias_2, mlstm_fg_bias_2, mlstm_head_gain_2,
        mlstm_w_out_2, ffn_norm_2, ffn_w_in_2, ffn_w_out_2, final_norm_2,
    )


_drawn_inputs = setup_inputs


def setup_inputs(seed=0):
    import zlib

    import numpy as np

    out = dict(_drawn_inputs(seed))
    spreads = {}
    factors = {'na_rpb': 8.0,
     'attn_norm_2': 2.963,
     'mlstm_conv_b_2': 26.423,
     'mlstm_ig_bias_2': 64.0,
     'mlstm_norm_2': 3.299,
     'mlstm_fg_bias_2': 43.776,
     'mlstm_head_gain_2': 5.546}
    for name, (base, spread) in spreads.items():
        noise = np.random.default_rng([zlib.crc32(name.encode()), seed]).standard_normal(out[name].shape)
        drawn = base * np.exp(spread * noise) if base else spread * noise
        out[name] = jnp.asarray(drawn.astype(out[name].dtype))
    for name, factor in factors.items():
        out[name] = (out[name] * factor).astype(out[name].dtype)
    return out
```

```python
from contextlib import ExitStack

import numpy as np
import concourse.bass as bass
from concourse import mybir

F32 = mybir.dt.float32
F32R = mybir.dt.float32r
I32 = mybir.dt.int32
ALU = mybir.AluOpType
ACT = mybir.ActivationFunctionType
AX = mybir.AxisListType.X

D = 1024
DFF = 2816
NF = DFF // 128
EPS = 1e-6
NEG = -1e30
RAW = 2
CUT = 3
UN = 2048
NP = 8

VEC = {}
_at = 0
for _name, _n in [("c", 8), ("c_ctx", 8), ("norm_g", 96), ("b_mod", 144), ("pool_scale", 8), ("attn_norm", 8),
                  ("mlstm_norm", 8), ("ffn_norm", 16), ("head_gain", 8), ("conv_b", 8), ("conv_w", 32)]:
    VEC[_name] = _at
    _at += _n
NVEC = _at

CST = {}
_at = 0
for _name, _n in [("ident", 128), ("rope", 256), ("colmask", 64), ("pool_x", 512),
                  ("upto", 128), ("after", 128), ("ones", 128), ("never", 128), ("sel", 256),
                  ("freq", 16), ("pool_c", 2048), ("causal", 1152)]:
    CST[_name] = (_at, _n)
    _at += _n
NCST = _at


class Line:

    def __init__(self, sem):
        self.sem, self.n, self.items, self.seen = sem, 0, [], {}

    def wait(self, *marks):
        for m in marks:
            if m is None:
                continue
            if isinstance(m, list):
                self.wait(*m)
                continue
            sem, value = m
            if self.seen.get(sem.name, 0) < value:
                self.seen[sem.name] = value
                self.items.append(lambda e, s=sem, v=value: e.wait_ge(s, v))

    def do(self, fn, *waits, mark=True):
        self.wait(*waits)
        if not mark:
            self.items.append(fn)
            return None
        self.n += 1
        self.items.append(lambda e: fn(e).then_inc(self.sem, 1))
        return (self.sem, self.n)

    def emit(self, eng):
        for f in self.items:
            f(eng)


def build(nc, a, out, tap=None, stop=None):
    with ExitStack() as ctx:
        def sb(name, shape, dt=F32):
            return ctx.enter_context(nc.sbuf_tensor(name, shape, dt))

        def sem(name):
            return ctx.enter_context(nc.semaphore(name))

        raw = [sb(f"raw{i}", [128, UN]) for i in range(RAW)]
        whi = [sb(f"whi{i}", [128, UN], F32R) for i in range(CUT)]
        wlo = [sb(f"wlo{i}", [128, UN], F32R) for i in range(CUT)]
        Hhi = sb("Hhi", [128, 8, 512], F32R)
        Hlo = sb("Hlo", [128, 8, 512], F32R)
        X = sb("X", [128, 2, D])
        vec = sb("vec", [128, NVEC])
        cst = sb("cst", [128, CST["pool_c"][0]])
        schi = sb("schi", [128, 8, 2], F32R)
        sclo = sb("sclo", [128, 8, 2], F32R)
        sc32 = sb("sc32", [128, 8, 2])
        SM = 960
        small = sb("small", [128, SM])
        mods = sb("mods", [128, 6, 8, 2])
        mtmp = sb("mtmp", [128, 8, 2])
        posi = sb("posi", [128, 2], I32)
        AR = 22016
        arena = sb("arena", [128, AR])
        ps = [ctx.enter_context(nc.psum_tensor(f"ps{i}", [128, 512], F32)) for i in range(NP)]

        PE, DV, AC, PO, SP = [Line(sem(n)) for n in ("s_pe", "s_dve", "s_act", "s_pool", "s_sp")]
        s_raw = [sem(f"s_raw{i}") for i in range(RAW)]
        dsems = {}

        def load(key, dst, src, *waits, line=None):
            if key not in dsems:
                dsems[key] = [sem(f"s_{key}"), 0]
            line = line or SP
            s = dsems[key][0]
            if dsems[key][1]:
                line.wait((s, dsems[key][1]))
            dsems[key][1] += 16
            line.do(lambda e: e.dma_start(dst, src).then_inc(s, 16), *waits, mark=False)
            return (s, dsems[key][1])

        def at(off, *dims):
            n = int(np.prod(dims))
            assert off + n <= AR, (off, n)
            v = arena[:, off:off + n]
            if len(dims) == 2:
                v = v.rearrange("p (a b) -> p a b", a=dims[0])
            elif len(dims) == 3:
                v = v.rearrange("p (a b c) -> p a b c", a=dims[0], b=dims[1])
            return v

        def cs(name):
            o, n = CST[name]
            return cst[:, o:o + n]

        cols = [0]

        def col(n=1):
            if cols[0] + n > SM:
                cols[0] = 0
            cols[0] += n
            return small[:, cols[0] - n:cols[0]]

        C = at(0, 2, D)
        G = [at(2048, D), at(3072, D)]
        XN = [at(4096, D), at(5120, D)]
        HS = [at(6144, 512), at(6656, 512)]
        U0 = 7168

        def ident(n=128):
            return cst[0:n, 0:n]

        pfree = [None] * NP
        bank_at = [0]
        held = set()

        def bank():
            while bank_at[0] % NP in held:
                bank_at[0] += 1
            b = bank_at[0] % NP
            bank_at[0] += 1
            PE.wait(pfree[b])
            return b

        def kview(w, c0, c1):
            return w[:, c0:c1].rearrange("(k p) n -> p k n", p=128)

        def units_of(step):
            kind = step[0]
            if kind == "mod":
                w = kview(a["w_mod"][step[1]], step[2] * D, step[2] * D + D)
                return [(w[:, 4 * k:4 * k + 4, 512 * h:512 * h + 512], 4, 512) for h in range(2) for k in range(2)]
            if kind == "gu":
                w = step[1]
                return [(kview(w, g * DFF + 256 * j, g * DFF + 256 * j + 256), 8, 256)
                        for j in range(NF // 2) for g in range(2)]
            if kind == "out":
                w = kview(step[1], 0, D)
                return [(w[:, 2 * j:2 * j + 2, :], 2, D) for j in range(step[2] // 2)]
            if kind == "cols":
                w = kview(step[1], step[2], step[2] + 512)
                return [(w[:, 4 * k:4 * k + 4, :], 4, 512) for k in range(2)]
            if kind == "rows":
                return [(kview(step[1], step[2], step[2] + 256), 8, 256)]
            if kind == "gates":
                return [(kview(step[1], 3072, 3088), 8, 16)]
            raise ValueError(kind)

        gu1 = a["w_ffn_gate_up"]
        dn1 = a["w_ffn_down"]
        sched = [("mod", 0, 0), ("mod", 0, 1)]
        for l in range(2):
            sched += [("mod", l, 2), ("gu", gu1[l, 0]), ("out", dn1[l, 0], NF), ("mod", l, 3), ("mod", l, 4),
                      ("mod", l, 5)]
            sched += [("cols", a["w_in"][l], 512 * g) for g in range(4)]
            sched += [("out", a["w_out"][l], 8), ("mod", l, 6), ("mod", l, 7)]
            sched += [("mod", l, 8), ("gu", gu1[l, 1]), ("out", dn1[l, 1], NF)]
            if l == 0:
                sched += [("mod", 1, 0), ("mod", 1, 1)]
        sched += [("cols", a["attn_w_in_2"][0], (3 * g + t) * 1024 + 512 * h)
                  for h in range(2) for g in range(3) for t in range(3)]
        sched += [("out", a["attn_w_out_2"][0], 8), ("gu", a["ffn_w_in_2"][0]), ("out", a["ffn_w_out_2"][0], NF)]
        mw = a["mlstm_w_in_2"][0]
        sched += [("rows", mw, 256 * j) for j in range(4)]
        sched += [("gates", mw)] + [("cols", mw, 1024 + 512 * j) for j in range(4)]
        sched += [("out", a["mlstm_w_out_2"][0], 8), ("gu", a["ffn_w_in_2"][1]), ("out", a["ffn_w_out_2"][1], NF)]
        if stop:
            sched = sched[:stop]
        units = [u for s in sched for u in units_of(s)]
        raw_in, lo_done, pe_done = [], [], {}
        used = [0]

        def fetch(n):
            if n >= len(units) or n < len(raw_in):
                return
            src, k, m = units[n]
            dst = raw[n % RAW][:, 0:k * m].rearrange("p (k m) -> p k m", k=k)
            s = s_raw[n % RAW]
            SP.do(lambda e: e.dma_start(dst, src).then_inc(s, 16), lo_done[n - RAW] if n >= RAW else None, mark=False)
            raw_in.append((s, 16 * (n // RAW + 1)))

        def cut(n):
            if n >= len(units):
                return
            _, k, m = units[n]
            r, h, o = raw[n % RAW][:, 0:k * m], whi[n % CUT][:, 0:k * m], wlo[n % CUT][:, 0:k * m]
            am = AC.do(lambda e: e.activation(h, r, ACT.Copy), raw_in[n], pe_done.get(n - CUT))
            lo_done.append(DV.do(lambda e: e.tensor_tensor(o, r, h.bitcast(F32), ALU.subtract), am))
            fetch(n + RAW)

        def unit(k, m):
            n = used[0]
            assert units[n][1:] == (k, m), (n, units[n][1:], k, m)
            PE.wait(lo_done[n])
            v = lambda t: t[n % CUT][:, 0:k * m].rearrange("p (k m) -> p k m", k=k)
            return v(whi), v(wlo)

        def unit_done(mark):
            n = used[0]
            pe_done[n] = mark
            used[0] += 1
            cut(n + CUT)

        def mm3(o, A, B, start, stop, mark=False):
            PE.do(lambda e: e.matmul(o, A[0], B[1], start=start, stop=False), mark=False)
            PE.do(lambda e: e.matmul(o, A[1], B[0], start=False, stop=False), mark=False)
            return PE.do(lambda e: e.matmul(o, A[0], B[0], start=False, stop=stop), mark=mark)

        def mm(o, A, B, start=True, stop=True, mark=True, *waits):
            return PE.do(lambda e: e.matmul(o, A, B, start=start, stop=stop), *waits, mark=mark)

        def tr(o, i, mark=True, *waits):
            n = i.shape[0]
            return PE.do(lambda e: e.transpose(o, i, ident(n)), *waits, mark=mark)

        def tt(line, o, x, y, op, *waits):
            return line.do(lambda e: e.tensor_tensor(o, x, y, op), *waits)

        def ts(line, o, x, s1, op0, s2, op1, *waits):
            if op1 is None:
                return line.do(lambda e: e.tensor_scalar(o, x, s1, None, op0), *waits)
            return line.do(lambda e: e.tensor_scalar(o, x, s1, s2, op0, op1), *waits)

        def stt(o, x, s, y, op0, op1, *waits, acc=None):
            return DV.do(lambda e: e.scalar_tensor_tensor(out=o, in0=x, scalar=s, in1=y, op0=op0, op1=op1,
                                                          **({"accum_out": acc} if acc is not None else {})), *waits)

        def red(o, x, op, *waits):
            return DV.do(lambda e: e.tensor_reduce(o, x, AX, op), *waits)

        def recip(o, x, *waits):
            return DV.do(lambda e: e.reciprocal(o, x), *waits)

        def act(o, x, f, *waits, **kw):
            return AC.do(lambda e: e.activation(o, x, f, **kw), *waits)

        def copy(line, o, x, *waits):
            if line is AC:
                return act(o, x, ACT.Copy, *waits)
            return line.do(lambda e: e.tensor_copy(o, x), *waits)

        def two_parts(hi, lo, x, *waits):
            am = act(hi, x, ACT.Copy, *waits)
            return DV.do(lambda e: e.tensor_tensor(lo, x, hi.bitcast(F32), ALU.subtract), am)

        m_vec = load("vec", vec[:, :], a["vec"])
        m_cst = load("cst", cst[:, :], a["cst"][:, 0:CST["pool_c"][0]])
        m_x = load("x", X[:, :, :], a["x"].rearrange("o (t p) d -> p (o t) d", p=128))
        m_c = load("c", C, a["ctx"].rearrange("o (t p) d -> p (o t) d", p=128))
        for n in range(RAW):
            fetch(n)
        rpbs = nc.dram_tensor("rpbs", (64, 7440), F32).ap()
        m_rpb = load("rpb", rpbs, bass.AP(a["na_rpb"].tensor, 0, [[0, 64], [1, 7440]]))
        m_pos = [load(f"pos{t}", posi[:, t:t + 1], a["positions_2"][:, 128 * t:128 * t + 128].rearrange("o p -> p o"))
                 for t in range(2)]
        for n in range(CUT):
            cut(n)

        v2 = vec[:, 0:16].rearrange("p (s k) -> p k s", s=2)
        m = act(sc32[:, :, :], v2, ACT.Silu, m_vec)
        m_sc = two_parts(schi[:, :, :], sclo[:, :, :], sc32[:, :, :], m)

        rope2 = sb("rope2", [128, 2, 2, 32])
        angs = sb("angs", [128, 6, 2, 16])
        posf, ANG, TT, KK, RR = small[:, SM - 2:SM], angs[:, 0], angs[:, 1], angs[:, 2], angs[:, 3]
        m = copy(DV, posf, posi[:, :], m_pos)
        for t in range(2):
            m1 = ts(DV, ANG[:, t, :], cs("freq"), posf[:, t:t + 1], ALU.mult, None, None, m, m_cst)
        m_ang = m1
        C1 = 6.28125
        C2 = round((2 * np.pi - C1) * 2.0 ** 18) / 2.0 ** 18
        C3 = float(np.float32(2 * np.pi - C1 - C2))
        m_r2 = []
        for f, (turns_, shift_) in enumerate([(0.25, float(np.float32(np.pi / 2))), (0.0, 0.0)]):
            m1 = ts(DV, TT, ANG, float(1 / (2 * np.pi)), ALU.mult, turns_, ALU.add, m_ang)
            m1 = ts(DV, KK, TT, 12582912.0, ALU.add, None, None, m1)
            m1 = ts(DV, KK, KK, -12582912.0, ALU.add, None, None, m1)
            m1 = stt(RR, KK, -C1, ANG, ALU.mult, ALU.add, m1)
            m1 = stt(RR, KK, -C2, RR, ALU.mult, ALU.add, m1)
            m1 = stt(RR, KK, -C3, RR, ALU.mult, ALU.add, m1)
            m1 = ts(DV, RR, RR, shift_, ALU.add, 3.1415925, ALU.min, m1)
            m1 = ts(DV, RR, RR, -3.1415925, ALU.max, None, None, m1)
            m1 = act(angs[:, 4 + f], RR, ACT.Sin, m1)
            DV.wait(m1)
            if f == 0:
                for z in range(2):
                    m_r2.append(copy(DV, rope2[:, :, 0, 16 * z:16 * z + 16], angs[:, 4]))
            else:
                m_r2.append(ts(DV, rope2[:, :, 1, 0:16], angs[:, 5], -1.0, ALU.mult, None, None))
                m_r2.append(copy(DV, rope2[:, :, 1, 16:32], angs[:, 5]))
        m_rope2 = m_r2

        MROW = U0 + 11264
        mrow = at(MROW, D)
        bg = at(MROW + 1024, 2, 512)
        U1 = U0
        mrow_free, bg_free, bb_free = [None], [None], [None]
        g_free = [None, None]
        g_ready = [None, None]
        mods_ready = {}
        mods_free = {}

        def mod(l, v, gain=None, half_gate=False):
            rows = []
            for h in range(2):
                b = bank()
                o = ps[b][0:2, :]
                if v % 3 == 2:
                    m_b = load("bg", bg[0:2, 0, :],
                               bass.AP(a["b_mod"].tensor, l * 9216 + v * D + 512 * h, [[0, 2], [1, 512]]),
                               bg_free[0], bb_free[0])
                    m_g = load("bh", bg[0:2, 1, :],
                               bass.AP(a["norm_g"].tensor, (l * 6 + gain) * D + 512 * h, [[0, 2], [1, 512]]),
                               bg_free[0], bb_free[0])
                for u in range(2):
                    hi, lo = unit(4, 512)
                    for k in range(4):
                        kt = 4 * u + k
                        m = mm3(o, (schi[:, kt, :], sclo[:, kt, :]), (hi[:, k, :], lo[:, k, :]),
                                kt == 0, kt == 7, mark=(k == 3))
                    if h == 0 and u == 0:
                        DV.wait(mrow_free[0], bb_free[0])
                    if u == 0:
                        unit_done(m)
                r = mrow[0:2, 512 * h:512 * h + 512]
                if v % 3 == 2:
                    m1 = tt(DV, r, o, bg[0:2, 0, :], ALU.add, m, m_b)
                    pfree[b] = m1
                    m2 = stt(r, r, 0.5 if half_gate else 1.0, bg[0:2, 1, :], ALU.mult, ALU.mult, m1, m_g)
                    bg_free[0] = m2
                    rows.append(m2)
                else:
                    m1 = copy(DV, r, o, m)
                    pfree[b] = m1
                    rows.append(m1)
                unit_done(m)
            if v % 3 == 2:
                for s in range(2):
                    for h in range(2):
                        b = bank()
                        m = mm(ps[b][:, :], cs("sel")[0:2, 128 * s:128 * s + 128],
                               mrow[0:2, 512 * h:512 * h + 512], True, True, True, rows)
                        pfree[b] = m1 = copy(AC, G[s][:, 512 * h:512 * h + 512], ps[b][:, :], m, g_free[s])
                    g_ready[s] = m1
                mrow_free[0] = m
            else:
                b = bank()
                for k in range(8):
                    m = tr(ps[b][:, 2 * k:2 * k + 2], mrow[0:2, 128 * k:128 * k + 128], k == 7, rows)
                mrow_free[0] = m
                i = v // 3 * 2 + v % 3
                o = mods[:, i, :, :]
                bT = vec[:, VEC["b_mod"] + 72 * l + 8 * v:VEC["b_mod"] + 72 * l + 8 * v + 8]
                bT = bT.unsqueeze(2).to_broadcast([128, 8, 2])
                pv = ps[b][:, 0:16].rearrange("p (k s) -> p k s", s=2)
                if v % 3 == 0:
                    m = tt(DV, o, pv, bT, ALU.add, m, mods_free.get(i))
                    pfree[b] = m
                else:
                    g0 = VEC["norm_g"] + 48 * l + 8 * gain
                    gT = vec[:, g0:g0 + 8].unsqueeze(2).to_broadcast([128, 8, 2])
                    m = tt(DV, mtmp[:, :, :], pv, bT, ALU.add, m)
                    pfree[b] = m
                    m = DV.do(lambda e: e.scalar_tensor_tensor(out=o, in0=mtmp[:, :, :], scalar=1.0, in1=gT,
                                                               op0=ALU.add, op1=ALU.mult), m, mods_free.get(i))
                mods_ready[i] = m

        h_free = [None]

        def rstd(ss, n, scale, *waits):
            v, q, r = col(n), col(n), col(n)
            m = ts(DV, v, ss, scale, ALU.mult, EPS, ALU.add, *waits)
            m = act(q, v, ACT.Sqrt, m)
            m = recip(r, q, m)
            return r, m

        xn_free = [None, None]
        hs_free = [None, None]
        hs_at = [0]

        def stats(tiles):
            ss = col(len(tiles))
            for i, (x, m) in enumerate(tiles):
                m = act(XN[i % 2], x, ACT.Square, m, xn_free[i % 2], accum_out=ss[:, i:i + 1])
                xn_free[i % 2] = m
            return rstd(ss, len(tiles), 1.0 / D, m)

        evac_at = [0]

        def turn(i, src, m_src, pos, gain, shift, m_ab):
            m_t = None
            for hb in range(2):
                b = bank()
                for k in range(4):
                    m_t = tr(ps[b][:, 128 * k:128 * k + 128], src[:, 512 * hb + 128 * k:512 * hb + 128 * k + 128],
                             k == 3, m_src)
                q = hs_at[0] % 2
                hs_at[0] += 1
                h32 = HS[q].rearrange("p (k t) -> p k t", k=4)
                pv = ps[b][:, :].rearrange("p (k t) -> p k t", k=4)
                k0 = 4 * hb
                evac_at[0] += 1
                if evac_at[0] % 2:
                    gb = gain[:, k0:k0 + 4].unsqueeze(2).to_broadcast([128, 4, 128])
                    m = tt(DV, h32, pv, gb, ALU.mult, m_t, m_ab, hs_free[q])
                    pfree[b] = m
                    if shift is not None:
                        sbb = shift[:, k0:k0 + 4].unsqueeze(2).to_broadcast([128, 4, 128])
                        m = tt(DV, h32, h32, sbb, ALU.add, m)
                else:
                    for k in range(4):
                        kw = {"scale": gain[:, k0 + k:k0 + k + 1]}
                        if shift is not None:
                            kw["bias"] = shift[:, k0 + k:k0 + k + 1]
                        m = act(h32[:, k, :], pv[:, k, :], ACT.Identity, m_t, m_ab, hs_free[q], **kw)
                    pfree[b] = m
                m = two_parts(Hhi[:, k0:k0 + 4, pos:pos + 128], Hlo[:, k0:k0 + 4, pos:pos + 128], h32, m, h_free[0])
                hs_free[q] = m
            return m_t, m

        def pre(tiles, r, m_r, ab):
            for i, (x, m) in enumerate(tiles):
                gain, shift, m_ab = ab(i)
                m = ts(DV, XN[i % 2], x, r[:, i:i + 1], ALU.mult, None, None, m_r, m, xn_free[i % 2])
                xn_free[i % 2], m_h = turn(i, XN[i % 2], m, 128 * i, gain, shift, m_ab)
            return m_h

        def gate_up(T, m_h, act_at):
            A = at(act_at, NF, T)
            PE.wait(m_h)
            marks = {}
            for j in range(NF // 2):
                bs = [bank() for _ in range(4)]
                done = []
                for g in range(2):
                    hi, lo = unit(8, 256)
                    for s in range(2):
                        for k in range(8):
                            m = mm3(ps[bs[2 * g + s]][:, 0:T],
                                    (hi[:, k, 128 * s:128 * s + 128], lo[:, k, 128 * s:128 * s + 128]),
                                    (Hhi[:, k, 0:T], Hlo[:, k, 0:T]), k == 0, k == 7, mark=(k == 7))
                        done.append(m)
                    if g == 0:
                        unit_done(m)
                for s in range(2):
                    q = XN[s][:, 0:T]
                    m1 = act(q, ps[bs[s]][:, 0:T], ACT.Silu, done[s], xn_free[s])
                    pfree[bs[s]] = m1
                    m2 = tt(DV, A[:, 2 * j + s, :], q, ps[bs[2 + s]][:, 0:T], ALU.mult, m1, done[2 + s])
                    xn_free[s] = m2
                    pfree[bs[2 + s]] = m2
                    marks[2 * j + s] = m2
                unit_done(m)
            h_free[0] = m
            return A, marks

        def out_product(nk, nt, left):
            bs = {(t, h): bank() for t in range(nt) for h in range(2)}
            for j in range(nk // 2):
                hi, lo = unit(2, D)
                for kk in range(2):
                    k = 2 * j + kk
                    Lh, Ll, after = left(k)
                    for t in range(nt):
                        for h in range(2):
                            m = mm3(ps[bs[t, h]][:, :],
                                    (Lh[:, 128 * t:128 * t + 128], Ll[:, 128 * t:128 * t + 128]),
                                    (hi[:, kk, 512 * h:512 * h + 512], lo[:, kk, 512 * h:512 * h + 512]),
                                    k == 0, k == nk - 1, mark=(t == nt - 1 and h == 1))
                    after(m)
                unit_done(m)
            return bs, m

        def down(T, A, a_marks):
            parts, slot_free = {}, {}

            def part(k):
                if k < NF:
                    s = k % 8
                    hi, lo = Hhi[:, s, 0:T], Hlo[:, s, 0:T]
                    parts[k] = (hi, lo, two_parts(hi, lo, A[:, k, :], a_marks[k], h_free[0], slot_free.get(s)))

            for k in range(4):
                part(k)

            def left(k):
                hi, lo, m = parts[k]
                PE.wait(m)

                def after(mark):
                    slot_free[k % 8] = mark
                    part(k + 4)
                return hi, lo, after
            bs, m = out_product(NF, T // 128, left)
            h_free[0] = m
            return bs, m

        def from_H(nk, nt, m_h, off=0):
            PE.wait(m_h)
            bs, m = out_product(nk, nt, lambda k: (Hhi[:, k, off:512], Hlo[:, k, off:512], lambda mark: None))
            h_free[0] = m
            return bs, m

        def post(bs, m_y, tiles, gs):
            n = len(tiles)
            ss, s1 = col(2 * n), col(n)
            for t in range(n):
                for h in range(2):
                    m = act(HS[h], ps[bs[t, h]][:, :], ACT.Square, m_y, hs_free[h],
                            accum_out=ss[:, h * n + t:h * n + t + 1])
                    hs_free[h] = m
            m = tt(DV, s1, ss[:, 0:n], ss[:, n:2 * n], ALU.add, m)
            r, m_r = rstd(s1, n, 1.0 / D, m)
            out_marks = []
            for t, (x, m_x) in enumerate(tiles):
                s = gs[t]
                for h in range(2):
                    q = XN[h][:, 512 * (t % 2):512 * (t % 2) + 512]
                    m = stt(q, ps[bs[t, h]][:, :], r[:, t:t + 1], G[s][:, 512 * h:512 * h + 512], ALU.mult, ALU.mult,
                            m_r, g_ready[s], xn_free[h])
                    pfree[bs[t, h]] = m
                    g_free[s] = m
                    m = tt(PO, x[:, 512 * h:512 * h + 512], x[:, 512 * h:512 * h + 512], q, ALU.add, m, m_x)
                    xn_free[h] = m
                out_marks.append((x, m))
            return out_marks

        def add(bs, m_y, tiles):
            res = []
            for t, (x, m_x) in enumerate(tiles):
                for h in range(2):
                    xs = x[:, 512 * h:512 * h + 512]
                    m = tt(DV, xs, xs, ps[bs[t, h]][:, :], ALU.add, m_y, m_x)
                    pfree[bs[t, h]] = m
                res.append((x, m))
            return res

        later = []

        def flush():
            todo = list(later)
            later.clear()
            for f in todo:
                f()

        def project(tts, evac, m_h=None):
            if m_h is not None:
                PE.wait(m_h)
            bs = {t: bank() for t in tts}
            last = {}
            for u in range(2):
                hi, lo = unit(4, 512)
                for t in tts:
                    for k in range(4):
                        kt = 4 * u + k
                        m = mm3(ps[bs[t]][:, :], (Hhi[:, kt, 128 * t:128 * t + 128], Hlo[:, kt, 128 * t:128 * t + 128]),
                                (hi[:, k, :], lo[:, k, :]), kt == 0, kt == 7, mark=(k == 3))
                    last[t] = m
                unit_done(m)
            flush()
            for i, t in enumerate(tts):
                if i == 2:
                    flush()
                evac(t, bs[t], last[t])
            return m

        QT = at(U1, 4, 512)
        KT = at(U1 + 2048, 4, 512)
        V = at(U1 + 4096, 4, 512)
        UU = at(U1 + 6144, 4, 512)
        S = [at(U1 + 8192, 512), at(U1 + 8704, 512)]
        PT_AT = U1 + 9216
        PT = [at(PT_AT, 4, 256), at(PT_AT + 1024, 4, 256)]
        BB = at(PT_AT + 2048, 8, 6, 64)
        ACT_AT = U1
        rope = cs("rope").rearrange("p (t c d) -> p t c d", t=2, c=2)

        def token_mix(l, m_h, m_act_free):
            ctx_out = l == 0
            bb = []
            for q in range(2):
                for i in range(6):
                    src = bass.AP(rpbs.tensor, 3720 * l + (5 - q + i) * 31 + 15, [[7439, 64], [465, 8], [1, 64]])
                    bb.append(load(f"bb{q}{i}", BB[64 * q:64 * q + 64, :, i, :], src, m_rpb, bb_free[0], mrow_free[0],
                                   bg_free[0], m_act_free))
            m_bb = DV.do(lambda e: e.tensor_tensor(
                BB.rearrange("p h i c -> p (h i) c"), BB.rearrange("p h i c -> p (h i) c"),
                cs("colmask").unsqueeze(1).to_broadcast([128, 48, 64]), ALU.add), bb, m_cst)
            tm = {}
            s_free = [None, None]

            def to_T(dst, scale, t, b, m):
                q = t % 2
                z = S[q]
                if t < 2:
                    ct = rope[:, t, 0, :].unsqueeze(1).to_broadcast([128, 8, 64])
                    m1 = tt(DV, XN[q][:, 0:512].rearrange("p (h d) -> p h d", h=8),
                            ps[b][:, :].rearrange("p (h d) -> p h d", h=8), ct, ALU.mult, m, xn_free[q], m_cst)
                    pv = ps[b][:, :].rearrange("p (h f d) -> p h f d", h=16, f=2)
                    xv = XN[q][:, 512:1024].rearrange("p (h f d) -> p h f d", h=16, f=2)
                    for f in range(2):
                        st = rope[:, t, 1, :].rearrange("p (r f d) -> p r f d", r=2, f=2)[:, :, f, :]
                        st = st.unsqueeze(1).to_broadcast([128, 8, 2, 16])
                        o4 = xv[:, :, f, :].rearrange("p (h r) d -> p h r d", r=2)
                        i4 = pv[:, :, 1 - f, :].rearrange("p (h r) d -> p h r d", r=2)
                        m2 = tt(DV, o4, i4, st, ALU.mult, m)
                    pfree[b] = m2
                    m = tt(PO, z, XN[q][:, 0:512], XN[q][:, 512:1024], ALU.add, m1, m2, s_free[q], m_act_free)
                    xn_free[q] = m
                else:
                    m = copy(AC, z, ps[b][:, :], m, s_free[q], m_act_free)
                    pfree[b] = m

                def turned():
                    b2 = bank()
                    for k in range(4):
                        m3 = tr(ps[b2][:, 128 * k:128 * k + 128], z[:, 128 * k:128 * k + 128], k == 3, m)
                    s_free[q] = m3
                    m4 = act(dst[:, :, 128 * t:128 * t + 128], ps[b2][:, :].rearrange("p (k t) -> p k t", k=4),
                             ACT.Copy, m3, scale=scale)
                    pfree[b2] = m4
                    tm["qk"] = m4
                later.append(turned)

            def keep(dst, name, t, b, m):
                m = copy(AC, dst[:, t, :], ps[b][:, :], m, m_act_free)
                pfree[b] = m
                tm[name] = m

            both, own = [0, 1, 2, 3], [0, 1]
            AC.wait(m_act_free)
            for g, (tts, ev) in enumerate([
                    (both if ctx_out else own, lambda t, b, m: to_T(QT, 0.125, t, b, m)),
                    (both, lambda t, b, m: to_T(KT, 1.0, t, b, m)),
                    (both, lambda t, b, m: keep(V, "v", t, b, m)),
                    (both if ctx_out else own, lambda t, b, m: keep(UU, "u", t, b, m))]):
                m_pe = project(tts, ev, m_h)
            flush()
            h_free[0] = m_pe
            m_wp = load("wp", WPOOL, a["w_pool"][l].rearrange("g c d -> c g d"), wp_free[0])

            items = [(h, qt) for h in range(8) for qt in (range(4) if ctx_out else range(2))]
            st = {}
            pt_free = [None, None]
            pair = {}

            def scores(n):
                h, qt = items[n]
                p0, hp = 64 * (h % 2), h // 2
                b = bank()
                k0 = 0 if qt < 2 else 256
                N = 512 - k0
                m = mm(ps[b][:, 0:N], QT[p0:p0 + 64, hp, 128 * qt:128 * qt + 128], KT[p0:p0 + 64, hp, k0:512],
                       True, True, True, tm["qk"])
                z = S[n % 2][:, 0:N]
                if qt < 2:
                    i0 = 2 if qt == 0 else 0
                    m1 = DV.do(lambda e: e.tensor_tensor(
                        z[:, 0:256].rearrange("p (i c) -> p i c", i=4),
                        ps[b][:, 0:256].rearrange("p (i c) -> p i c", i=4), BB[:, h, i0:i0 + 4, :], ALU.add),
                        m, m_bb, s_free[n % 2])
                    m2 = copy(DV, z[:, 256:512], ps[b][:, 256:512], m)
                    bb_free[0] = m1
                else:
                    m2 = copy(DV, z, ps[b][:, 0:N], m, s_free[n % 2])
                pfree[b] = m2
                mx, nm, den, rd = col(), col(), col(), col()
                m = red(mx, z, ALU.max, m2)
                m = ts(DV, nm, mx, -1.0, ALU.mult, None, None, m)
                m = act(z, z, ACT.Exp, m, bias=nm, accum_out=den)
                m = recip(rd, den, m)
                m = ts(DV, z, z, rd, ALU.mult, None, None, m)
                st[n] = m

            def turns(n):
                h, qt = items[n]
                nb = 4 if qt < 2 else 2
                z = S[n % 2]
                b = bank()
                for k in range(nb):
                    m = tr(ps[b][:, 128 * k:128 * k + 128], z[:, 128 * k:128 * k + 128], k == nb - 1, st[n])
                s_free[n % 2] = m
                g = n // 2 % 2
                m = copy(AC, PT[g][:, 0:nb, 128 * (qt % 2):128 * (qt % 2) + 128],
                         ps[b][:, 0:128 * nb].rearrange("p (k t) -> p k t", k=nb), m, pt_free[g])
                pfree[b] = m
                st[n] = m

            def values(n):
                h, qt = items[n]
                if qt % 2 == 0:
                    return
                g = n // 2 % 2
                s = qt // 2
                p0 = 64 * (h % 2)
                if h % 2 == 0:
                    pair[s] = bank()
                    held.add(pair[s])
                b = pair[s]
                kb = range(4) if s == 0 else range(2, 4)
                for k in kb:
                    m = mm(ps[b][p0:p0 + 64, 0:256], V[:, k, 64 * h:64 * h + 64], PT[g][:, k - kb[0], :],
                           k == kb[0], k == 3, k == 3, st[n], tm["v"])
                pt_free[g] = m
                if h % 2:
                    o = 256 * s
                    hi, lo = Hhi[:, h // 2, o:o + 256], Hlo[:, h // 2, o:o + 256]
                    m = two_parts(hi, lo, ps[b][:, 0:256], m, h_free[0])
                    pfree[b] = m
                    held.discard(b)
                    tm["mix"] = m

            for n in range(len(items) + 4):
                if n < len(items):
                    scores(n)
                if 0 <= n - 1 < len(items):
                    turns(n - 1)
                if 0 <= n - 3 < len(items):
                    values(n - 3)

            T = 512 if ctx_out else 256
            if ctx_out:
                o, n_ = CST["pool_c"]
                m_pc = load("pc", at(PT_AT, 2048), a["cst"][:, o:o + n_], list(pt_free), st[len(items) - 1])
                pc = at(PT_AT, 4, 2, 256)
            px = cs("pool_x").rearrange("p (g t) -> p g t", g=4)
            for g in range(4):
                b = bank()
                for t in range(2):
                    m = mm(ps[b][:, 128 * t:128 * t + 128], UU[:, t, 128 * g:128 * g + 128], px[:, g, :],
                           True, True, True, tm["u"], m_cst)
                if ctx_out:
                    for t in range(2):
                        m = mm(ps[b][:, 256:512], UU[:, 2 + t, 128 * g:128 * g + 128], pc[:, g, t, :],
                               t == 0, t == 1, True, m_pc)
                q = g % 2
                z = S[q][:, 0:T]
                m = copy(AC, z, ps[b][:, 0:T], m, s_free[q])
                pfree[b] = m
                b = bank()
                m = mm(ps[b][:, 0:T], WPOOL[:, g, :], z, True, True, True, m, m_wp)
                s_free[q] = m
                wp_free[0] = m
                sc_ = VEC["pool_scale"] + 4 * l + g
                y = HS[q][:, 0:T]
                m = act(y, ps[b][:, 0:T], ACT.Copy, m, hs_free[q], scale=vec[:, sc_:sc_ + 1])
                pfree[b] = m
                m = two_parts(Hhi[:, 4 + g, 0:T], Hlo[:, 4 + g, 0:T], y, m, h_free[0])
                hs_free[q] = m
            return [m, tm["mix"]]

        WPOOL = at(PT_AT + 2048 + 3072, 4, 128)
        wp_free = [None]

        def xs(m0=None):
            return [(X[:, t, :], m0) for t in range(2)]

        def taps(name, ap, *marks):
            if tap is not None:
                tap(name, ap, SP, load, marks)

        tiles_x = xs(m_x)
        tiles_c = [(C[:, t, :], m_c) for t in range(2)]

        class Stop(Exception):
            pass

        def check_stop():
            if stop and used[0] >= len(units):
                raise Stop

        def ab(v):
            def f(i):
                s = 0 if i < 2 else 1
                return (mods[:, v // 3 * 2 + 1, :, s], mods[:, v // 3 * 2, :, s],
                        [mods_ready[v // 3 * 2], mods_ready[v // 3 * 2 + 1]])
            return f

        try:
            PE.wait(m_sc, m_cst)
            DV.wait(m_cst)
            act_free = None
            tiles = tiles_x + tiles_c
            r, m_r = stats(tiles)
            mod(0, 0)
            mod(0, 1, gain=0)
            for l in range(2):
                m_h = pre(tiles, r, m_r, ab(0))
                mods_free[0] = mods_free[1] = m_h
                mod(l, 2, gain=1, half_gate=True)
                A, am = gate_up(512, m_h, ACT_AT)
                bs, m_y = down(512, A, am)
                act_free = [m_y, h_free[0], (DV.sem, DV.n)]
                tiles = post(bs, m_y, tiles, [0, 0, 1, 1])
                for i, (x_, m_) in enumerate(tiles):
                    taps(f"l{l}a{i}", x_, m_)
                r, m_r = stats(tiles)
                check_stop()
                mod(l, 3)
                mod(l, 4, gain=2)
                m_h = pre(tiles, r, m_r, ab(3))
                mods_free[2] = mods_free[3] = m_h
                mod(l, 5, gain=3)
                m_mix = token_mix(l, m_h, act_free)
                if l == 1:
                    tiles = tiles[0:2]
                nt = len(tiles)
                bs, m_y = from_H(8, nt, m_mix)
                tiles = post(bs, m_y, tiles, [0, 0, 1, 1])
                for i, (x_, m_) in enumerate(tiles):
                    taps(f"l{l}b{i}", x_, m_)
                r, m_r = stats(tiles)
                check_stop()
                mod(l, 6)
                mod(l, 7, gain=4)
                m_h = pre(tiles, r, m_r, ab(6))
                mods_free[4] = mods_free[5] = m_h
                mod(l, 8, gain=5, half_gate=True)
                A, am = gate_up(128 * nt, m_h, ACT_AT)
                bs, m_y = down(128 * nt, A, am)
                tiles = post(bs, m_y, tiles, [0, 0, 1, 1])
                for i, (x_, m_) in enumerate(tiles):
                    taps(f"l{l}c{i}", x_, m_)
                r, m_r = stats(tiles)
                check_stop()
                if l == 0:
                    mod(1, 0)
                    mod(1, 1, gain=0)

            def gain(name, n=0):
                v = vec[:, VEC[name] + 8 * n:VEC[name] + 8 * n + 8]
                return lambda i: (v, None, m_vec)

            def ffn2(n, tiles):
                r, m_r = stats(tiles)
                m_h = pre(tiles, r, m_r, gain("ffn_norm", n))
                A, am = gate_up(256, m_h, ACT_AT)
                bs, m_y = down(256, A, am)
                return add(bs, m_y, tiles)

            m_h = pre(tiles, r, m_r, gain("attn_norm"))
            region_free = [m_y, h_free[0], (DV.sem, DV.n)]
            Q3, K3, V3 = at(U0, 12, 256), at(U0 + 3072, 12, 256), at(U0 + 6144, 6, 512)
            S3 = [at(U0 + 9216, 768), at(U0 + 9984, 768)]
            P3 = [at(1152, 3, 384), at(2304, 3, 384)]
            o_, n_ = CST["causal"]
            m_ca = load("pc", at(0, n_), a["cst"][:, o_:o_ + n_], region_free, (PO.sem, PO.n))
            qk3, v3 = [None], [None]
            s3_free, p3_free = [None, None], [None, None]
            attended = [region_free]

            def ev_qk(dst, g, scale, t, b, m):
                q = t % 2
                z = XN[q][:, 0:512]
                z4 = z.rearrange("p (h d) -> p h d", h=4)
                t1 = XN[q][:, 512:640].rearrange("p (h d) -> p h d", h=4)
                t2 = XN[q][:, 640:768].rearrange("p (h d) -> p h d", h=4)
                m = copy(AC, z, ps[b][:, :], m, xn_free[q])
                pfree[b] = m
                cc = rope2[:, t, 0, :].unsqueeze(1).to_broadcast([128, 4, 32])
                m1 = tt(DV, t1, z4[:, :, 0:32], cc, ALU.mult, m, m_rope2)
                for f in range(2):
                    sn = rope2[:, t, 1, 16 * f:16 * f + 16].unsqueeze(1).to_broadcast([128, 4, 16])
                    m2 = tt(DV, t2[:, :, 16 * f:16 * f + 16], z4[:, :, 16 - 16 * f:32 - 16 * f], sn, ALU.mult, m)
                m = tt(DV, z4[:, :, 0:32], t1, t2, ALU.add, m1, m2)

                def turned():
                    b2 = bank()
                    for k in range(4):
                        mt = tr(ps[b2][:, 128 * k:128 * k + 128], z[:, 128 * k:128 * k + 128], k == 3, m)
                    xn_free[q] = mt
                    mt = act(dst[:, 4 * g:4 * g + 4, 128 * t:128 * t + 128],
                             ps[b2][:, :].rearrange("p (k t) -> p k t", k=4), ACT.Copy, mt, attended[0], scale=scale)
                    pfree[b2] = mt
                    qk3[0] = mt
                later.append(turned)

            def ev_v(g, t, b, m):
                m = copy(AC, V3[:, 2 * g + t, :], ps[b][:, :], m, attended[0])
                pfree[b] = m
                v3[0] = m

            def attend(half):
                items = [(h, qt) for h in range(4) for qt in range(2)]
                st = {}
                ca = at(0, 1152)

                def scores(n):
                    h, qt = items[n]
                    w = 128 * (qt + 1)
                    z = S3[n % 2][:, 0:3 * w]
                    ms = [s3_free[n % 2], m_ca]
                    for gs in ((0, 1, 2),) if qt == 0 else ((0, 1), (2,)):
                        b = bank()
                        for i, g in enumerate(gs):
                            m = mm(ps[b][:, w * i:w * i + w], Q3[:, 4 * g + h, 128 * qt:128 * qt + 128],
                                   K3[:, 4 * g + h, 0:w], True, True, True, qk3[0])
                        o = 384 * qt + w * gs[0]
                        m = tt(DV, z[:, w * gs[0]:w * gs[0] + w * len(gs)], ps[b][:, 0:w * len(gs)],
                               ca[:, o:o + w * len(gs)], ALU.add, m, ms)
                        pfree[b] = m
                    mx, nm, den, rd = col(), col(), col(), col()
                    m = red(mx, z, ALU.max, m)
                    m = ts(DV, nm, mx, -1.0, ALU.mult, None, None, m)
                    m = act(z, z, ACT.Exp, m, bias=nm, accum_out=den)
                    m = recip(rd, den, m)
                    st[n] = ts(DV, z, z, rd, ALU.mult, None, None, m)

                def turns(n):
                    h, qt = items[n]
                    z = S3[n % 2]
                    pt = P3[n // 2 % 2]
                    f = p3_free[n // 2 % 2]
                    if qt == 0:
                        b = bank()
                        for g in range(3):
                            m = tr(ps[b][:, 128 * g:128 * g + 128], z[:, 128 * g:128 * g + 128], g == 2, st[n])
                        s3_free[n % 2] = m
                        m = copy(AC, pt[:, :, 0:128], ps[b][:, 0:384].rearrange("p (g t) -> p g t", g=3), m, f)
                        pfree[b] = m
                    else:
                        for gs in ((0, 1), (2,)):
                            b = bank()
                            for i, g in enumerate(gs):
                                for k in range(2):
                                    o = 256 * i + 128 * k
                                    m = tr(ps[b][:, o:o + 128], z[:, 256 * g + 128 * k:256 * g + 128 * k + 128],
                                           True, st[n])
                            s3_free[n % 2] = m
                            m = copy(AC, pt[:, gs[0]:gs[0] + len(gs), 128:384],
                                     ps[b][:, 0:256 * len(gs)].rearrange("p (g t) -> p g t", g=len(gs)), m, f)
                            pfree[b] = m
                    st[n] = m

                def values(n):
                    h, qt = items[n]
                    if qt == 0:
                        return
                    pt = P3[n // 2 % 2]
                    b = bank()
                    o = ps[b][:, 0:256]
                    for g in range(3):
                        mm(o, V3[:, 2 * g, 128 * h:128 * h + 128], pt[:, g, 0:256], g == 0, False, False, st[n], v3[0])
                        m = mm(ps[b][:, 128:256], V3[:, 2 * g + 1, 128 * h:128 * h + 128], pt[:, g, 256:384],
                               False, g == 2, g == 2)
                    p3_free[n // 2 % 2] = m
                    hh = 4 * half + h
                    mo = two_parts(Hhi[:, hh, 256:512], Hlo[:, hh, 256:512], o, m, h_free[0])
                    pfree[b] = mo
                    return mo, m

                for n in range(len(items) + 4):
                    if n < len(items):
                        scores(n)
                    if 0 <= n - 1 < len(items):
                        turns(n - 1)
                    if 0 <= n - 3 < len(items):
                        r_ = values(n - 3)
                        if r_:
                            mo, m_ = r_
                attended[0] = m_
                return mo

            for half in range(2):
                for g in range(3):
                    project([0, 1], lambda t, b, m: ev_qk(Q3, g, 128.0 ** -0.5, t, b, m), m_h)
                    project([0, 1], lambda t, b, m: ev_qk(K3, g, 1.0, t, b, m))
                    project([0, 1], lambda t, b, m: ev_v(g, t, b, m))
                flush()
                m_o = attend(half)
            bs, m_y = from_H(8, 2, m_o, 256)
            tiles = add(bs, m_y, tiles)
            for i, (x_, m_) in enumerate(tiles):
                taps(f"p{i}", x_, m_)
            check_stop()
            tiles = ffn2(0, tiles)
            for i, (x_, m_) in enumerate(tiles):
                taps(f"q{i}", x_, m_)
            check_stop()

            QK = at(U0, 8, 256)
            VM, OG, HO = at(U0 + 2048, 2, D), at(U0 + 4096, 2, D), at(U0 + 6144, 2, D)
            XP = [at(U0 + 8192, 260), at(U0 + 8452, 260)]
            CV = [at(U0 + 8712, 256), at(U0 + 8968, 256)]
            R0, R1 = [at(U0 + 9224 + 384 * i, 128) for i in range(2)], [at(U0 + 9352 + 384 * i, 256) for i in range(2)]
            DW = [at(384 * i, 384) for i in range(2)]
            SS = [at(768 + 384 * i, 384) for i in range(2)]
            ST = [at(1536 + 384 * i, 384) for i in range(2)]
            SQ = at(2304, D)
            GT = at(3328, 16, 2, 8)
            GB = at(3584, 16)
            Fs = at(3600, 2, 8)
            m_free = [m_y, h_free[0], (DV.sem, DV.n), (AC.sem, AC.n)]
            m_gb = [load("gb0", GB[:, 0:8], bass.AP(a["mlstm_ig_bias_2"].tensor, 0, [[0, 128], [1, 8]]), m_free),
                    load("gb1", GB[:, 8:16], bass.AP(a["mlstm_fg_bias_2"].tensor, 0, [[0, 128], [1, 8]]), m_free)]
            r, m_r = stats(tiles)
            m_h = pre(tiles, r, m_r, gain("mlstm_norm"))
            m_z = [ts(DV, XP[i][:, 0:3], vec[:, 0:3], 0.0, ALU.mult, None, None, m_free) for i in range(2)]
            AC.wait(m_free)
            xp_free, cv_free = [None, None], [None, None]
            PE.wait(m_h)
            for j in range(4):
                hi, lo = unit(8, 256)
                b2 = []
                for s in range(2):
                    b = bank()
                    for k in range(8):
                        m = mm3(ps[b][:, 0:256], (hi[:, k, 128 * s:128 * s + 128], lo[:, k, 128 * s:128 * s + 128]),
                                (Hhi[:, k, 0:256], Hlo[:, k, 0:256]), k == 0, k == 7, mark=(k == 7))
                    b2.append((b, m))
                for s, (b, mb) in enumerate(b2):
                    c_ = 2 * j + s
                    xp, cv = XP[s], CV[s]
                    mc = copy(AC, xp[:, 3:259], ps[b][:, 0:256], mb, xp_free[s])
                    pfree[b] = mc
                    w = lambda i: vec[:, VEC["conv_w"] + 8 * i + c_:VEC["conv_w"] + 8 * i + c_ + 1]
                    bi = vec[:, VEC["conv_b"] + c_:VEC["conv_b"] + c_ + 1]
                    mc = ts(DV, cv, xp[:, 3:259], w(3), ALU.mult, bi, ALU.add, mc, m_z, cv_free[s])
                    for i in range(3):
                        mc = stt(cv, xp[:, i:i + 256], w(i), cv, ALU.mult, ALU.add, mc)
                    xp_free[s] = mc
                    m_qk = act(QK[:, c_, :], cv, ACT.Silu, mc)
                    cv_free[s] = m_qk
                unit_done(m)
            hi, lo = unit(8, 16)
            b = bank()
            for t in range(2):
                for k in range(8):
                    m = mm3(ps[b][:, 16 * t:16 * t + 16], (Hhi[:, k, 128 * t:128 * t + 128],
                                                          Hlo[:, k, 128 * t:128 * t + 128]),
                            (hi[:, k, :], lo[:, k, :]), k == 0, k == 7, mark=(k == 7))
            unit_done(m)
            gv = ps[b][:, 0:32].rearrange("p (t g) -> p t g", t=2)
            IG, FG, NFG, AF, E, UE, DE, RU, LN, CO, MF, LF = [GT[:, i, :, :] for i in range(12)]
            gbb = lambda c0: GB[:, c0:c0 + 8].unsqueeze(1).to_broadcast([128, 2, 8])
            m_ig = tt(DV, IG, gv[:, :, 0:8], gbb(0), ALU.add, m, m_gb, m_free)
            m = tt(DV, FG, gv[:, :, 8:16], gbb(8), ALU.add)
            pfree[b] = m
            m = ts(DV, NFG, FG, -1.0, ALU.mult, None, None, m)
            m = tt(DV, AF, FG, NFG, ALU.max, m)
            m_f = ts(DV, MF, FG, 0.0, ALU.min, None, None)

            def ev_vo(dst, f, j, t, b, m):
                m = act(dst[:, t, 512 * j:512 * j + 512], ps[b][:, :], f, m)
                pfree[b] = m
                return m

            mv = []
            for j in range(2):
                project([0, 1], lambda t, b, m: mv.append(ev_vo(VM, ACT.Copy, j, t, b, m)))
            for j in range(2):
                m_pe = project([0, 1], lambda t, b, m: mv.append(ev_vo(OG, ACT.Sigmoid, j, t, b, m)))
            h_free[0] = m_pe
            m = act(E, AF, ACT.Exp, m, scale=-1.0)
            m = ts(DV, UE, E, 1.0, ALU.add, None, None, m)
            m_l = act(LN, UE, ACT.Ln, m)
            m = ts(DV, DE, UE, -1.0, ALU.add, None, None, m)
            m = tt(DV, CO, E, DE, ALU.subtract, m)
            m1 = recip(RU, UE)
            m = tt(DV, CO, CO, RU, ALU.mult, m, m1)
            m = tt(DV, LN, LN, CO, ALU.add, m, m_l)
            m_lf = tt(DV, LF, MF, LN, ALU.subtract, m, m_f)
            b = bank()
            mm(ps[b][:, 0:8], cs("upto"), LF[:, 0, :], True, True, True, m_lf, m_cst)
            mm(ps[b][:, 8:16], cs("upto"), LF[:, 1, :], True, False)
            m = mm(ps[b][:, 8:16], cs("ones"), LF[:, 0, :], False, True)
            m_F = copy(DV, Fs, ps[b][:, 0:16].rearrange("p (t h) -> p t h", t=2), m)
            pfree[b] = m_F
            r_free, d_free, ss_free, stt_free = [None, None], [None, None], [None, None], [None, None]
            st = {}

            def weights(h):
                q = h % 2
                rf = r_free[q]
                lf, ig = (lambda t: LF[:, t, h:h + 1]), (lambda t: IG[:, t, h:h + 1])
                m = ts(DV, R0[q], cs("after"), lf(0), ALU.mult, None, None, m_lf, rf)
                m = stt(R0[q], ident(), ig(0), R0[q], ALU.mult, ALU.add, m, m_ig)
                ma = ts(DV, R1[q][:, 0:128], cs("ones"), lf(1), ALU.mult, None, None)
                mb = ts(DV, R1[q][:, 128:256], cs("after"), lf(1), ALU.mult, None, None)
                mb = stt(R1[q][:, 128:256], ident(), ig(1), R1[q][:, 128:256], ALU.mult, ALU.add, mb)
                b = bank()
                mm(ps[b][:, 0:128], cs("upto"), R0[q], True, True, True, m, ma, mb)
                mm(ps[b][:, 128:384], cs("upto"), R1[q], True, False)
                m = mm(ps[b][:, 128:256], cs("ones"), R0[q], False, True)
                r_free[q] = m
                d = DW[q]
                nv = cs("never")
                m1 = tt(DV, d[:, 0:128], ps[b][:, 0:128], nv, ALU.add, m, d_free[q])
                m2 = copy(DV, d[:, 128:256], ps[b][:, 128:256])
                m3 = tt(DV, d[:, 256:384], ps[b][:, 256:384], nv, ALU.add)
                pfree[b] = m3
                mx, nm, en = col(2), col(2), col(2)
                ma = red(mx[:, 0:1], d[:, 0:128], ALU.max, m1)
                mb = red(mx[:, 1:2], d[:, 128:384], ALU.max, m2, m3)
                m = tt(DV, mx, mx, Fs[:, :, h], ALU.max, ma, mb, m_F)
                m = ts(DV, nm, mx, -1.0, ALU.mult, None, None, m)
                act(d[:, 0:128], d[:, 0:128], ACT.Exp, m, bias=nm[:, 0:1])
                act(d[:, 128:384], d[:, 128:384], ACT.Exp, bias=nm[:, 1:2])
                m_w = act(en, nm, ACT.Exp)
                b = bank()
                p0, c_ = 64 * (h % 2), h // 2
                mm(ps[b][:, 0:128], QK[p0:p0 + 64, c_, 0:128], QK[p0:p0 + 64, 4 + c_, 0:128], True, True, True, m_qk)
                m = mm(ps[b][:, 128:384], QK[p0:p0 + 64, c_, 128:256], QK[p0:p0 + 64, 4 + c_, 0:256])
                den, nd, rd = col(2), col(2), col(2)
                s_ = SS[q]
                m1 = stt(s_[:, 0:128], ps[b][:, 0:128], 0.125, d[:, 0:128], ALU.mult, ALU.mult, m, m_w, ss_free[q],
                         acc=den[:, 0:1])
                m2 = stt(s_[:, 128:384], ps[b][:, 128:384], 0.125, d[:, 128:384], ALU.mult, ALU.mult,
                         acc=den[:, 1:2])
                pfree[b] = m2
                d_free[q] = m2
                m = ts(DV, nd, den, -1.0, ALU.mult, None, None, m1, m2)
                m = tt(DV, den, den, nd, ALU.max, m)
                m = tt(DV, den, den, en, ALU.max, m)
                m_rd = recip(rd, den, m)
                st[h] = (m2, rd, m_rd)

            def outs(h):
                q = h % 2
                m2, rd, m_rd = st[h]
                b = bank()
                for k in range(3):
                    m = tr(ps[b][:, 128 * k:128 * k + 128], SS[q][:, 128 * k:128 * k + 128], k == 2, m2)
                ss_free[q] = m
                m = copy(AC, ST[q], ps[b][:, 0:384], m, stt_free[q])
                pfree[b] = m
                b = bank()
                c_ = slice(128 * h, 128 * h + 128)
                mm(ps[b][:, 0:128], ST[q][:, 0:128], VM[:, 0, c_], True, True, True, m, mv)
                mm(ps[b][:, 128:256], ST[q][:, 256:384], VM[:, 1, c_], True, False)
                m = mm(ps[b][:, 128:256], ST[q][:, 128:256], VM[:, 0, c_], False, True)
                stt_free[q] = m
                for t in range(2):
                    m = ts(DV, HO[:, t, c_], ps[b][:, 128 * t:128 * t + 128], rd[:, t:t + 1], ALU.mult, None, None,
                           m, m_rd)
                pfree[b] = m
                return m

            for h in range(9):
                if h < 8:
                    weights(h)
                if h >= 1:
                    m_ho = outs(h - 1)
            m_h2 = []
            for t in range(2):
                ho = HO[:, t, :]
                ss = col(8)
                m = tt(DV, SQ, ho, ho, ALU.mult, m_ho)
                m = red(ss, SQ.rearrange("p (h d) -> p h d", h=8), ALU.add, m)
                r, m_r = rstd(ss, 8, 1.0 / 128, m)
                m = tt(DV, ho.rearrange("p (h d) -> p h d", h=8), ho.rearrange("p (h d) -> p h d", h=8),
                       r.unsqueeze(2).to_broadcast([128, 8, 128]), ALU.mult, m_r)
                m = tt(DV, ho, ho, OG[:, t, :], ALU.mult, m, mv)
                g_, _, mg_ = gain("head_gain")(0)
                _, m_h = turn(t, ho, m, 128 * t, g_, None, mg_)
            bs, m_y = from_H(8, 2, m_h)
            tiles = add(bs, m_y, tiles)
            for i, (x_, m_) in enumerate(tiles):
                taps(f"r{i}", x_, m_)
            check_stop()
            tiles = ffn2(1, tiles)
            m_fn = load("fn", G[0], bass.AP(a["final_norm_2"].tensor, 0, [[0, 128], [1, D]]), g_free[0])
            r, m_r = stats(tiles)
            for t, (x_, m_) in enumerate(tiles):
                m = stt(XN[t], x_, r[:, t:t + 1], G[0], ALU.mult, ALU.mult, m_r, m_fn, xn_free[t])
                load(f"out{t}", out[0, 128 * t:128 * t + 128, :], XN[t], m)
        except Stop:
            pass

        for s, n in dsems.values():
            SP.wait((s, n))
        for ln in (PE, DV, AC, PO):
            SP.wait((ln.sem, ln.n))
        block = ctx.enter_context(nc.Block())

        @block.sync
        def _(e):
            SP.emit(e)

        @block.tensor
        def _(e):
            PE.emit(e)

        @block.vector
        def _(e):
            DV.emit(e)

        @block.scalar
        def _(e):
            AC.emit(e)

        @block.gpsimd
        def _(e):
            PO.emit(e)


def tables():
    f = np.float32
    c = np.zeros((128, NCST), f)

    def put(name, v):
        o, n = CST[name]
        c[:v.shape[0], o:o + n] = v.reshape(v.shape[0], n)

    put("ident", np.eye(128, dtype=f))
    tok = np.arange(256)
    inv = f(10000.0) ** (-np.arange(16, dtype=f) / f(16))
    t = np.zeros((256, 2, 2, 2, 16), f)
    for i, pos in enumerate((tok // 64, tok % 64)):
        ang = pos.astype(f)[:, None] * inv
        t[:, 0, i, 0], t[:, 0, i, 1] = np.cos(ang), np.cos(ang)
        t[:, 1, i, 0], t[:, 1, i, 1] = -np.sin(ang), np.sin(ang)
    put("rope", t.reshape(2, 128, 128).transpose(1, 0, 2).copy())
    j = np.arange(64)
    start = np.clip(j - 8, 0, 48)
    ok = (j[None] >= start[:, None]) & (j[None] < start[:, None] + 16)
    put("colmask", np.tile(np.where(ok, f(0), f(NEG)), (2, 1)).astype(f))

    def window(n, w):
        q = np.arange(n)
        lo, hi = np.clip(q - w // 2, 0, n), np.clip(q - w // 2 + w, 0, n)
        m = ((q[:, None] >= lo[None]) & (q[:, None] < hi[None])) / (hi - lo)[None]
        return (m - np.eye(n)).astype(f)

    px = np.zeros((128, 4, 128), f)
    pc = np.zeros((128, 4, 2, 256), f)
    for g, w in enumerate((2, 4, 8, 16)):
        for r in range(2):
            px[64 * r:64 * r + 64, g, 64 * r:64 * r + 64] = window(64, w)
        pc[:, g] = window(256, w).reshape(2, 128, 256).transpose(1, 0, 2)
    put("pool_x", px)
    put("pool_c", pc)
    i, k = np.arange(256)[:, None], np.arange(256)[None]
    ca = np.zeros((128, 1152), f)
    for g, (window_, dil) in enumerate(((128, 1), (512, 4), (2048, 16))):
        ok = (k <= i) & ((i - k) % dil == 0) & ((i - k) // dil <= window_ // dil)
        m = np.where(ok, f(0), f(NEG))
        ca[:, 128 * g:128 * g + 128] = m[0:128, 0:128]
        ca[:, 384 + 256 * g:384 + 256 * g + 256] = m[128:256]
    put("causal", ca)
    u, v = np.arange(128)[:, None], np.arange(128)[None]
    put("upto", (u <= v).astype(f))
    put("after", (u > v).astype(f))
    put("ones", np.ones((128, 128), f))
    put("never", np.where(v > u, f(NEG), f(0)).astype(f))
    sel = np.zeros((2, 2, 128), f)
    sel[0, 0], sel[1, 1] = 1, 1
    put("sel", sel)
    put("freq", np.tile(f(500000.0) ** (-np.arange(16, dtype=f) * f(2.0) / f(32)), (128, 1)))
    return c


def lay_out(inputs):
    x = {k: np.ascontiguousarray(np.asarray(v)) for k, v in inputs.items()}

    def cols(v):
        return v.reshape(-1, 128).T

    parts = [x["c"], x["c_ctx"], x["norm_g"], x["b_mod"], x["pool_scale"], x["attn_norm_2"], x["mlstm_norm_2"],
             x["ffn_norm_2"], x["mlstm_head_gain_2"], x["mlstm_conv_b_2"], x["mlstm_conv_w_2"]]
    arrays = {n: x[n] for n in BIG}
    arrays["vec"] = np.ascontiguousarray(np.concatenate([cols(p) for p in parts], axis=1))
    arrays["cst"] = tables()
    return arrays


BIG = ["x", "ctx", "w_mod", "b_mod", "norm_g", "w_ffn_gate_up", "w_ffn_down", "w_in", "w_out", "na_rpb", "w_pool",
       "positions_2", "attn_w_in_2", "attn_w_out_2", "mlstm_w_in_2", "mlstm_ig_bias_2", "mlstm_fg_bias_2",
       "mlstm_w_out_2", "ffn_w_in_2", "ffn_w_out_2", "final_norm_2"]


def kernel(**inputs):
    import concourse.bacc as bacc
    from concourse.bass_utils import run_bass_kernel_spmd

    nc = bacc.Bacc("TRN2", target_bir_lowering=False, num_devices=1)
    arrays = lay_out(inputs)
    args = {n: nc.dram_tensor(f"in_{n}", v.shape, mybir.dt.from_np(v.dtype), kind="ExternalInput").ap()
            for n, v in arrays.items()}
    out = nc.dram_tensor("out_0", (1, 256, D), F32, kind="ExternalOutput").ap()
    build(nc, args, out)
    r = run_bass_kernel_spmd(nc, [{f"in_{n}": v for n, v in arrays.items()}], core_ids=[0])
    return r.results[0]["out_0"]
```

```python
from contextlib import ExitStack

import numpy as np
import concourse.bass as bass
from concourse import mybir

F32 = mybir.dt.float32
F32R = mybir.dt.float32r
I32 = mybir.dt.int32
ALU = mybir.AluOpType
ACT = mybir.ActivationFunctionType
AX = mybir.AxisListType.X

D = 1024
DFF = 2816
NF = DFF // 128
EPS = 1e-6
NEG = -1e30
RAW = 2
CUT = 3
UN = 2048
NP = 8

VEC = {}
_at = 0
for _name, _n in [("c", 8), ("c_ctx", 8), ("norm_g", 96), ("b_mod", 144), ("pool_scale", 8), ("attn_norm", 8),
                  ("mlstm_norm", 8), ("ffn_norm", 16), ("head_gain", 8), ("conv_b", 8), ("conv_w", 32)]:
    VEC[_name] = _at
    _at += _n
NVEC = _at

CST = {}
_at = 0
for _name, _n in [("ident", 128), ("rope", 256), ("colmask", 64), ("pool_x", 512),
                  ("upto", 128), ("after", 128), ("ones", 128), ("never", 128), ("sel", 256),
                  ("freq", 16), ("pool_c", 2048), ("causal", 1152)]:
    CST[_name] = (_at, _n)
    _at += _n
NCST = _at


class Line:

    def __init__(self, sem):
        self.sem, self.n, self.items, self.seen = sem, 0, [], {}

    def wait(self, *marks):
        for m in marks:
            if m is None:
                continue
            if isinstance(m, list):
                self.wait(*m)
                continue
            sem, value = m
            if self.seen.get(sem.name, 0) < value:
                self.seen[sem.name] = value
                self.items.append(lambda e, s=sem, v=value: e.wait_ge(s, v))

    def do(self, fn, *waits, mark=True):
        self.wait(*waits)
        if not mark:
            self.items.append(fn)
            return None
        self.n += 1
        self.items.append(lambda e: fn(e).then_inc(self.sem, 1))
        return (self.sem, self.n)

    def emit(self, eng):
        for f in self.items:
            f(eng)


def build(nc, a, out, tap=None, stop=None):
    with ExitStack() as ctx:
        def sb(name, shape, dt=F32):
            return ctx.enter_context(nc.sbuf_tensor(name, shape, dt))

        def sem(name):
            return ctx.enter_context(nc.semaphore(name))

        raw = [sb(f"raw{i}", [128, UN]) for i in range(RAW)]
        whi = [sb(f"whi{i}", [128, UN], F32R) for i in range(CUT)]
        wlo = [sb(f"wlo{i}", [128, UN], F32R) for i in range(CUT)]
        Hhi = sb("Hhi", [128, 8, 512], F32R)
        Hlo = sb("Hlo", [128, 8, 512], F32R)
        X = sb("X", [128, 2, D])
        vec = sb("vec", [128, NVEC])
        cst = sb("cst", [128, CST["pool_c"][0]])
        sc32 = sb("sc32", [128, 8, 2])
        SM = 960
        dg = sb("dg", [128, 4, 128])
        small = sb("small", [128, SM])
        mods = sb("mods", [128, 6, 8, 2])
        mtmp = sb("mtmp", [128, 8, 2])
        posi = sb("posi", [128, 2], I32)
        AR = 22016
        arena = sb("arena", [128, AR])
        ps = [ctx.enter_context(nc.psum_tensor(f"ps{i}", [128, 512], F32)) for i in range(NP)]

        PE, DV, AC, PO, SP = [Line(sem(n)) for n in ("s_pe", "s_dve", "s_act", "s_pool", "s_sp")]
        s_raw = [sem(f"s_raw{i}") for i in range(RAW)]
        dsems = {}

        def load(key, dst, src, *waits, line=None):
            if key not in dsems:
                dsems[key] = [sem(f"s_{key}"), 0]
            line = line or SP
            s = dsems[key][0]
            if dsems[key][1]:
                line.wait((s, dsems[key][1]))
            dsems[key][1] += 16
            line.do(lambda e: e.dma_start(dst, src).then_inc(s, 16), *waits, mark=False)
            return (s, dsems[key][1])

        def at(off, *dims):
            n = int(np.prod(dims))
            assert off + n <= AR, (off, n)
            v = arena[:, off:off + n]
            if len(dims) == 2:
                v = v.rearrange("p (a b) -> p a b", a=dims[0])
            elif len(dims) == 3:
                v = v.rearrange("p (a b c) -> p a b c", a=dims[0], b=dims[1])
            return v

        def cs(name):
            o, n = CST[name]
            return cst[:, o:o + n]

        cols = [0]

        def col(n=1):
            if cols[0] + n > SM:
                cols[0] = 0
            cols[0] += n
            return small[:, cols[0] - n:cols[0]]

        C = at(0, 2, D)
        G = [at(2048, D), at(3072, D)]
        XN = [at(4096, D), at(5120, D)]
        HS = [at(6144, 512), at(6656, 512)]
        U0 = 7168

        def ident(n=128):
            return cst[0:n, 0:n]

        pfree = [None] * NP
        bank_at = [0]
        held = set()

        def bank():
            while bank_at[0] % NP in held:
                bank_at[0] += 1
            b = bank_at[0] % NP
            bank_at[0] += 1
            PE.wait(pfree[b])
            return b

        def kview(w, c0, c1):
            return w[:, c0:c1].rearrange("(k p) n -> p k n", p=128)

        def units_of(step):
            kind = step[0]
            if kind == "mod":
                w = kview(a["w_mod"][step[1]], step[2] * D, step[2] * D + D)
                return [(w[:, 4 * k:4 * k + 4, 512 * h:512 * h + 512], 4, 512) for h in range(2) for k in range(2)]
            if kind == "gu":
                w = step[1]
                return [(kview(w, g * DFF + 256 * j, g * DFF + 256 * j + 256), 8, 256)
                        for j in range(NF // 2) for g in range(2)]
            if kind == "out":
                w = kview(step[1], 0, D)
                return [(w[:, 2 * j:2 * j + 2, :], 2, D) for j in range(step[2] // 2)]
            if kind == "cols":
                w = kview(step[1], step[2], step[2] + 512)
                return [(w[:, 4 * k:4 * k + 4, :], 4, 512) for k in range(2)]
            if kind == "rows":
                return [(kview(step[1], step[2], step[2] + 256), 8, 256)]
            if kind == "gates":
                return [(kview(step[1], 3072, 3088), 8, 16)]
            raise ValueError(kind)

        gu1 = a["w_ffn_gate_up"]
        dn1 = a["w_ffn_down"]
        sched = [("mod", 0, 0), ("mod", 0, 1)]
        for l in range(2):
            sched += [("mod", l, 2), ("gu", gu1[l, 0]), ("out", dn1[l, 0], NF), ("mod", l, 3), ("mod", l, 4),
                      ("mod", l, 5)]
            sched += [("cols", a["w_in"][l], 512 * g) for g in range(4)]
            sched += [("out", a["w_out"][l], 8), ("mod", l, 6), ("mod", l, 7)]
            sched += [("mod", l, 8), ("gu", gu1[l, 1]), ("out", dn1[l, 1], NF)]
            if l == 0:
                sched += [("mod", 1, 0), ("mod", 1, 1)]
        sched += [("cols", a["attn_w_in_2"][0], (3 * g + t) * 1024 + 512 * h)
                  for h in range(2) for g in range(3) for t in range(3)]
        sched += [("out", a["attn_w_out_2"][0], 8), ("gu", a["ffn_w_in_2"][0]), ("out", a["ffn_w_out_2"][0], NF)]
        mw = a["mlstm_w_in_2"][0]
        sched += [("rows", mw, 256 * j) for j in range(4)]
        sched += [("gates", mw)] + [("cols", mw, 1024 + 512 * j) for j in range(4)]
        sched += [("out", a["mlstm_w_out_2"][0], 8), ("gu", a["ffn_w_in_2"][1]), ("out", a["ffn_w_out_2"][1], NF)]
        if stop:
            sched = sched[:stop]
        units = [u + (s[0] == "mod",) for s in sched for u in units_of(s)]
        nth, free, landed, cut_done, done_at = {}, {}, {}, {}, {}
        for n, u in enumerate(units):
            if not u[3]:
                nth[n] = len(nth)
        cut_units = sorted(nth)
        used, fetched, seen = [0], [0], [0]

        def fetch_one(n):
            src, k, m, _ = units[n]
            dst = raw[n % RAW][:, 0:k * m].rearrange("p (k m) -> p k m", k=k)
            s = s_raw[n % RAW]
            SP.do(lambda e: e.dma_start(dst, src).then_inc(s, 16), free.get(n - RAW), mark=False)
            landed[n] = (s, 16 * (n // RAW + 1))

        def advance():
            while True:
                n = fetched[0]
                if n < len(units) and (n < RAW or n - RAW in free):
                    fetch_one(n)
                    fetched[0] += 1
                    continue
                n = seen[0]
                if n >= fetched[0]:
                    return
                _, k, m, plain = units[n]
                if not plain:
                    c = nth[n]
                    if c >= CUT and cut_units[c - CUT] >= used[0]:
                        return
                    r, h, o = raw[n % RAW][:, 0:k * m], whi[c % CUT][:, 0:k * m], wlo[c % CUT][:, 0:k * m]
                    before = done_at.get(cut_units[c - CUT]) if c >= CUT else None
                    cut_done[n] = free[n] = two_parts(h, o, r, landed[n], before)
                seen[0] += 1

        def unit(k, m):
            n = used[0]
            assert units[n][1:3] == (k, m), (n, units[n][1:3], k, m)
            v = lambda t: t[:, 0:k * m].rearrange("p (k m) -> p k m", k=k)
            if units[n][3]:
                PE.wait(landed[n])
                return v(raw[n % RAW])
            PE.wait(cut_done[n])
            return v(whi[nth[n] % CUT]), v(wlo[nth[n] % CUT])

        def unit_done(mark):
            n = used[0]
            done_at[n] = mark
            if units[n][3]:
                free[n] = mark
            used[0] += 1
            advance()

        def mm3(o, A, B, start, stop, mark=False):
            PE.do(lambda e: e.matmul(o, A[0], B[1], start=start, stop=False), mark=False)
            PE.do(lambda e: e.matmul(o, A[1], B[0], start=False, stop=False), mark=False)
            return PE.do(lambda e: e.matmul(o, A[0], B[0], start=False, stop=stop), mark=mark)

        def mm(o, A, B, start=True, stop=True, mark=True, *waits):
            return PE.do(lambda e: e.matmul(o, A, B, start=start, stop=stop), *waits, mark=mark)

        def tr(o, i, mark=True, *waits):
            n = i.shape[0]
            return PE.do(lambda e: e.transpose(o, i, ident(n)), *waits, mark=mark)

        def tt(line, o, x, y, op, *waits):
            return line.do(lambda e: e.tensor_tensor(o, x, y, op), *waits)

        def ts(line, o, x, s1, op0, s2, op1, *waits):
            if op1 is None:
                return line.do(lambda e: e.tensor_scalar(o, x, s1, None, op0), *waits)
            return line.do(lambda e: e.tensor_scalar(o, x, s1, s2, op0, op1), *waits)

        def stt(o, x, s, y, op0, op1, *waits, acc=None):
            return DV.do(lambda e: e.scalar_tensor_tensor(out=o, in0=x, scalar=s, in1=y, op0=op0, op1=op1,
                                                          **({"accum_out": acc} if acc is not None else {})), *waits)

        def red(o, x, op, *waits):
            return DV.do(lambda e: e.tensor_reduce(o, x, AX, op), *waits)

        def recip(o, x, *waits):
            return DV.do(lambda e: e.reciprocal(o, x), *waits)

        def act(o, x, f, *waits, **kw):
            return AC.do(lambda e: e.activation(o, x, f, **kw), *waits)

        def copy(line, o, x, *waits):
            if line is AC:
                return act(o, x, ACT.Copy, *waits)
            return line.do(lambda e: e.tensor_copy(o, x), *waits)

        def two_parts(hi, lo, x, *waits):
            am = act(hi, x, ACT.Copy, *waits)
            return DV.do(lambda e: e.tensor_tensor(lo, x, hi.bitcast(F32), ALU.subtract), am)

        m_vec = load("vec", vec[:, :], a["vec"])
        advance()
        m_x = load("x", X[:, :, :], a["x"].rearrange("o (t p) d -> p (o t) d", p=128))
        m_c = load("c", C, a["ctx"].rearrange("o (t p) d -> p (o t) d", p=128))
        m_cst = load("cst", cst[:, :], a["cst"][:, 0:CST["pool_c"][0]])
        rpbs = nc.dram_tensor("rpbs", (64, 7440), F32).ap()
        m_rpb = load("rpb", rpbs, bass.AP(a["na_rpb"].tensor, 0, [[0, 64], [1, 7440]]))
        m_pos = [load(f"pos{t}", posi[:, t:t + 1], a["positions_2"][:, 128 * t:128 * t + 128].rearrange("o p -> p o"))
                 for t in range(2)]
        v2 = vec[:, 0:16].rearrange("p (s k) -> p k s", s=2)
        m = act(sc32[:, :, :], v2, ACT.Silu, m_vec)
        m_sc = m

        rope2 = sb("rope2", [128, 2, 2, 32])
        angs = sb("angs", [128, 6, 2, 16])
        posf, ANG, TT, KK, RR = small[:, SM - 2:SM], angs[:, 0], angs[:, 1], angs[:, 2], angs[:, 3]
        m = copy(DV, posf, posi[:, :], m_pos)
        for t in range(2):
            m1 = ts(DV, ANG[:, t, :], cs("freq"), posf[:, t:t + 1], ALU.mult, None, None, m, m_cst)
        m_ang = m1
        C1 = 6.28125
        C2 = round((2 * np.pi - C1) * 2.0 ** 18) / 2.0 ** 18
        C3 = float(np.float32(2 * np.pi - C1 - C2))
        m_r2 = []
        for f, (turns_, shift_) in enumerate([(0.25, float(np.float32(np.pi / 2))), (0.0, 0.0)]):
            m1 = ts(DV, TT, ANG, float(1 / (2 * np.pi)), ALU.mult, turns_, ALU.add, m_ang)
            m1 = ts(DV, KK, TT, 12582912.0, ALU.add, None, None, m1)
            m1 = ts(DV, KK, KK, -12582912.0, ALU.add, None, None, m1)
            m1 = stt(RR, KK, -C1, ANG, ALU.mult, ALU.add, m1)
            m1 = stt(RR, KK, -C2, RR, ALU.mult, ALU.add, m1)
            m1 = stt(RR, KK, -C3, RR, ALU.mult, ALU.add, m1)
            m1 = ts(DV, RR, RR, shift_, ALU.add, 3.1415925, ALU.min, m1)
            m1 = ts(DV, RR, RR, -3.1415925, ALU.max, None, None, m1)
            m1 = act(angs[:, 4 + f], RR, ACT.Sin, m1)
            DV.wait(m1)
            if f == 0:
                for z in range(2):
                    m_r2.append(copy(DV, rope2[:, :, 0, 16 * z:16 * z + 16], angs[:, 4]))
            else:
                m_r2.append(ts(DV, rope2[:, :, 1, 0:16], angs[:, 5], -1.0, ALU.mult, None, None))
                m_r2.append(copy(DV, rope2[:, :, 1, 16:32], angs[:, 5]))
        m_rope2 = m_r2

        MROW = U0 + 11264
        mrow = at(MROW, D)
        bg = at(MROW + 1024, 2, 512)
        U1 = U0
        mrow_free, bg_free, bb_free = [None], [None], [None]
        g_free = [None, None]
        g_ready = [None, None]
        mods_ready = {}
        mods_free = {}

        def mod(l, v, gain=None, half_gate=False):
            rows = []
            for h in range(2):
                b = bank()
                o = ps[b][0:2, :]
                if v % 3 == 2:
                    m_b = load("bg", bg[0:2, 0, :],
                               bass.AP(a["b_mod"].tensor, l * 9216 + v * D + 512 * h, [[0, 2], [1, 512]]),
                               bg_free[0], bb_free[0])
                    m_g = load("bh", bg[0:2, 1, :],
                               bass.AP(a["norm_g"].tensor, (l * 6 + gain) * D + 512 * h, [[0, 2], [1, 512]]),
                               bg_free[0], bb_free[0])
                for u in range(2):
                    w = unit(4, 512)
                    for k in range(4):
                        kt = 4 * u + k
                        m = mm(o, sc32[:, kt, :], w[:, k, :], kt == 0, kt == 7, k == 3)
                    if h == 0 and u == 0:
                        DV.wait(mrow_free[0], bb_free[0])
                    if u == 0:
                        unit_done(m)
                r = mrow[0:2, 512 * h:512 * h + 512]
                if v % 3 == 2:
                    m1 = tt(DV, r, o, bg[0:2, 0, :], ALU.add, m, m_b)
                    pfree[b] = m1
                    m2 = stt(r, r, 0.5 if half_gate else 1.0, bg[0:2, 1, :], ALU.mult, ALU.mult, m1, m_g)
                    bg_free[0] = m2
                    rows.append(m2)
                else:
                    m1 = copy(DV, r, o, m)
                    pfree[b] = m1
                    rows.append(m1)
                unit_done(m)
            if v % 3 == 2:
                for s in range(2):
                    for h in range(2):
                        b = bank()
                        m = mm(ps[b][:, :], cs("sel")[0:2, 128 * s:128 * s + 128],
                               mrow[0:2, 512 * h:512 * h + 512], True, True, True, rows)
                        pfree[b] = m1 = copy(AC, G[s][:, 512 * h:512 * h + 512], ps[b][:, :], m, g_free[s])
                    g_ready[s] = m1
                mrow_free[0] = m
            else:
                b = bank()
                for k in range(8):
                    m = tr(ps[b][:, 2 * k:2 * k + 2], mrow[0:2, 128 * k:128 * k + 128], k == 7, rows)
                mrow_free[0] = m
                i = v // 3 * 2 + v % 3
                o = mods[:, i, :, :]
                bT = vec[:, VEC["b_mod"] + 72 * l + 8 * v:VEC["b_mod"] + 72 * l + 8 * v + 8]
                bT = bT.unsqueeze(2).to_broadcast([128, 8, 2])
                pv = ps[b][:, 0:16].rearrange("p (k s) -> p k s", s=2)
                if v % 3 == 0:
                    m = tt(DV, o, pv, bT, ALU.add, m, mods_free.get(i))
                    pfree[b] = m
                else:
                    g0 = VEC["norm_g"] + 48 * l + 8 * gain
                    gT = vec[:, g0:g0 + 8].unsqueeze(2).to_broadcast([128, 8, 2])
                    m = tt(DV, mtmp[:, :, :], pv, bT, ALU.add, m)
                    pfree[b] = m
                    m = DV.do(lambda e: e.scalar_tensor_tensor(out=o, in0=mtmp[:, :, :], scalar=1.0, in1=gT,
                                                               op0=ALU.add, op1=ALU.mult), m, mods_free.get(i))
                mods_ready[i] = m

        h_free = [None]

        def rstd(ss, n, scale, *waits):
            v, q, r = col(n), col(n), col(n)
            m = ts(DV, v, ss, scale, ALU.mult, EPS, ALU.add, *waits)
            m = act(q, v, ACT.Sqrt, m)
            m = recip(r, q, m)
            return r, m

        xn_free = [None, None]
        hs_free = [None, None]
        hs_at = [0]

        evac_at = [0]

        def turn(i, src, m_src, pos, gain, shift, m_ab, q_dg=None):
            m_t = None
            for hb in range(2):
                b = bank()
                for k in range(4):
                    o, x_ = ps[b][:, 128 * k:128 * k + 128], src[:, 512 * hb + 128 * k:512 * hb + 128 * k + 128]
                    if q_dg is None:
                        m_t = tr(o, x_, k == 3, m_src)
                    else:
                        m_t = mm(o, x_, dg[:, q_dg, :], True, True, k == 3, m_src)
                q = hs_at[0] % 2
                hs_at[0] += 1
                h32 = HS[q].rearrange("p (k t) -> p k t", k=4)
                pv = ps[b][:, :].rearrange("p (k t) -> p k t", k=4)
                k0 = 4 * hb
                evac_at[0] += 1
                if evac_at[0] % 2:
                    gb = gain[:, k0:k0 + 4].unsqueeze(2).to_broadcast([128, 4, 128])
                    m = tt(DV, h32, pv, gb, ALU.mult, m_t, m_ab, hs_free[q])
                    pfree[b] = m
                    if shift is not None:
                        sbb = shift[:, k0:k0 + 4].unsqueeze(2).to_broadcast([128, 4, 128])
                        m = tt(DV, h32, h32, sbb, ALU.add, m)
                else:
                    for k in range(4):
                        kw = {"scale": gain[:, k0 + k:k0 + k + 1]}
                        if shift is not None:
                            kw["bias"] = shift[:, k0 + k:k0 + k + 1]
                        m = act(h32[:, k, :], pv[:, k, :], ACT.Identity, m_t, m_ab, hs_free[q], **kw)
                    pfree[b] = m
                m = two_parts(Hhi[:, k0:k0 + 4, pos:pos + 128], Hlo[:, k0:k0 + 4, pos:pos + 128], h32, m, h_free[0])
                hs_free[q] = m
            return m_t, m

        def pre(tiles, diag, ab):
            for i, (x, m) in enumerate(tiles):
                gain, shift, m_ab = ab(i)
                _, _, q, md = diag[i]
                dg_free[q], m_h = turn(i, x, [md, m] if not isinstance(m, list) else [md] + m, 128 * i, gain, shift,
                                       m_ab, q)
            return m_h

        def gate_up(T, m_h, act_at):
            A = at(act_at, NF, T)
            PE.wait(m_h)
            marks = {}
            for j in range(NF // 2):
                bs = [bank() for _ in range(4)]
                done = []
                for g in range(2):
                    hi, lo = unit(8, 256)
                    for s in range(2):
                        for k in range(8):
                            m = mm3(ps[bs[2 * g + s]][:, 0:T],
                                    (hi[:, k, 128 * s:128 * s + 128], lo[:, k, 128 * s:128 * s + 128]),
                                    (Hhi[:, k, 0:T], Hlo[:, k, 0:T]), k == 0, k == 7, mark=(k == 7))
                        done.append(m)
                    if g == 0:
                        unit_done(m)
                for s in range(2):
                    q = XN[s][:, 0:T]
                    m1 = act(q, ps[bs[s]][:, 0:T], ACT.Silu, done[s], xn_free[s])
                    pfree[bs[s]] = m1
                    m2 = tt(DV, A[:, 2 * j + s, :], q, ps[bs[2 + s]][:, 0:T], ALU.mult, m1, done[2 + s])
                    xn_free[s] = m2
                    pfree[bs[2 + s]] = m2
                    marks[2 * j + s] = m2
                unit_done(m)
            h_free[0] = m
            return A, marks

        def out_product(nk, nt, left):
            bs = {(t, h): bank() for t in range(nt) for h in range(2)}
            my = {}
            for j in range(nk // 2):
                hi, lo = unit(2, D)
                last = j == nk // 2 - 1
                ks = [2 * j, 2 * j + 1]
                order = [(k, [t]) for t in range(nt) for k in ks] if last else [(k, range(nt)) for k in ks]
                parts = {k: left(k) for k in ks}
                for k, tiles_ in order:
                    Lh, Ll, m_l, after = parts[k]
                    PE.wait(m_l)
                    for t in tiles_:
                        for h in range(2):
                            m = mm3(ps[bs[t, h]][:, :],
                                    (Lh[:, 128 * t:128 * t + 128], Ll[:, 128 * t:128 * t + 128]),
                                    (hi[:, k % 2, 512 * h:512 * h + 512], lo[:, k % 2, 512 * h:512 * h + 512]),
                                    k == 0, k == nk - 1, mark=(h == 1 and (last or t == nt - 1)))
                        if k == nk - 1:
                            my[t] = m
                    if not last:
                        after(m)
                unit_done(m)
            return bs, my, m

        def down(T, A, a_marks):
            parts, slot_free = {}, {}

            def part(k):
                if k < NF:
                    s = k % 8
                    hi, lo = Hhi[:, s, 0:T], Hlo[:, s, 0:T]
                    parts[k] = (hi, lo, two_parts(hi, lo, A[:, k, :], a_marks[k], h_free[0], slot_free.get(s)))

            for k in range(4):
                part(k)

            def left(k):
                def after(mark):
                    slot_free[k % 8] = mark
                    part(k + 4)
                return parts[k] + (after,)
            bs, my, m = out_product(NF, T // 128, left)
            h_free[0] = m
            return bs, my

        def from_H(nk, nt, m_h, off=0):
            PE.wait(m_h)
            bs, my, m = out_product(nk, nt, lambda k: (Hhi[:, k, off:512], Hlo[:, k, off:512], None,
                                                       lambda mark: None))
            h_free[0] = m
            return bs, my

        def skew(chains):
            for n in range(len(chains) + max(len(c) for c in chains) - 1):
                for t, c in enumerate(chains):
                    if 0 <= n - t < len(c):
                        c[n - t]()

        dg_at = [0]
        dg_free = [None] * 4

        def square(x, acc, *waits):
            hs_at[0] += 1
            q = hs_at[0] % 2
            hs_free[q] = act(HS[q], x, ACT.Square, *waits, hs_free[q], accum_out=acc)
            return hs_free[q]

        def rms_stages(x, marks, done):
            st = {}
            ss, s1 = col(2), col()

            def squares():
                for h in range(2):
                    m = square(x[:, 512 * h:512 * h + 512], ss[:, h:h + 1], marks()[h])
                st["m"] = tt(DV, s1, ss[:, 0:1], ss[:, 1:2], ALU.add, m)

            def root():
                r, m = rstd(s1, 1, 1.0 / D, st["m"])
                q = dg_at[0] % 4
                dg_at[0] += 1
                md = ts(DV, dg[:, q, :], ident(), r, ALU.mult, None, None, m, dg_free[q])
                done((r, m, q, md))
            return [squares, root]

        def post(bs, my, tiles, gs):
            res, diag = [None] * len(tiles), [None] * len(tiles)

            def chain(t):
                x, m_x = tiles[t]
                st = {}
                ss, s1 = col(2), col()
                b0, b1 = bs[t, 0], bs[t, 1]

                def y_squares():
                    m0 = square(ps[b0][:, :], ss[:, 0:1], my[t])
                    m1 = square(ps[b1][:, :], ss[:, 1:2], my[t])
                    st["m"] = tt(DV, s1, ss[:, 0:1], ss[:, 1:2], ALU.add, m0, m1)

                def y_root():
                    st["r"], st["m"] = rstd(s1, 1, 1.0 / D, st["m"])

                def update():
                    s = gs[t]
                    out_ = []
                    for h, b in enumerate((b0, b1)):
                        q = XN[h][:, 512 * (t % 2):512 * (t % 2) + 512]
                        xs = x[:, 512 * h:512 * h + 512]
                        m = stt(q, ps[b][:, :], st["r"], G[s][:, 512 * h:512 * h + 512], ALU.mult, ALU.mult,
                                st["m"], g_ready[s], xn_free[h])
                        pfree[b] = m
                        g_free[s] = m
                        m = tt(PO if h == 0 else DV, xs, xs, q, ALU.add, m, m_x)
                        xn_free[h] = m
                        out_.append(m)
                    st["x"] = out_
                    res[t] = (x, out_)

                def plain_update():
                    out_ = []
                    for h, b in enumerate((b0, b1)):
                        xs = x[:, 512 * h:512 * h + 512]
                        m = tt(DV, xs, xs, ps[b][:, :], ALU.add, my[t], m_x)
                        pfree[b] = m
                        out_.append(m)
                    st["x"] = out_
                    res[t] = (x, out_)

                def done(d):
                    diag[t] = d
                return ([y_squares, y_root, update] if gs else [plain_update]) + \
                    rms_stages(x, lambda: st["x"], done)

            skew([chain(t) for t in range(len(tiles))])
            return res, diag

        def first_stats(tiles):
            diag = [None] * len(tiles)

            def one(t):
                def done(d):
                    diag[t] = d
                return rms_stages(tiles[t][0], lambda: [tiles[t][1]] * 2, done)
            skew([one(t) for t in range(len(tiles))])
            return diag

        later = []

        def flush():
            todo = list(later)
            later.clear()
            for f in todo:
                f()

        def project(tts, evac, m_h=None):
            if m_h is not None:
                PE.wait(m_h)
            bs = {t: bank() for t in tts}
            last = {}
            for u in range(2):
                hi, lo = unit(4, 512)
                for t in tts:
                    for k in range(4):
                        kt = 4 * u + k
                        m = mm3(ps[bs[t]][:, :], (Hhi[:, kt, 128 * t:128 * t + 128], Hlo[:, kt, 128 * t:128 * t + 128]),
                                (hi[:, k, :], lo[:, k, :]), kt == 0, kt == 7, mark=(k == 3))
                    last[t] = m
                unit_done(m)
            flush()
            for i, t in enumerate(tts):
                if i == 2:
                    flush()
                evac(t, bs[t], last[t])
            return m

        QT = at(U1, 4, 512)
        KT = at(U1 + 2048, 4, 512)
        V = at(U1 + 4096, 4, 512)
        UU = at(U1 + 6144, 4, 512)
        S = [at(U1 + 8192, 512), at(U1 + 8704, 512)]
        PT_AT = U1 + 9216
        PT = [at(PT_AT, 4, 256), at(PT_AT + 1024, 4, 256)]
        BB = at(PT_AT + 2048, 8, 6, 64)
        ACT_AT = U1
        rope = cs("rope").rearrange("p (t c d) -> p t c d", t=2, c=2)

        def token_mix(l, m_h, m_act_free):
            ctx_out = l == 0
            bb = []
            for q in range(2):
                for i in range(6):
                    src = bass.AP(rpbs.tensor, 3720 * l + (5 - q + i) * 31 + 15, [[7439, 64], [465, 8], [1, 64]])
                    bb.append(load(f"bb{q}{i}", BB[64 * q:64 * q + 64, :, i, :], src, m_rpb, bb_free[0], mrow_free[0],
                                   bg_free[0], m_act_free))
            m_bb = DV.do(lambda e: e.tensor_tensor(
                BB.rearrange("p h i c -> p (h i) c"), BB.rearrange("p h i c -> p (h i) c"),
                cs("colmask").unsqueeze(1).to_broadcast([128, 48, 64]), ALU.add), bb, m_cst)
            tm = {}
            s_free = [None, None]

            def to_T(dst, scale, t, b, m):
                q = t % 2
                z = S[q]
                if t < 2:
                    ct = rope[:, t, 0, :].unsqueeze(1).to_broadcast([128, 8, 64])
                    m1 = tt(DV, XN[q][:, 0:512].rearrange("p (h d) -> p h d", h=8),
                            ps[b][:, :].rearrange("p (h d) -> p h d", h=8), ct, ALU.mult, m, xn_free[q], m_cst)
                    pv = ps[b][:, :].rearrange("p (h f d) -> p h f d", h=16, f=2)
                    xv = XN[q][:, 512:1024].rearrange("p (h f d) -> p h f d", h=16, f=2)
                    for f in range(2):
                        st = rope[:, t, 1, :].rearrange("p (r f d) -> p r f d", r=2, f=2)[:, :, f, :]
                        st = st.unsqueeze(1).to_broadcast([128, 8, 2, 16])
                        o4 = xv[:, :, f, :].rearrange("p (h r) d -> p h r d", r=2)
                        i4 = pv[:, :, 1 - f, :].rearrange("p (h r) d -> p h r d", r=2)
                        m2 = tt(DV, o4, i4, st, ALU.mult, m)
                    pfree[b] = m2
                    m = tt(PO, z, XN[q][:, 0:512], XN[q][:, 512:1024], ALU.add, m1, m2, s_free[q], m_act_free)
                    xn_free[q] = m
                else:
                    m = copy(AC, z, ps[b][:, :], m, s_free[q], m_act_free)
                    pfree[b] = m

                def turned():
                    b2 = bank()
                    for k in range(4):
                        m3 = tr(ps[b2][:, 128 * k:128 * k + 128], z[:, 128 * k:128 * k + 128], k == 3, m)
                    s_free[q] = m3
                    m4 = act(dst[:, :, 128 * t:128 * t + 128], ps[b2][:, :].rearrange("p (k t) -> p k t", k=4),
                             ACT.Copy, m3, scale=scale)
                    pfree[b2] = m4
                    tm["qk"] = m4
                later.append(turned)

            def keep(dst, name, t, b, m):
                m = copy(AC, dst[:, t, :], ps[b][:, :], m, m_act_free)
                pfree[b] = m
                tm[name] = m

            both, own = [0, 1, 2, 3], [0, 1]
            AC.wait(m_act_free)
            for g, (tts, ev) in enumerate([
                    (both if ctx_out else own, lambda t, b, m: to_T(QT, 0.125, t, b, m)),
                    (both, lambda t, b, m: to_T(KT, 1.0, t, b, m)),
                    (both, lambda t, b, m: keep(V, "v", t, b, m)),
                    (both if ctx_out else own, lambda t, b, m: keep(UU, "u", t, b, m))]):
                m_pe = project(tts, ev, m_h)
            flush()
            h_free[0] = m_pe
            m_wp = load("wp", WPOOL, a["w_pool"][l].rearrange("g c d -> c g d"), wp_free[0])

            items = [(h, qt) for h in range(8) for qt in (range(4) if ctx_out else range(2))]
            SR = [S[0], S[1]] + [XN[i][:, 512 * j:512 * j + 512] for i in range(2) for j in range(2)]
            sr_free = [s_free[0], s_free[1], xn_free[0], xn_free[0], xn_free[1], xn_free[1]]
            st = {}
            pt_free = [None, None]
            pair = {}

            def scores(n):
                h, qt = items[n]
                p0, hp = 64 * (h % 2), h // 2
                b = bank()
                k0 = 0 if qt < 2 else 256
                N = 512 - k0
                m = mm(ps[b][:, 0:N], QT[p0:p0 + 64, hp, 128 * qt:128 * qt + 128], KT[p0:p0 + 64, hp, k0:512],
                       True, True, True, tm["qk"])
                z = SR[n % 6][:, 0:N]
                if qt < 2:
                    i0 = 2 if qt == 0 else 0
                    m1 = DV.do(lambda e: e.tensor_tensor(
                        z[:, 0:256].rearrange("p (i c) -> p i c", i=4),
                        ps[b][:, 0:256].rearrange("p (i c) -> p i c", i=4), BB[:, h, i0:i0 + 4, :], ALU.add),
                        m, m_bb, sr_free[n % 6])
                    m2 = copy(DV, z[:, 256:512], ps[b][:, 256:512], m)
                    bb_free[0] = m1
                else:
                    m2 = copy(DV, z, ps[b][:, 0:N], m, sr_free[n % 6])
                pfree[b] = m2
                mx, nm, den, rd = col(), col(), col(), col()
                m = red(mx, z, ALU.max, m2)
                m = ts(DV, nm, mx, -1.0, ALU.mult, None, None, m)
                m = act(z, z, ACT.Exp, m, bias=nm, accum_out=den)
                m = recip(rd, den, m)
                m = ts(DV, z, z, rd, ALU.mult, None, None, m)
                st[n] = m

            def turns(n):
                h, qt = items[n]
                nb = 4 if qt < 2 else 2
                z = SR[n % 6]
                b = bank()
                for k in range(nb):
                    m = tr(ps[b][:, 128 * k:128 * k + 128], z[:, 128 * k:128 * k + 128], k == nb - 1, st[n])
                sr_free[n % 6] = m
                g = n // 2 % 2
                m = copy(AC, PT[g][:, 0:nb, 128 * (qt % 2):128 * (qt % 2) + 128],
                         ps[b][:, 0:128 * nb].rearrange("p (k t) -> p k t", k=nb), m, pt_free[g])
                pfree[b] = m
                st[n] = m

            def values(n):
                h, qt = items[n]
                if qt % 2 == 0:
                    return
                g = n // 2 % 2
                s = qt // 2
                p0 = 64 * (h % 2)
                if h % 2 == 0:
                    pair[s] = bank()
                    held.add(pair[s])
                b = pair[s]
                kb = range(4) if s == 0 else range(2, 4)
                for k in kb:
                    m = mm(ps[b][p0:p0 + 64, 0:256], V[:, k, 64 * h:64 * h + 64], PT[g][:, k - kb[0], :],
                           k == kb[0], k == 3, k == 3, st[n], tm["v"])
                pt_free[g] = m
                if h % 2:
                    o = 256 * s
                    hi, lo = Hhi[:, h // 2, o:o + 256], Hlo[:, h // 2, o:o + 256]
                    m = two_parts(hi, lo, ps[b][:, 0:256], m, h_free[0])
                    pfree[b] = m
                    held.discard(b)
                    tm["mix"] = m

            for n in range(len(items) + 5):
                if n < len(items):
                    scores(n)
                if 0 <= n - 3 < len(items):
                    turns(n - 3)
                if 0 <= n - 5 < len(items):
                    values(n - 5)
            s_free[0], s_free[1] = sr_free[0], sr_free[1]
            xn_free[0], xn_free[1] = sr_free[2:4], sr_free[4:6]

            T = 512 if ctx_out else 256
            if ctx_out:
                o, n_ = CST["pool_c"]
                m_pc = load("pc", at(PT_AT, 2048), a["cst"][:, o:o + n_], list(pt_free), st[len(items) - 1])
                pc = at(PT_AT, 4, 2, 256)
            px = cs("pool_x").rearrange("p (g t) -> p g t", g=4)
            for g in range(4):
                b = bank()
                for t in range(2):
                    m = mm(ps[b][:, 128 * t:128 * t + 128], UU[:, t, 128 * g:128 * g + 128], px[:, g, :],
                           True, True, True, tm["u"], m_cst)
                if ctx_out:
                    for t in range(2):
                        m = mm(ps[b][:, 256:512], UU[:, 2 + t, 128 * g:128 * g + 128], pc[:, g, t, :],
                               t == 0, t == 1, True, m_pc)
                q = g % 2
                z = S[q][:, 0:T]
                m = copy(AC, z, ps[b][:, 0:T], m, s_free[q])
                pfree[b] = m
                b = bank()
                m = mm(ps[b][:, 0:T], WPOOL[:, g, :], z, True, True, True, m, m_wp)
                s_free[q] = m
                wp_free[0] = m
                sc_ = VEC["pool_scale"] + 4 * l + g
                y = HS[q][:, 0:T]
                m = act(y, ps[b][:, 0:T], ACT.Copy, m, hs_free[q], scale=vec[:, sc_:sc_ + 1])
                pfree[b] = m
                m = two_parts(Hhi[:, 4 + g, 0:T], Hlo[:, 4 + g, 0:T], y, m, h_free[0])
                hs_free[q] = m
            return [m, tm["mix"]]

        WPOOL = at(PT_AT + 2048 + 3072, 4, 128)
        wp_free = [None]

        def xs(m0=None):
            return [(X[:, t, :], m0) for t in range(2)]

        def taps(name, ap, *marks):
            if tap is not None:
                tap(name, ap, SP, load, marks)

        tiles_x = xs(m_x)
        tiles_c = [(C[:, t, :], m_c) for t in range(2)]

        class Stop(Exception):
            pass

        def check_stop():
            if stop and used[0] >= len(units):
                raise Stop

        def ab(v):
            def f(i):
                s = 0 if i < 2 else 1
                return (mods[:, v // 3 * 2 + 1, :, s], mods[:, v // 3 * 2, :, s],
                        [mods_ready[v // 3 * 2], mods_ready[v // 3 * 2 + 1]])
            return f

        try:
            PE.wait(m_sc, m_cst)
            DV.wait(m_cst)
            act_free = None
            tiles = tiles_x + tiles_c
            diag = first_stats(tiles)
            mod(0, 0)
            mod(0, 1, gain=0)
            for l in range(2):
                m_h = pre(tiles, diag, ab(0))
                mods_free[0] = mods_free[1] = m_h
                mod(l, 2, gain=1, half_gate=True)
                A, am = gate_up(512, m_h, ACT_AT)
                bs, m_y = down(512, A, am)
                act_free = [h_free[0], (DV.sem, DV.n)]
                tiles, diag = post(bs, m_y, tiles, [0, 0, 1, 1])
                for i, (x_, m_) in enumerate(tiles):
                    taps(f"l{l}a{i}", x_, m_)
                check_stop()
                mod(l, 3)
                mod(l, 4, gain=2)
                m_h = pre(tiles, diag, ab(3))
                mods_free[2] = mods_free[3] = m_h
                mod(l, 5, gain=3)
                m_mix = token_mix(l, m_h, act_free)
                if l == 1:
                    tiles = tiles[0:2]
                nt = len(tiles)
                bs, m_y = from_H(8, nt, m_mix)
                tiles, diag = post(bs, m_y, tiles, [0, 0, 1, 1])
                for i, (x_, m_) in enumerate(tiles):
                    taps(f"l{l}b{i}", x_, m_)
                check_stop()
                mod(l, 6)
                mod(l, 7, gain=4)
                m_h = pre(tiles, diag, ab(6))
                mods_free[4] = mods_free[5] = m_h
                mod(l, 8, gain=5, half_gate=True)
                A, am = gate_up(128 * nt, m_h, ACT_AT)
                bs, m_y = down(128 * nt, A, am)
                tiles, diag = post(bs, m_y, tiles, [0, 0, 1, 1])
                for i, (x_, m_) in enumerate(tiles):
                    taps(f"l{l}c{i}", x_, m_)
                check_stop()
                if l == 0:
                    mod(1, 0)
                    mod(1, 1, gain=0)

            def gain(name, n=0):
                v = vec[:, VEC[name] + 8 * n:VEC[name] + 8 * n + 8]
                return lambda i: (v, None, m_vec)

            def ffn2(n, tiles, diag):
                m_h = pre(tiles, diag, gain("ffn_norm", n))
                A, am = gate_up(256, m_h, ACT_AT)
                bs, my = down(256, A, am)
                return post(bs, my, tiles, None)

            m_h = pre(tiles, diag, gain("attn_norm"))
            region_free = [ h_free[0], (DV.sem, DV.n)]
            Q3, K3, V3 = at(U0, 12, 256), at(U0 + 3072, 12, 256), at(U0 + 6144, 6, 512)
            S3 = [at(U0 + 9216, 768), at(U0 + 9984, 768)]
            P3 = [at(1152, 3, 384), at(2304, 3, 384)]
            o_, n_ = CST["causal"]
            m_ca = load("pc", at(0, n_), a["cst"][:, o_:o_ + n_], region_free, (PO.sem, PO.n))
            qk3, v3 = [None], [None]
            s3_free, p3_free = [None, None], [None, None]
            attended = [region_free]

            def ev_qk(dst, g, scale, t, b, m):
                q = t % 2
                z = XN[q][:, 0:512]
                z4 = z.rearrange("p (h d) -> p h d", h=4)
                t1 = XN[q][:, 512:640].rearrange("p (h d) -> p h d", h=4)
                t2 = XN[q][:, 640:768].rearrange("p (h d) -> p h d", h=4)
                m = copy(AC, z, ps[b][:, :], m, xn_free[q])
                pfree[b] = m
                cc = rope2[:, t, 0, :].unsqueeze(1).to_broadcast([128, 4, 32])
                m1 = tt(DV, t1, z4[:, :, 0:32], cc, ALU.mult, m, m_rope2)
                for f in range(2):
                    sn = rope2[:, t, 1, 16 * f:16 * f + 16].unsqueeze(1).to_broadcast([128, 4, 16])
                    m2 = tt(DV, t2[:, :, 16 * f:16 * f + 16], z4[:, :, 16 - 16 * f:32 - 16 * f], sn, ALU.mult, m)
                m = tt(DV, z4[:, :, 0:32], t1, t2, ALU.add, m1, m2)

                def turned():
                    b2 = bank()
                    for k in range(4):
                        mt = tr(ps[b2][:, 128 * k:128 * k + 128], z[:, 128 * k:128 * k + 128], k == 3, m)
                    xn_free[q] = mt
                    mt = act(dst[:, 4 * g:4 * g + 4, 128 * t:128 * t + 128],
                             ps[b2][:, :].rearrange("p (k t) -> p k t", k=4), ACT.Copy, mt, attended[0], scale=scale)
                    pfree[b2] = mt
                    qk3[0] = mt
                later.append(turned)

            def ev_v(g, t, b, m):
                m = copy(AC, V3[:, 2 * g + t, :], ps[b][:, :], m, attended[0])
                pfree[b] = m
                v3[0] = m

            def attend(half):
                items = [(h, qt) for h in range(4) for qt in range(2)]
                st = {}
                ca = at(0, 1152)

                def scores(n):
                    h, qt = items[n]
                    w = 128 * (qt + 1)
                    z = S3[n % 2][:, 0:3 * w]
                    ms = [s3_free[n % 2], m_ca]
                    for gs in ((0, 1, 2),) if qt == 0 else ((0, 1), (2,)):
                        b = bank()
                        for i, g in enumerate(gs):
                            m = mm(ps[b][:, w * i:w * i + w], Q3[:, 4 * g + h, 128 * qt:128 * qt + 128],
                                   K3[:, 4 * g + h, 0:w], True, True, True, qk3[0])
                        o = 384 * qt + w * gs[0]
                        m = tt(DV, z[:, w * gs[0]:w * gs[0] + w * len(gs)], ps[b][:, 0:w * len(gs)],
                               ca[:, o:o + w * len(gs)], ALU.add, m, ms)
                        pfree[b] = m
                    mx, nm, den, rd = col(), col(), col(), col()
                    m = red(mx, z, ALU.max, m)
                    m = ts(DV, nm, mx, -1.0, ALU.mult, None, None, m)
                    m = act(z, z, ACT.Exp, m, bias=nm, accum_out=den)
                    m = recip(rd, den, m)
                    st[n] = ts(DV, z, z, rd, ALU.mult, None, None, m)

                def turns(n):
                    h, qt = items[n]
                    z = S3[n % 2]
                    pt = P3[n // 2 % 2]
                    f = p3_free[n // 2 % 2]
                    if qt == 0:
                        b = bank()
                        for g in range(3):
                            m = tr(ps[b][:, 128 * g:128 * g + 128], z[:, 128 * g:128 * g + 128], g == 2, st[n])
                        s3_free[n % 2] = m
                        m = copy(AC, pt[:, :, 0:128], ps[b][:, 0:384].rearrange("p (g t) -> p g t", g=3), m, f)
                        pfree[b] = m
                    else:
                        for gs in ((0, 1), (2,)):
                            b = bank()
                            for i, g in enumerate(gs):
                                for k in range(2):
                                    o = 256 * i + 128 * k
                                    m = tr(ps[b][:, o:o + 128], z[:, 256 * g + 128 * k:256 * g + 128 * k + 128],
                                           True, st[n])
                            s3_free[n % 2] = m
                            m = copy(AC, pt[:, gs[0]:gs[0] + len(gs), 128:384],
                                     ps[b][:, 0:256 * len(gs)].rearrange("p (g t) -> p g t", g=len(gs)), m, f)
                            pfree[b] = m
                    st[n] = m

                def values(n):
                    h, qt = items[n]
                    if qt == 0:
                        return
                    pt = P3[n // 2 % 2]
                    b = bank()
                    o = ps[b][:, 0:256]
                    for g in range(3):
                        mm(o, V3[:, 2 * g, 128 * h:128 * h + 128], pt[:, g, 0:256], g == 0, False, False, st[n], v3[0])
                        m = mm(ps[b][:, 128:256], V3[:, 2 * g + 1, 128 * h:128 * h + 128], pt[:, g, 256:384],
                               False, g == 2, g == 2)
                    p3_free[n // 2 % 2] = m
                    hh = 4 * half + h
                    mo = two_parts(Hhi[:, hh, 256:512], Hlo[:, hh, 256:512], o, m, h_free[0])
                    pfree[b] = mo
                    return mo, m

                for n in range(len(items) + 4):
                    if n < len(items):
                        scores(n)
                    if 0 <= n - 1 < len(items):
                        turns(n - 1)
                    if 0 <= n - 3 < len(items):
                        r_ = values(n - 3)
                        if r_:
                            mo, m_ = r_
                attended[0] = m_
                return mo

            for half in range(2):
                for g in range(3):
                    project([0, 1], lambda t, b, m: ev_qk(Q3, g, 128.0 ** -0.5, t, b, m), m_h)
                    project([0, 1], lambda t, b, m: ev_qk(K3, g, 1.0, t, b, m))
                    project([0, 1], lambda t, b, m: ev_v(g, t, b, m))
                flush()
                m_o = attend(half)
            bs, m_y = from_H(8, 2, m_o, 256)
            tiles, diag = post(bs, m_y, tiles, None)
            for i, (x_, m_) in enumerate(tiles):
                taps(f"p{i}", x_, m_)
            check_stop()
            tiles, diag = ffn2(0, tiles, diag)
            for i, (x_, m_) in enumerate(tiles):
                taps(f"q{i}", x_, m_)
            check_stop()

            QK = at(U0, 8, 256)
            VM, OG, HO = at(U0 + 2048, 2, D), at(U0 + 4096, 2, D), at(U0 + 6144, 2, D)
            XP = [at(U0 + 8192, 260), at(U0 + 8452, 260)]
            CV = [at(U0 + 8712, 256), at(U0 + 8968, 256)]
            R0, R1 = [at(U0 + 9224 + 384 * i, 128) for i in range(2)], [at(U0 + 9352 + 384 * i, 256) for i in range(2)]
            DW = [at(384 * i, 384) for i in range(2)]
            SS = [at(768 + 384 * i, 384) for i in range(2)]
            ST = [at(1536 + 384 * i, 384) for i in range(2)]
            SQ = at(2304, D)
            GT = at(3328, 16, 2, 8)
            GB = at(3584, 16)
            Fs = at(3600, 2, 8)
            m_free = [h_free[0], (DV.sem, DV.n), (AC.sem, AC.n)]
            m_gb = [load("gb0", GB[:, 0:8], bass.AP(a["mlstm_ig_bias_2"].tensor, 0, [[0, 128], [1, 8]]), m_free),
                    load("gb1", GB[:, 8:16], bass.AP(a["mlstm_fg_bias_2"].tensor, 0, [[0, 128], [1, 8]]), m_free)]
            m_h = pre(tiles, diag, gain("mlstm_norm"))
            m_z = [ts(DV, XP[i][:, 0:3], vec[:, 0:3], 0.0, ALU.mult, None, None, m_free) for i in range(2)]
            AC.wait(m_free)
            xp_free, cv_free = [None, None], [None, None]
            PE.wait(m_h)
            for j in range(4):
                hi, lo = unit(8, 256)
                b2 = []
                for s in range(2):
                    b = bank()
                    for k in range(8):
                        m = mm3(ps[b][:, 0:256], (hi[:, k, 128 * s:128 * s + 128], lo[:, k, 128 * s:128 * s + 128]),
                                (Hhi[:, k, 0:256], Hlo[:, k, 0:256]), k == 0, k == 7, mark=(k == 7))
                    b2.append((b, m))
                for s, (b, mb) in enumerate(b2):
                    c_ = 2 * j + s
                    xp, cv = XP[s], CV[s]
                    mc = copy(AC, xp[:, 3:259], ps[b][:, 0:256], mb, xp_free[s])
                    pfree[b] = mc
                    w = lambda i: vec[:, VEC["conv_w"] + 8 * i + c_:VEC["conv_w"] + 8 * i + c_ + 1]
                    bi = vec[:, VEC["conv_b"] + c_:VEC["conv_b"] + c_ + 1]
                    mc = ts(DV, cv, xp[:, 3:259], w(3), ALU.mult, bi, ALU.add, mc, m_z, cv_free[s])
                    for i in range(3):
                        mc = stt(cv, xp[:, i:i + 256], w(i), cv, ALU.mult, ALU.add, mc)
                    xp_free[s] = mc
                    m_qk = act(QK[:, c_, :], cv, ACT.Silu, mc)
                    cv_free[s] = m_qk
                unit_done(m)
            hi, lo = unit(8, 16)
            b = bank()
            for t in range(2):
                for k in range(8):
                    m = mm3(ps[b][:, 16 * t:16 * t + 16], (Hhi[:, k, 128 * t:128 * t + 128],
                                                          Hlo[:, k, 128 * t:128 * t + 128]),
                            (hi[:, k, :], lo[:, k, :]), k == 0, k == 7, mark=(k == 7))
            unit_done(m)
            gv = ps[b][:, 0:32].rearrange("p (t g) -> p t g", t=2)
            IG, FG, NFG, AF, E, UE, DE, RU, LN, CO, MF, LF = [GT[:, i, :, :] for i in range(12)]
            gbb = lambda c0: GB[:, c0:c0 + 8].unsqueeze(1).to_broadcast([128, 2, 8])
            m_ig = tt(DV, IG, gv[:, :, 0:8], gbb(0), ALU.add, m, m_gb, m_free)
            m = tt(DV, FG, gv[:, :, 8:16], gbb(8), ALU.add)
            pfree[b] = m
            m = ts(DV, NFG, FG, -1.0, ALU.mult, None, None, m)
            m = tt(DV, AF, FG, NFG, ALU.max, m)
            m_f = ts(DV, MF, FG, 0.0, ALU.min, None, None)

            def ev_vo(dst, f, j, t, b, m):
                m = act(dst[:, t, 512 * j:512 * j + 512], ps[b][:, :], f, m)
                pfree[b] = m
                return m

            mv = []
            for j in range(2):
                project([0, 1], lambda t, b, m: mv.append(ev_vo(VM, ACT.Copy, j, t, b, m)))
            for j in range(2):
                m_pe = project([0, 1], lambda t, b, m: mv.append(ev_vo(OG, ACT.Sigmoid, j, t, b, m)))
            h_free[0] = m_pe
            m = act(E, AF, ACT.Exp, m, scale=-1.0)
            m = ts(DV, UE, E, 1.0, ALU.add, None, None, m)
            m_l = act(LN, UE, ACT.Ln, m)
            m = ts(DV, DE, UE, -1.0, ALU.add, None, None, m)
            m = tt(DV, CO, E, DE, ALU.subtract, m)
            m1 = recip(RU, UE)
            m = tt(DV, CO, CO, RU, ALU.mult, m, m1)
            m = tt(DV, LN, LN, CO, ALU.add, m, m_l)
            m_lf = tt(DV, LF, MF, LN, ALU.subtract, m, m_f)
            b = bank()
            mm(ps[b][:, 0:8], cs("upto"), LF[:, 0, :], True, True, True, m_lf, m_cst)
            mm(ps[b][:, 8:16], cs("upto"), LF[:, 1, :], True, False)
            m = mm(ps[b][:, 8:16], cs("ones"), LF[:, 0, :], False, True)
            m_F = copy(DV, Fs, ps[b][:, 0:16].rearrange("p (t h) -> p t h", t=2), m)
            pfree[b] = m_F
            r_free, d_free, ss_free, stt_free = [None, None], [None, None], [None, None], [None, None]
            st = {}

            def weights(h):
                q = h % 2
                rf = r_free[q]
                lf, ig = (lambda t: LF[:, t, h:h + 1]), (lambda t: IG[:, t, h:h + 1])
                m = ts(DV, R0[q], cs("after"), lf(0), ALU.mult, None, None, m_lf, rf)
                m = stt(R0[q], ident(), ig(0), R0[q], ALU.mult, ALU.add, m, m_ig)
                ma = ts(DV, R1[q][:, 0:128], cs("ones"), lf(1), ALU.mult, None, None)
                mb = ts(DV, R1[q][:, 128:256], cs("after"), lf(1), ALU.mult, None, None)
                mb = stt(R1[q][:, 128:256], ident(), ig(1), R1[q][:, 128:256], ALU.mult, ALU.add, mb)
                b = bank()
                mm(ps[b][:, 0:128], cs("upto"), R0[q], True, True, True, m, ma, mb)
                mm(ps[b][:, 128:384], cs("upto"), R1[q], True, False)
                m = mm(ps[b][:, 128:256], cs("ones"), R0[q], False, True)
                r_free[q] = m
                d = DW[q]
                nv = cs("never")
                m1 = tt(DV, d[:, 0:128], ps[b][:, 0:128], nv, ALU.add, m, d_free[q])
                m2 = copy(DV, d[:, 128:256], ps[b][:, 128:256])
                m3 = tt(DV, d[:, 256:384], ps[b][:, 256:384], nv, ALU.add)
                pfree[b] = m3
                mx, nm, en = col(2), col(2), col(2)
                ma = red(mx[:, 0:1], d[:, 0:128], ALU.max, m1)
                mb = red(mx[:, 1:2], d[:, 128:384], ALU.max, m2, m3)
                m = tt(DV, mx, mx, Fs[:, :, h], ALU.max, ma, mb, m_F)
                m = ts(DV, nm, mx, -1.0, ALU.mult, None, None, m)
                act(d[:, 0:128], d[:, 0:128], ACT.Exp, m, bias=nm[:, 0:1])
                act(d[:, 128:384], d[:, 128:384], ACT.Exp, bias=nm[:, 1:2])
                m_w = act(en, nm, ACT.Exp)
                b = bank()
                p0, c_ = 64 * (h % 2), h // 2
                mm(ps[b][:, 0:128], QK[p0:p0 + 64, c_, 0:128], QK[p0:p0 + 64, 4 + c_, 0:128], True, True, True, m_qk)
                m = mm(ps[b][:, 128:384], QK[p0:p0 + 64, c_, 128:256], QK[p0:p0 + 64, 4 + c_, 0:256])
                den, nd, rd = col(2), col(2), col(2)
                s_ = SS[q]
                m1 = stt(s_[:, 0:128], ps[b][:, 0:128], 0.125, d[:, 0:128], ALU.mult, ALU.mult, m, m_w, ss_free[q],
                         acc=den[:, 0:1])
                m2 = stt(s_[:, 128:384], ps[b][:, 128:384], 0.125, d[:, 128:384], ALU.mult, ALU.mult,
                         acc=den[:, 1:2])
                pfree[b] = m2
                d_free[q] = m2
                m = ts(DV, nd, den, -1.0, ALU.mult, None, None, m1, m2)
                m = tt(DV, den, den, nd, ALU.max, m)
                m = tt(DV, den, den, en, ALU.max, m)
                m_rd = recip(rd, den, m)
                st[h] = (m2, rd, m_rd)

            def outs(h):
                q = h % 2
                m2, rd, m_rd = st[h]
                b = bank()
                for k in range(3):
                    m = tr(ps[b][:, 128 * k:128 * k + 128], SS[q][:, 128 * k:128 * k + 128], k == 2, m2)
                ss_free[q] = m
                m = copy(AC, ST[q], ps[b][:, 0:384], m, stt_free[q])
                pfree[b] = m
                b = bank()
                c_ = slice(128 * h, 128 * h + 128)
                mm(ps[b][:, 0:128], ST[q][:, 0:128], VM[:, 0, c_], True, True, True, m, mv)
                mm(ps[b][:, 128:256], ST[q][:, 256:384], VM[:, 1, c_], True, False)
                m = mm(ps[b][:, 128:256], ST[q][:, 128:256], VM[:, 0, c_], False, True)
                stt_free[q] = m
                for t in range(2):
                    m = ts(DV, HO[:, t, c_], ps[b][:, 128 * t:128 * t + 128], rd[:, t:t + 1], ALU.mult, None, None,
                           m, m_rd)
                pfree[b] = m
                return m

            for h in range(9):
                if h < 8:
                    weights(h)
                if h >= 1:
                    m_ho = outs(h - 1)
            m_h2 = []
            for t in range(2):
                ho = HO[:, t, :]
                ss = col(8)
                m = tt(DV, SQ, ho, ho, ALU.mult, m_ho)
                m = red(ss, SQ.rearrange("p (h d) -> p h d", h=8), ALU.add, m)
                r, m_r = rstd(ss, 8, 1.0 / 128, m)
                m = tt(DV, ho.rearrange("p (h d) -> p h d", h=8), ho.rearrange("p (h d) -> p h d", h=8),
                       r.unsqueeze(2).to_broadcast([128, 8, 128]), ALU.mult, m_r)
                m = tt(DV, ho, ho, OG[:, t, :], ALU.mult, m, mv)
                g_, _, mg_ = gain("head_gain")(0)
                _, m_h = turn(t, ho, m, 128 * t, g_, None, mg_)
            bs, m_y = from_H(8, 2, m_h)
            tiles, diag = post(bs, m_y, tiles, None)
            for i, (x_, m_) in enumerate(tiles):
                taps(f"r{i}", x_, m_)
            check_stop()
            tiles, diag = ffn2(1, tiles, diag)
            m_fn = load("fn", G[0], bass.AP(a["final_norm_2"].tensor, 0, [[0, 128], [1, D]]), g_free[0])
            for t, (x_, m_) in enumerate(tiles):
                m = stt(XN[t], x_, diag[t][0], G[0], ALU.mult, ALU.mult, diag[t][1], m_fn, xn_free[t])
                load(f"out{t}", out[0, 128 * t:128 * t + 128, :], XN[t], m)
        except Stop:
            pass

        for s, n in dsems.values():
            SP.wait((s, n))
        for ln in (PE, DV, AC, PO):
            SP.wait((ln.sem, ln.n))
        block = ctx.enter_context(nc.Block())

        @block.sync
        def _(e):
            SP.emit(e)

        @block.tensor
        def _(e):
            PE.emit(e)

        @block.vector
        def _(e):
            DV.emit(e)

        @block.scalar
        def _(e):
            AC.emit(e)

        @block.gpsimd
        def _(e):
            PO.emit(e)


def tables():
    f = np.float32
    c = np.zeros((128, NCST), f)

    def put(name, v):
        o, n = CST[name]
        c[:v.shape[0], o:o + n] = v.reshape(v.shape[0], n)

    put("ident", np.eye(128, dtype=f))
    tok = np.arange(256)
    inv = f(10000.0) ** (-np.arange(16, dtype=f) / f(16))
    t = np.zeros((256, 2, 2, 2, 16), f)
    for i, pos in enumerate((tok // 64, tok % 64)):
        ang = pos.astype(f)[:, None] * inv
        t[:, 0, i, 0], t[:, 0, i, 1] = np.cos(ang), np.cos(ang)
        t[:, 1, i, 0], t[:, 1, i, 1] = -np.sin(ang), np.sin(ang)
    put("rope", t.reshape(2, 128, 128).transpose(1, 0, 2).copy())
    j = np.arange(64)
    start = np.clip(j - 8, 0, 48)
    ok = (j[None] >= start[:, None]) & (j[None] < start[:, None] + 16)
    put("colmask", np.tile(np.where(ok, f(0), f(NEG)), (2, 1)).astype(f))

    def window(n, w):
        q = np.arange(n)
        lo, hi = np.clip(q - w // 2, 0, n), np.clip(q - w // 2 + w, 0, n)
        m = ((q[:, None] >= lo[None]) & (q[:, None] < hi[None])) / (hi - lo)[None]
        return (m - np.eye(n)).astype(f)

    px = np.zeros((128, 4, 128), f)
    pc = np.zeros((128, 4, 2, 256), f)
    for g, w in enumerate((2, 4, 8, 16)):
        for r in range(2):
            px[64 * r:64 * r + 64, g, 64 * r:64 * r + 64] = window(64, w)
        pc[:, g] = window(256, w).reshape(2, 128, 256).transpose(1, 0, 2)
    put("pool_x", px)
    put("pool_c", pc)
    i, k = np.arange(256)[:, None], np.arange(256)[None]
    ca = np.zeros((128, 1152), f)
    for g, (window_, dil) in enumerate(((128, 1), (512, 4), (2048, 16))):
        ok = (k <= i) & ((i - k) % dil == 0) & ((i - k) // dil <= window_ // dil)
        m = np.where(ok, f(0), f(NEG))
        ca[:, 128 * g:128 * g + 128] = m[0:128, 0:128]
        ca[:, 384 + 256 * g:384 + 256 * g + 256] = m[128:256]
    put("causal", ca)
    u, v = np.arange(128)[:, None], np.arange(128)[None]
    put("upto", (u <= v).astype(f))
    put("after", (u > v).astype(f))
    put("ones", np.ones((128, 128), f))
    put("never", np.where(v > u, f(NEG), f(0)).astype(f))
    sel = np.zeros((2, 2, 128), f)
    sel[0, 0], sel[1, 1] = 1, 1
    put("sel", sel)
    put("freq", np.tile(f(500000.0) ** (-np.arange(16, dtype=f) * f(2.0) / f(32)), (128, 1)))
    return c


def lay_out(inputs):
    x = {k: np.ascontiguousarray(np.asarray(v)) for k, v in inputs.items()}

    def cols(v):
        return v.reshape(-1, 128).T

    parts = [x["c"], x["c_ctx"], x["norm_g"], x["b_mod"], x["pool_scale"], x["attn_norm_2"], x["mlstm_norm_2"],
             x["ffn_norm_2"], x["mlstm_head_gain_2"], x["mlstm_conv_b_2"], x["mlstm_conv_w_2"]]
    arrays = {n: x[n] for n in BIG}
    arrays["vec"] = np.ascontiguousarray(np.concatenate([cols(p) for p in parts], axis=1))
    arrays["cst"] = tables()
    return arrays


BIG = ["x", "ctx", "w_mod", "b_mod", "norm_g", "w_ffn_gate_up", "w_ffn_down", "w_in", "w_out", "na_rpb", "w_pool",
       "positions_2", "attn_w_in_2", "attn_w_out_2", "mlstm_w_in_2", "mlstm_ig_bias_2", "mlstm_fg_bias_2",
       "mlstm_w_out_2", "ffn_w_in_2", "ffn_w_out_2", "final_norm_2"]


def kernel(**inputs):
    import concourse.bacc as bacc
    from concourse.bass_utils import run_bass_kernel_spmd

    nc = bacc.Bacc("TRN2", target_bir_lowering=False, num_devices=1)
    arrays = lay_out(inputs)
    args = {n: nc.dram_tensor(f"in_{n}", v.shape, mybir.dt.from_np(v.dtype), kind="ExternalInput").ap()
            for n, v in arrays.items()}
    out = nc.dram_tensor("out_0", (1, 256, D), F32, kind="ExternalOutput").ap()
    build(nc, args, out)
    r = run_bass_kernel_spmd(nc, [{f"in_{n}": v for n, v in arrays.items()}], core_ids=[0])
    return r.results[0]["out_0"]
```

```python
from contextlib import ExitStack

import numpy as np
import concourse.bass as bass
from concourse import mybir

F32 = mybir.dt.float32
F32R = mybir.dt.float32r
I32 = mybir.dt.int32
ALU = mybir.AluOpType
ACT = mybir.ActivationFunctionType
AX = mybir.AxisListType.X

D = 1024
DFF = 2816
NF = DFF // 128
EPS = 1e-6
NEG = -1e30
RAW = 2
FIRST = 7
CUT = 3
UN = 2048
NP = 8

VEC = {}
_at = 0
for _name, _n in [("c", 8), ("c_ctx", 8), ("norm_g", 96), ("b_mod", 144), ("pool_scale", 8), ("attn_norm", 8),
                  ("mlstm_norm", 8), ("ffn_norm", 16), ("head_gain", 8), ("conv_b", 8), ("conv_w", 32)]:
    VEC[_name] = _at
    _at += _n
NVEC = _at

CST = {}
_at = 0
for _name, _n in [("ident", 128), ("rope", 256), ("colmask", 64), ("pool_x", 512),
                  ("upto", 128), ("after", 128), ("ones", 128), ("never", 128), ("sel", 256), ("pick", 4),
                  ("freq", 16), ("pool_c", 2048), ("causal", 1152)]:
    CST[_name] = (_at, _n)
    _at += _n
NCST = _at


class Line:

    def __init__(self, sem):
        self.sem, self.n, self.items, self.seen = sem, 0, [], {}

    def wait(self, *marks):
        for m in marks:
            if m is None:
                continue
            if isinstance(m, list):
                self.wait(*m)
                continue
            sem, value = m
            if self.seen.get(sem.name, 0) < value:
                self.seen[sem.name] = value
                self.items.append(lambda e, s=sem, v=value: e.wait_ge(s, v))

    def do(self, fn, *waits, mark=True):
        self.wait(*waits)
        if not mark:
            self.items.append(fn)
            return None
        self.n += 1
        self.items.append(lambda e: fn(e).then_inc(self.sem, 1))
        return (self.sem, self.n)

    def emit(self, eng):
        for f in self.items:
            f(eng)


class Banks:

    def __init__(self):
        self.marks, self.queue = {b: None for b in range(NP)}, list(range(NP))

    def take(self):
        return self.queue.pop(0)

    def __setitem__(self, b, mark):
        self.marks[b] = mark
        if b in self.queue:
            self.queue.remove(b)
        self.queue.append(b)


def build(nc, a, out):
    with ExitStack() as ctx:
        def sb(name, shape, dt=F32):
            return ctx.enter_context(nc.sbuf_tensor(name, shape, dt))

        def sem(name):
            return ctx.enter_context(nc.semaphore(name))

        raw = [sb(f"raw{i}", [128, UN]) for i in range(RAW)]
        whi = [sb(f"whi{i}", [128, UN], F32R) for i in range(CUT)]
        wlo = [sb(f"wlo{i}", [128, UN], F32R) for i in range(CUT)]
        Hhi = sb("Hhi", [128, 8, 512], F32R)
        Hlo = sb("Hlo", [128, 8, 512], F32R)
        X = sb("X", [128, 2, D])
        vec = sb("vec", [128, NVEC])
        cst = sb("cst", [128, CST["pool_c"][0]])
        sc32 = sb("sc32", [128, 8, 2])
        SM = 440
        dg = sb("dg", [128, 4, 128])
        small = sb("small", [128, SM])
        mods = sb("mods", [128, 12, 8, 2])
        mtmp = sb("mtmp", [128, 8, 2])
        posi = sb("posi", [128, 2], I32)
        AR = 22016
        hs = sb("hs", [128, 2, 512], F32R)
        arena = sb("arena", [128, AR])
        ps = [ctx.enter_context(nc.psum_tensor(f"ps{i}", [128, 512], F32)) for i in range(NP)]

        PE, DV, AC, PO, SP = [Line(sem(n)) for n in ("s_pe", "s_dve", "s_act", "s_pool", "s_sp")]
        s_first = [sem(f"s_first{i}") for i in range(FIRST)]
        s_raw = [sem(f"s_raw{i}") for i in range(RAW)]
        dsems = {}

        def load(key, dst, src, *waits, line=None):
            if key not in dsems:
                dsems[key] = [sem(f"s_{key}"), 0]
            line = line or SP
            s = dsems[key][0]
            if dsems[key][1]:
                line.wait((s, dsems[key][1]))
            dsems[key][1] += 16
            line.do(lambda e: e.dma_start(dst, src).then_inc(s, 16), *waits, mark=False)
            return (s, dsems[key][1])

        def at(off, *dims):
            n = int(np.prod(dims))
            assert off + n <= AR, (off, n)
            v = arena[:, off:off + n]
            if len(dims) == 2:
                v = v.rearrange("p (a b) -> p a b", a=dims[0])
            elif len(dims) == 3:
                v = v.rearrange("p (a b c) -> p a b c", a=dims[0], b=dims[1])
            return v

        def cs(name):
            o, n = CST[name]
            return cst[:, o:o + n]

        cols = [0]

        def col(n=1):
            if cols[0] + n > SM:
                cols[0] = 0
            cols[0] += n
            return small[:, cols[0] - n:cols[0]]

        C = at(0, 2, D)
        G = [at(2048, D), at(3072, D)]
        XN = [at(4096, D), at(5120, D)]
        HS = [hs[:, i, :] for i in range(2)]
        U0 = 6144

        def ident(n=128):
            return cst[0:n, 0:n]

        pfree = Banks()

        def bank():
            b = pfree.take()
            PE.wait(pfree.marks[b])
            return b

        def kview(w, c0, c1):
            return w[:, c0:c1].rearrange("(k p) n -> p k n", p=128)

        def units_of(step):
            kind = step[0]
            if kind == "mod":
                w = kview(a["w_mod"][step[1]], step[2] * D, step[2] * D + D)
                return [(w[:, 4 * k:4 * k + 4, 512 * h:512 * h + 512], 4, 512) for h in range(2) for k in range(2)]
            if kind == "gu":
                w = step[1]
                return [(kview(w, g * DFF + 256 * j, g * DFF + 256 * j + 256), 8, 256)
                        for j in range(NF // 2) for g in range(2)]
            if kind == "out":
                w = kview(step[1], 0, D)
                return [(w[:, 2 * j:2 * j + 2, :], 2, D) for j in range(step[2] // 2)]
            if kind == "cols":
                w = kview(step[1], step[2], step[2] + 512)
                return [(w[:, 4 * k:4 * k + 4, :], 4, 512) for k in range(2)]
            if kind == "rows":
                return [(kview(step[1], step[2], step[2] + 256), 8, 256)]
            if kind == "gates":
                return [(kview(step[1], 3072, 3088), 8, 16)]
            raise ValueError(kind)

        gu1 = a["w_ffn_gate_up"]
        dn1 = a["w_ffn_down"]
        SIDE = {(0, 0): [(0, 2), (0, 3), (0, 4), (0, 6)], (0, 1): [(1, 0), (1, 1), (1, 2, 1)],
                (1, 0): [(1, 3), (1, 4), (1, 6), (1, 5, 1)]}

        def side_units(key):
            return [(x[0], x[1], h, u) for x in SIDE.get(key, []) for h in (range(2) if len(x) == 2 else x[2:])
                    for u in range(2)]

        def side_of(key):
            q = side_units(key)
            res = []
            for j in range(NF // 2):
                n = -(-len(q) // max(1, NF // 2 - 2 - j)) if j else 1
                res.append(q[:n])
                q = q[n:]
            assert not q and not res[-1] and not res[-2], [len(r) for r in res]
            return res

        def side_src(l, v, h, u):
            w = kview(a["w_mod"][l], v * D, v * D + D)
            return (w[:, 4 * u:4 * u + 4, 512 * h:512 * h + 512], 4, 512)

        stream = []

        def push(step, kind, n=None):
            for u in units_of(step)[:n]:
                stream.append(u + (kind, None))

        def push_gu(w, key=None):
            us = units_of(("gu", w))
            side = side_of(key)
            for j in range(NF // 2):
                for i, u in enumerate(us[2 * j:2 * j + 2]):
                    stream.append(u + ("cut", None))
                    cut_at = 1 if j else 0
                    for what in side[j][cut_at:] if i else side[j][:cut_at]:
                        stream.append(side_src(*what) + ("side", what))

        for h in range(2):
            for u in range(2):
                stream.append(side_src(0, 0, h, u) + ("side", (0, 0, h, u)))
                stream.append(side_src(0, 1, h, u) + ("plain", None))
        for l in range(2):
            push_gu(gu1[l, 0], (l, 0))
            us = units_of(("out", dn1[l, 0], NF))
            for j, u in enumerate(us):
                stream.append(u + ("cut", None))
                if j in (1, 3, 5, 7):
                    what = (l, 7, (j - 1) // 4, (j - 1) // 2 % 2)
                    stream.append(side_src(*what) + ("side", what))
            push(("mod", l, 5), "plain", 2 if l else None)
            for g in range(4):
                push(("cols", a["w_in"][l], 512 * g), "cut")
            push(("out", a["w_out"][l], 8), "cut")
            push(("mod", l, 8), "plain")
            push_gu(gu1[l, 1], (l, 1))
            push(("out", dn1[l, 1], NF), "cut")
            if l == 0:
                push(("mod", 1, 2), "plain", 2)
        for h in range(2):
            for g in range(3):
                for t in range(3):
                    push(("cols", a["attn_w_in_2"][0], (3 * g + t) * 1024 + 512 * h), "cut")
        push(("out", a["attn_w_out_2"][0], 8), "cut")
        push_gu(a["ffn_w_in_2"][0])
        push(("out", a["ffn_w_out_2"][0], NF), "cut")
        mw = a["mlstm_w_in_2"][0]
        push(("gates", mw), "cut")
        for j in range(4):
            push(("rows", mw, 256 * j), "cut")
        for j in range(4):
            push(("cols", mw, 1024 + 512 * j), "cut")
        push(("out", a["mlstm_w_out_2"][0], 8), "cut")
        push_gu(a["ffn_w_in_2"][1])
        push(("out", a["ffn_w_out_2"][1], NF), "cut")
        order = [n for n in range(len(stream)) if stream[n][3] != "side"]
        place = list(range(len(stream)))
        for n in range(8, len(stream) - 6):
            for c in (2, 4):
                if [x[3] for x in stream[n - 1:n + c + 2]] == ["cut"] + ["plain"] * c + ["cut"] * 2:
                    place[n:n + c + 2] = [n + c, n + c + 1] + list(range(n, n + c))
        units = [stream[n] for n in place]
        where = {n: i for i, n in enumerate(place)}
        order = [where[n] for n in order]
        first = [at(U0 + UN * i, UN) for i in range(5)] + [at(4096, UN), at(2048, UN)]
        hold, until = [False], [8]
        nth, free, landed, cut_done, done_at = {}, {}, {}, {}, {}
        for n, u in enumerate(units):
            if u[3] == "cut":
                nth[n] = len(nth)
        cut_units = sorted(nth)
        used, fetched, seen = [0], [0], [0]

        def slot(n):
            return first[n] if n < FIRST else raw[(n - FIRST) % RAW]

        def room(n):
            return n < FIRST + RAW or n - RAW in free

        def fetch_one(n):
            src, k, m = units[n][0:3]
            dst = slot(n)[:, 0:k * m].rearrange("p (k m) -> p k m", k=k)
            if n < FIRST:
                s, v, before = s_first[n], 16, None
            else:
                s, v = s_raw[(n - FIRST) % RAW], 16 * ((n - FIRST) // RAW + 1)
                before = free[n - RAW] if n >= FIRST + RAW else None
            SP.do(lambda e: e.dma_start(dst, src).then_inc(s, 16), before, mark=False)
            landed[n] = (s, v)

        def advance():
            while True:
                n = fetched[0]
                if n < len(units) and room(n):
                    fetch_one(n)
                    fetched[0] += 1
                    continue
                n = seen[0]
                if n >= fetched[0]:
                    return
                _, k, m, kind, what = units[n]
                if kind != "plain" and (hold[0] or n >= until[0]):
                    return
                if kind == "side":
                    if not side_room(*what):
                        return
                    free[n] = side_sum(slot(n)[:, :].rearrange("p (k m) -> p k m", k=4), landed[n], *what)
                if kind == "cut":
                    c = nth[n]
                    if c >= CUT and cut_units[c - CUT] not in done_at:
                        return
                    r, h, o = slot(n)[:, 0:k * m], whi[c % CUT][:, 0:k * m], wlo[c % CUT][:, 0:k * m]
                    before = done_at.get(cut_units[c - CUT]) if c >= CUT else None
                    cut_done[n] = free[n] = two_parts(h, o, r, landed[n], before)
                seen[0] += 1

        def unit(k, m):
            n = order[used[0]]
            assert units[n][1:3] == (k, m), (n, units[n][1:3], k, m)
            v = lambda t: t[:, 0:k * m].rearrange("p (k m) -> p k m", k=k)
            if units[n][3] == "plain":
                PE.wait(landed[n])
                return v(slot(n))
            PE.wait(cut_done[n])
            return v(whi[nth[n] % CUT]), v(wlo[nth[n] % CUT])

        def unit_done(mark):
            n = order[used[0]]
            done_at[n] = mark
            if units[n][3] == "plain":
                free[n] = mark
            used[0] += 1
            advance()

        def mm3(o, A, B, start, stop, mark=False):
            PE.do(lambda e: e.matmul(o, A[0], B[1], start=start, stop=False), mark=False)
            PE.do(lambda e: e.matmul(o, A[1], B[0], start=False, stop=False), mark=False)
            return PE.do(lambda e: e.matmul(o, A[0], B[0], start=False, stop=stop), mark=mark)

        def mm(o, A, B, start=True, stop=True, mark=True, *waits):
            return PE.do(lambda e: e.matmul(o, A, B, start=start, stop=stop), *waits, mark=mark)

        def tr(o, i, mark=True, *waits):
            n = i.shape[0]
            return PE.do(lambda e: e.transpose(o, i, ident(n)), *waits, mark=mark)

        def tt(line, o, x, y, op, *waits):
            return line.do(lambda e: e.tensor_tensor(o, x, y, op), *waits)

        def ts(line, o, x, s1, op0, s2, op1, *waits):
            if op1 is None:
                return line.do(lambda e: e.tensor_scalar(o, x, s1, None, op0), *waits)
            return line.do(lambda e: e.tensor_scalar(o, x, s1, s2, op0, op1), *waits)

        def stt(o, x, s, y, op0, op1, *waits, acc=None):
            return DV.do(lambda e: e.scalar_tensor_tensor(out=o, in0=x, scalar=s, in1=y, op0=op0, op1=op1,
                                                          **({"accum_out": acc} if acc is not None else {})), *waits)

        def red(o, x, op, *waits):
            return DV.do(lambda e: e.tensor_reduce(o, x, AX, op), *waits)

        def recip(o, x, *waits):
            return DV.do(lambda e: e.reciprocal(o, x), *waits)

        def act(o, x, f, *waits, **kw):
            return AC.do(lambda e: e.activation(o, x, f, **kw), *waits)

        def copy(line, o, x, *waits):
            if line is AC:
                return act(o, x, ACT.Copy, *waits)
            return line.do(lambda e: e.tensor_copy(o, x), *waits)

        def two_parts(hi, lo, x, *waits):
            am = act(hi, x, ACT.Copy, *waits)
            return DV.do(lambda e: e.tensor_tensor(lo, x, hi.bitcast(F32), ALU.subtract), am)

        m_vec = load("vec", vec[:, :], a["vec"])
        for n in range(4):
            fetch_one(n)
            fetched[0] += 1
        m_cst = load("cst", cst[:, :], a["cst"][:, 0:CST["pool_c"][0]])
        m_x = load("x", X[:, :, :], a["x"].rearrange("o (t p) d -> p (o t) d", p=128))
        for n in range(4, FIRST + RAW):
            fetch_one(n)
            fetched[0] += 1
        m_c = load("c", C, a["ctx"].rearrange("o (t p) d -> p (o t) d", p=128))
        m_pos = [load(f"pos{t}", posi[:, t:t + 1], a["positions_2"][:, 128 * t:128 * t + 128].rearrange("o p -> p o"),
                      line=PO)
                 for t in range(2)]
        rpbs = nc.dram_tensor("rpbs", (64, 7440), F32).ap()
        m_rpb = load("rpb", rpbs, bass.AP(a["na_rpb"].tensor, 0, [[0, 64], [1, 7440]]),
                     m_c, landed[FIRST + RAW - 1], line=PO)
        v2 = vec[:, 0:16].rearrange("p (s k) -> p k s", s=2)
        m = act(sc32[:, :, :], v2, ACT.Silu, m_vec)
        m_sc = m

        MROW = U0 + 11264
        mrow = at(MROW, D)
        bg = at(MROW + 1024, 2, 512)
        mrow_free, bg_free, bb_free = [None], [None], [None]
        g_free = [None, None]
        g_ready = [None, None]
        mods_ready = {}

        acc = [[at(MROW + 2048 + 512 * i, 512) for i in range(2)], [at(MROW + 3584 + 512 * i, 512) for i in range(2)]]
        acc_ready, acc_free, acc_turn = {}, [None, None], [0]
        acc_of = {}

        def side_room(l, v, h, u):
            return u == 1 or acc_turn[0] < 2 or acc_free[acc_turn[0] % 2] is not False

        side_summed = []

        def side_sum(w, m_w, l, v, h, u):
            if u == 0:
                q = acc_turn[0] % 2
                acc_of[l, v, h] = q
                acc_turn[0] += 1
                DV.wait(acc_free[q], bb_free[0], m_sc)
                acc_free[q] = False
            q = acc_of[l, v, h]
            m = [None, None]
            if u == 1:
                m = acc_ready[l, v, h, 0]
            for k in range(4):
                for s in range(2):
                    o, c_ = acc[q][s], sc32[:, 4 * u + k, s:s + 1]
                    if u == 0 and k == 0:
                        m[s] = ts(DV, o, w[:, k, :], c_, ALU.mult, None, None, m_w)
                    else:
                        m[s] = stt(o, w[:, k, :], c_, o, ALU.mult, ALU.add, m[s], m_w)
            acc_ready[l, v, h, u] = list(m)
            if u == 1:
                side_summed.append(((l, v, h), used[0]))
            return m[1]

        def side_rows(l, v, h):
            q = acc_of[l, v, h]
            b = bank()
            for s in range(2):
                m = mm(ps[b][0:2, :], cs("pick")[:, 2 * s:2 * s + 2], acc[q][s], s == 0, s == 1, s == 1,
                       acc_ready[l, v, h, 1], m_cst)
            acc_free[q] = m
            advance()
            return b, m

        def plain_rows(halves=2):
            res = []
            for h in range(halves):
                b = bank()
                for u in range(2):
                    w = unit(4, 512)
                    for k in range(4):
                        kt = 4 * u + k
                        m = mm(ps[b][0:2, :], sc32[:, kt, :], w[:, k, :], kt == 0, kt == 7, k == 3)
                    unit_done(m)
                res.append((b, m))
            return res

        def plain_units(rows, halves):
            for h in range(halves):
                b = bank()
                for u in range(2):
                    w = unit(4, 512)
                    for k in range(4):
                        kt = 4 * u + k
                        m = mm(ps[b][0:2, :], sc32[:, kt, :], w[:, k, :], kt == 0, kt == 7, k == 3)
                    unit_done(m)
                    if u == 1:
                        rows.append((b, m))
                    yield

        def gate_loads(l, v, gain, h):
            return [load("bg", bg[0:2, 0, :],
                         bass.AP(a["b_mod"].tensor, l * 9216 + v * D + 512 * h, [[0, 2], [1, 512]]),
                         bg_free[0], bb_free[0], line=PO),
                    load("bh", bg[0:2, 1, :],
                         bass.AP(a["norm_g"].tensor, (l * 6 + gain) * D + 512 * h, [[0, 2], [1, 512]]),
                         bg_free[0], bb_free[0], line=PO)]

        GATE = {2: (1, True), 5: (3, False), 8: (5, True)}

        def gate_rows(rows, l, v, h0=0):
            gain, half_gate = GATE[v]
            ms = []
            for h, (b, m) in enumerate(rows, h0):
                m_l = gate_loads(l, v, gain, h)
                r = mrow[0:2, 512 * h:512 * h + 512]
                m1 = tt(DV, r, ps[b][0:2, :], bg[0:2, 0, :], ALU.add, m, m_l[0], mrow_free[0], bb_free[0])
                pfree[b] = m1
                m2 = stt(r, r, 0.5 if half_gate else 1.0, bg[0:2, 1, :], ALU.mult, ALU.mult, m1, m_l[1])
                bg_free[0] = m2
                ms.append(m2)
            return ms

        grow = nc.dram_tensor("grow", (2, D), F32).ap()
        grow_free = [None]

        def gate_spread(ms):
            m = load("grow", grow, mrow[0:2, :], ms, grow_free[0], line=PO)
            mrow_free[0] = m
            for s in range(2):
                g_ready[s] = load(f"g{s}", G[s], bass.AP(grow.tensor, s * D, [[0, 128], [1, D]]), m, g_free[s], line=PO)
            grow_free[0] = [g_ready[0], g_ready[1]]

        def vector_row(l, v, h, b, m):
            m1 = copy(DV, mrow[0:2, 512 * h:512 * h + 512], ps[b][0:2, :], m, mrow_free[0], bb_free[0])
            pfree[b] = m1
            return m1

        def vector_turn(l, v, gain, ms):
            b = bank()
            for k in range(8):
                m = tr(ps[b][:, 2 * k:2 * k + 2], mrow[0:2, 128 * k:128 * k + 128], k == 7, ms)
            mrow_free[0] = m
            i = 6 * l + v // 3 * 2 + v % 3
            o = mods[:, i, :, :]
            b0 = VEC["b_mod"] + 72 * l + 8 * v
            bT = vec[:, b0:b0 + 8].unsqueeze(2).to_broadcast([128, 8, 2])
            pv = ps[b][:, 0:16].rearrange("p (k s) -> p k s", s=2)
            if v % 3 == 0:
                m = tt(DV, o, pv, bT, ALU.add, m)
                pfree[b] = m
            else:
                g0 = VEC["norm_g"] + 48 * l + 8 * gain
                gT = vec[:, g0:g0 + 8].unsqueeze(2).to_broadcast([128, 8, 2])
                m = tt(DV, mtmp[:, :, :], pv, bT, ALU.add, m)
                pfree[b] = m
                m = stt(o, mtmp[:, :, :], 1.0, gT, ALU.add, ALU.mult, m)
            mods_ready[i] = m

        PRE_GAIN = {1: 0, 4: 2, 7: 4}
        side_rest = []

        def side_tick():
            side_finish(2)
            if side_summed and used[0] - side_summed[0][1] >= 2:
                side_finish()
                side_step(side_summed.pop(0)[0])

        side_ms = {}

        def side_step(todo):
            l, v, h = todo
            b, m = side_rows(l, v, h)
            if v in GATE:
                side_ms.setdefault((l, v), []).extend(gate_rows([(b, m)], l, v, h))
            else:
                side_ms.setdefault((l, v), []).append(vector_row(l, v, h, b, m))
            if h == 1:
                side_rest.append((l, v, used[0]))

        def side_finish(wait=0):
            while side_rest and used[0] - side_rest[0][2] >= wait:
                l, v, _ = side_rest.pop(0)
                if (l, v) == (0, 2):
                    gate_spread(side_ms[l, v])
                elif v not in GATE:
                    vector_turn(l, v, PRE_GAIN.get(v), side_ms[l, v])

        h_free = [None]

        def rstd(ss, n, scale, *waits):
            v, q, r = col(n), col(n), col(n)
            m = ts(DV, v, ss, scale, ALU.mult, EPS, ALU.add, *waits)
            m = act(q, v, ACT.Sqrt, m)
            m = recip(r, q, m)
            return r, m

        xn_free = [None, None]
        hs_free = [None, None]
        hs_at = [0]

        evac_at, tq_at = [0], [0]
        TQ = [XN[i][:, 512 * j:512 * j + 512] for j in range(2) for i in range(2)]
        tq_free = [None] * 4

        turned_ = []

        def turn_parts(todo):
            hi, lo, h32, m, q = todo
            m = two_parts(hi, lo, h32, m, h_free[0])
            tq_free[q] = m
            return m

        def turn_end():
            while turned_:
                m = turn_parts(turned_.pop(0))
            for i in range(2):
                xn_free[i] = [tq_free[i], tq_free[i + 2]]
            tq_free[:] = [None] * 4
            return m

        def turn(i, src, m_src, pos, gain, shift, m_ab, q_dg=None):
            m_t = None
            for hb in range(2):
                b = bank()
                for k in range(4):
                    o, x_ = ps[b][:, 128 * k:128 * k + 128], src[:, 512 * hb + 128 * k:512 * hb + 128 * k + 128]
                    if q_dg is None:
                        m_t = tr(o, x_, k == 3, m_src)
                    else:
                        m_t = mm(o, x_, dg[:, q_dg, :], True, True, k == 3, m_src)
                q = tq_at[0] % 4
                tq_at[0] += 1
                h32 = TQ[q].rearrange("p (k t) -> p k t", k=4)
                q_free = tq_free[q] or xn_free[q % 2]
                pv = ps[b][:, :].rearrange("p (k t) -> p k t", k=4)
                k0 = 4 * hb
                evac_at[0] += 1
                for k in range(4):
                    g_ = gain[:, k0 + k:k0 + k + 1]
                    s_ = shift[:, k0 + k:k0 + k + 1] if shift is not None else None
                    if evac_at[0] % 2:
                        m = ts(DV, h32[:, k, :], pv[:, k, :], g_, ALU.mult, s_, None if s_ is None else ALU.add,
                               m_t, m_ab, q_free)
                    else:
                        kw = {"scale": g_} if s_ is None else {"scale": g_, "bias": s_}
                        m = act(h32[:, k, :], pv[:, k, :], ACT.Identity, m_t, m_ab, q_free, **kw)
                pfree[b] = m
                hi, lo = Hhi[:, k0:k0 + 4, pos:pos + 128], Hlo[:, k0:k0 + 4, pos:pos + 128]
                turned_.append((hi, lo, h32, m, q))
                while len(turned_) > 1:
                    turn_parts(turned_.pop(0))
            return m_t

        FILL = {(4, 2): [1, 0, 0, 0, 1], (4, 4): [1, 1, 1, 0, 1], (2, 4): [2, 1, 1]}

        def pre(tiles, diag, ab, gate=None):
            rows = []
            fill, filled = [0] * 5, iter(())
            if gate:
                fill, filled = FILL[len(tiles), 2 * gate[2]], plain_units(rows, gate[2])
            for i, (x, m) in enumerate(tiles):
                for _ in range(fill[i]):
                    next(filled)
                gain, shift, m_ab = ab(i)
                _, _, q, md = diag[i]
                dg_free[q] = turn(i, x, [md, m] if not isinstance(m, list) else [md] + m, 128 * i, gain, shift,
                                       m_ab, q)
            m_h = turn_end()
            for _ in filled:
                pass
            hold[0], until[0] = False, len(units)
            advance()
            if gate:
                l, v, _ = gate
                gate_spread(gate_rows(rows, l, v) + side_ms.get((l, v), []))
            return m_h

        class Parts:

            def __init__(self, T, A, marks, before):
                self.T, self.A, self.marks, self.before = T, A, marks, before
                self.made, self.slot_free = {}, {}

            def part(self, k):
                if k < NF:
                    s, o = k % 8, 256 if self.T == 256 else 0
                    hi, lo = Hhi[:, s, o:o + self.T], Hlo[:, s, o:o + self.T]
                    before = [self.before, self.slot_free.get(s)]
                    if k == 0 and self.T == 512:
                        hi, lo, before = HS[0], HS[1], list(hs_free)
                    self.made[k] = (hi, lo, two_parts(hi, lo, self.A[:, k, :], self.marks[k], before))

            def start(self, k0, k1):
                for k in range(k0, k1):
                    self.part(k)

            def used(self, k, mark):
                self.slot_free[k % 8] = mark
                if k == 0 and self.T == 512:
                    hs_free[0] = hs_free[1] = mark
                self.part(k + 4)

        def gate_up(T, m_h, act_at):
            A = at(act_at, NF, T)
            PE.wait(m_h)
            marks = {}
            parts = Parts(T, A, marks, h_free[0])
            for j in range(NF // 2):
                if j == NF // 2 - 1:
                    parts.start(0, 4 if T == 256 else 1)
                bs = [bank() for _ in range(4)]
                done = []
                for g in range(2):
                    hi, lo = unit(8, 256)
                    for s in range(2):
                        for k in range(8):
                            m = mm3(ps[bs[2 * g + s]][:, 0:T],
                                    (hi[:, k, 128 * s:128 * s + 128], lo[:, k, 128 * s:128 * s + 128]),
                                    (Hhi[:, k, 0:T], Hlo[:, k, 0:T]), k == 0, k == 7, mark=(k == 7))
                        done.append(m)
                    if g == 0:
                        unit_done(m)
                        side_tick()
                for s in range(2):
                    q = XN[s][:, 0:T]
                    m1 = act(q, ps[bs[s]][:, 0:T], ACT.Silu, done[s], xn_free[s])
                    pfree[bs[s]] = m1
                    m2 = tt(DV, A[:, 2 * j + s, :], q, ps[bs[2 + s]][:, 0:T], ALU.mult, m1, done[2 + s])
                    xn_free[s] = m2
                    pfree[bs[2 + s]] = m2
                    marks[2 * j + s] = m2
                unit_done(m)
                side_tick()
            assert not side_summed and not side_rest
            h_free[0] = m
            if T != 256:
                parts.before = m
                parts.start(1, 4)
            return parts

        def out_product(nk, nt, left):
            bs = {(t, h): bank() for t in range(nt) for h in range(2)}
            my = {}
            for j in range(nk // 2):
                hi, lo = unit(2, D)
                last = j == nk // 2 - 1
                ks = [2 * j, 2 * j + 1]
                order = [(k, [t]) for t in range(nt) for k in ks] if last else [(k, range(nt)) for k in ks]
                parts = {k: left(k) for k in ks}
                for k, tiles_ in order:
                    Lh, Ll, m_l, after = parts[k]
                    PE.wait(m_l)
                    for t in tiles_:
                        for h in range(2):
                            m = mm3(ps[bs[t, h]][:, :],
                                    (Lh[:, 128 * t:128 * t + 128], Ll[:, 128 * t:128 * t + 128]),
                                    (hi[:, k % 2, 512 * h:512 * h + 512], lo[:, k % 2, 512 * h:512 * h + 512]),
                                    k == 0, k == nk - 1, mark=(h == 1 and (last or t == nt - 1)))
                        if k == nk - 1:
                            my[t] = m
                    if not last:
                        after(m)
                hold[0] = last
                unit_done(m)
            return bs, my, m

        def down(T, parts):
            def left(k):
                def after(mark):
                    parts.used(k, mark)
                return parts.made[k] + (after,)
            bs, my, m = out_product(NF, T // 128, left)
            h_free[0] = m
            return bs, my

        def from_H(nk, nt, m_h, off=0):
            PE.wait(m_h)
            bs, my, m = out_product(nk, nt, lambda k: (Hhi[:, k, off:512], Hlo[:, k, off:512], None,
                                                       lambda mark: None))
            h_free[0] = m
            return bs, my

        def skew(chains):
            for n in range(len(chains) + max(len(c) for c in chains) - 1):
                for t, c in enumerate(chains):
                    if 0 <= n - t < len(c):
                        c[n - t]()

        dg_at = [0]
        dg_free = [None] * 4

        def square(x, acc, *waits):
            hs_at[0] += 1
            q = hs_at[0] % 2
            hs_free[q] = act(HS[q], x, ACT.Square, *waits, hs_free[q], accum_out=acc)
            return hs_free[q]

        def rms_stages(x, marks, done):
            st = {}
            ss, s1 = col(2), col()

            def squares():
                for h in range(2):
                    m = square(x[:, 512 * h:512 * h + 512], ss[:, h:h + 1], marks()[h])
                st["m"] = tt(DV, s1, ss[:, 0:1], ss[:, 1:2], ALU.add, m)

            def root():
                r, m = rstd(s1, 1, 1.0 / D, st["m"])
                q = dg_at[0] % 4
                dg_at[0] += 1
                md = ts(DV, dg[:, q, :], ident(), r, ALU.mult, None, None, m, dg_free[q])
                done((r, m, q, md))
            return [squares, root]

        def post(bs, my, tiles, gs):
            res, diag = [None] * len(tiles), [None] * len(tiles)

            def chain(t):
                x, m_x = tiles[t]
                st = {}
                ss, s1 = col(2), col()
                b0, b1 = bs[t, 0], bs[t, 1]

                def y_squares():
                    m0 = square(ps[b0][:, :], ss[:, 0:1], my[t])
                    m1 = square(ps[b1][:, :], ss[:, 1:2], my[t])
                    st["m"] = tt(DV, s1, ss[:, 0:1], ss[:, 1:2], ALU.add, m0, m1)

                def y_root():
                    st["r"], st["m"] = rstd(s1, 1, 1.0 / D, st["m"])

                def update():
                    s = gs[t]
                    out_ = []
                    for h, b in enumerate((b0, b1)):
                        q = XN[h][:, 512 * (t % 2):512 * (t % 2) + 512]
                        xs = x[:, 512 * h:512 * h + 512]
                        m = stt(q, ps[b][:, :], st["r"], G[s][:, 512 * h:512 * h + 512], ALU.mult, ALU.mult,
                                st["m"], g_ready[s], xn_free[h])
                        pfree[b] = m
                        g_free[s] = m
                        m = tt(PO if h == 0 else DV, xs, xs, q, ALU.add, m, m_x)
                        xn_free[h] = m
                        out_.append(m)
                    st["x"] = out_
                    res[t] = (x, out_)

                def plain_update():
                    out_ = []
                    for h, b in enumerate((b0, b1)):
                        xs = x[:, 512 * h:512 * h + 512]
                        m = tt(DV, xs, xs, ps[b][:, :], ALU.add, my[t], m_x)
                        pfree[b] = m
                        out_.append(m)
                    st["x"] = out_
                    res[t] = (x, out_)

                def done(d):
                    diag[t] = d
                return ([y_squares, y_root, update] if gs else [plain_update]) + \
                    rms_stages(x, lambda: st["x"], done)

            skew([chain(t) for t in range(len(tiles))])
            return res, diag

        def first_stats(tiles):
            diag = [None] * len(tiles)

            def one(t):
                def done(d):
                    diag[t] = d
                return rms_stages(tiles[t][0], lambda: [tiles[t][1]] * 2, done)
            skew([one(t) for t in range(len(tiles))])
            return diag

        later = []

        def flush():
            todo = list(later)
            later.clear()
            for f in todo:
                f()

        def project(tts, evac, m_h=None):
            if m_h is not None:
                PE.wait(m_h)
            bs = {t: bank() for t in tts}
            last = {}
            for u in range(2):
                hi, lo = unit(4, 512)
                for t in tts:
                    for k in range(4):
                        kt = 4 * u + k
                        m = mm3(ps[bs[t]][:, :], (Hhi[:, kt, 128 * t:128 * t + 128], Hlo[:, kt, 128 * t:128 * t + 128]),
                                (hi[:, k, :], lo[:, k, :]), kt == 0, kt == 7, mark=(k == 3))
                    last[t] = m
                unit_done(m)
                if u == 0:
                    flush()
            for t in tts:
                evac(t, bs[t], last[t])
            return m

        QT = at(U0, 4, 512)
        KT = at(U0 + 2048, 4, 512)
        V = at(U0 + 4096, 4, 512)
        UU = at(U0 + 6144, 4, 512)
        S = [at(U0 + 8192, 512), at(U0 + 8704, 512)]
        PT_AT = U0 + 9216
        PT = [at(PT_AT, 4, 256), at(PT_AT + 1024, 4, 256)]
        BB = at(PT_AT + 2048, 8, 6, 64)
        ACT_AT = U0
        rope = cs("rope").rearrange("p (t c d) -> p t c d", t=2, c=2)

        rope2 = sb("rope2", [128, 2, 2, 32])

        def rope_tables():
            angs = at(MROW + 3072, 192).rearrange("p (a t c) -> p a t c", a=6, t=2)
            posf, ANG, TT, KK, RR = small[:, SM - 2:SM], angs[:, 0], angs[:, 1], angs[:, 2], angs[:, 3]
            m = copy(DV, posf, posi[:, :], m_pos)
            for t in range(2):
                m1 = ts(DV, ANG[:, t, :], cs("freq"), posf[:, t:t + 1], ALU.mult, None, None, m, m_cst)
            m_ang = m1
            C1 = 6.28125
            C2 = round((2 * np.pi - C1) * 2.0 ** 18) / 2.0 ** 18
            C3 = float(np.float32(2 * np.pi - C1 - C2))
            m_r2 = []
            for f, (turns_, shift_) in enumerate([(0.25, float(np.float32(np.pi / 2))), (0.0, 0.0)]):
                m1 = ts(DV, TT, ANG, float(1 / (2 * np.pi)), ALU.mult, turns_, ALU.add, m_ang)
                m1 = ts(DV, KK, TT, 12582912.0, ALU.add, None, None, m1)
                m1 = ts(DV, KK, KK, -12582912.0, ALU.add, None, None, m1)
                m1 = stt(RR, KK, -C1, ANG, ALU.mult, ALU.add, m1)
                m1 = stt(RR, KK, -C2, RR, ALU.mult, ALU.add, m1)
                m1 = stt(RR, KK, -C3, RR, ALU.mult, ALU.add, m1)
                m1 = ts(DV, RR, RR, shift_, ALU.add, 3.1415925, ALU.min, m1)
                m1 = ts(DV, RR, RR, -3.1415925, ALU.max, None, None, m1)
                m1 = act(angs[:, 4 + f], RR, ACT.Sin, m1)
                DV.wait(m1)
                if f == 0:
                    for z in range(2):
                        m_r2.append(copy(DV, rope2[:, :, 0, 16 * z:16 * z + 16], angs[:, 4]))
                else:
                    m_r2.append(ts(DV, rope2[:, :, 1, 0:16], angs[:, 5], -1.0, ALU.mult, None, None))
                    m_r2.append(copy(DV, rope2[:, :, 1, 16:32], angs[:, 5]))
            return m_r2

        def token_mix(l, m_h, m_act_free):
            ctx_out = l == 0
            tm = {}

            def bias():
                bb = []
                for q in range(2):
                    for i in range(6):
                        src = bass.AP(rpbs.tensor, 3720 * l + (5 - q + i) * 31 + 15, [[7439, 64], [465, 8], [1, 64]])
                        bb.append(load(f"bb{q}{i}", BB[64 * q:64 * q + 64, :, i, :], src, m_rpb, bb_free[0], list(mrow_free),
                                       bg_free[0], acc_free[0], m_act_free, line=PO))
                tm["bb"] = DV.do(lambda e: e.tensor_tensor(
                    BB.rearrange("p h i c -> p (h i) c"), BB.rearrange("p h i c -> p (h i) c"),
                    cs("colmask").unsqueeze(1).to_broadcast([128, 48, 64]), ALU.add), bb, m_cst)

            s_free = [None, None]
            ZQ = [S[0], S[1]] + [at(PT_AT + 1024 * i, 512) for i in range(2)]
            z_free = [None] * 4

            def to_T(dst, scale, t, b, m):
                q = t % 2
                z = ZQ[t]
                if t < 2:
                    ct = rope[:, t, 0, :].unsqueeze(1).to_broadcast([128, 8, 64])
                    m1 = tt(DV, XN[q][:, 0:512].rearrange("p (h d) -> p h d", h=8),
                            ps[b][:, :].rearrange("p (h d) -> p h d", h=8), ct, ALU.mult, m, xn_free[q], m_cst)
                    pv = ps[b][:, :].rearrange("p (h f d) -> p h f d", h=16, f=2)
                    xv = XN[q][:, 512:1024].rearrange("p (h f d) -> p h f d", h=16, f=2)
                    for f in range(2):
                        st = rope[:, t, 1, :].rearrange("p (r f d) -> p r f d", r=2, f=2)[:, :, f, :]
                        st = st.unsqueeze(1).to_broadcast([128, 8, 2, 16])
                        o4 = xv[:, :, f, :].rearrange("p (h r) d -> p h r d", r=2)
                        i4 = pv[:, :, 1 - f, :].rearrange("p (h r) d -> p h r d", r=2)
                        m2 = tt(DV, o4, i4, st, ALU.mult, m)
                    pfree[b] = m2
                    m = tt(PO, z, XN[q][:, 0:512], XN[q][:, 512:1024], ALU.add, m1, m2, z_free[t], m_act_free)
                    xn_free[q] = m
                else:
                    m = copy(AC, z, ps[b][:, :], m, z_free[t], m_act_free)
                    pfree[b] = m

                def turned():
                    b2 = bank()
                    for k in range(4):
                        m3 = tr(ps[b2][:, 128 * k:128 * k + 128], z[:, 128 * k:128 * k + 128], k == 3, m)
                    z_free[t] = m3
                    m4 = act(dst[:, :, 128 * t:128 * t + 128], ps[b2][:, :].rearrange("p (k t) -> p k t", k=4),
                             ACT.Copy, m3, scale=scale)
                    pfree[b2] = m4
                    tm["qk"] = m4
                later.append(turned)

            def keep(dst, name, t, b, m):
                m = copy(AC, dst[:, t, :], ps[b][:, :], m, m_act_free)
                pfree[b] = m
                tm[name] = m

            both, own = [0, 1, 2, 3], [0, 1]
            AC.wait(m_act_free)
            for g, (tts, ev) in enumerate([
                    (both if ctx_out else own, lambda t, b, m: to_T(QT, 0.125, t, b, m)),
                    (both, lambda t, b, m: to_T(KT, 1.0, t, b, m)),
                    (both, lambda t, b, m: keep(V, "v", t, b, m)),
                    (both if ctx_out else own, lambda t, b, m: keep(UU, "u", t, b, m))]):
                m_pe = project(tts, ev, m_h)
                if g == 0:
                    while side_summed:
                        side_step(side_summed.pop(0)[0])
                    side_finish()
                    bias()
            flush()
            h_free[0] = m_pe
            m_wp = load("wp", WPOOL, a["w_pool"][l].rearrange("g c d -> c g d"), wp_free[0], line=PO)

            items = [(h, qt) for h in range(8) for qt in (range(4) if ctx_out else range(2))]
            SR = [S[0], S[1]] + [XN[i][:, 512 * j:512 * j + 512] for i in range(2) for j in range(2)]
            sr_free = [s_free[0], s_free[1], xn_free[0], xn_free[0], xn_free[1], xn_free[1]]
            st = {}
            pt_free = [z_free[2], z_free[3]]
            s_free[0], s_free[1] = z_free[0], z_free[1]
            pair = {}

            def scores(n):
                h, qt = items[n]
                p0, hp = 64 * (h % 2), h // 2
                b = bank()
                k0 = 0 if qt < 2 else 256
                N = 512 - k0
                m = mm(ps[b][:, 0:N], QT[p0:p0 + 64, hp, 128 * qt:128 * qt + 128], KT[p0:p0 + 64, hp, k0:512],
                       True, True, True, tm["qk"])
                z = SR[n % 6][:, 0:N]
                if qt < 2:
                    i0 = 2 if qt == 0 else 0
                    m1 = DV.do(lambda e: e.tensor_tensor(
                        z[:, 0:256].rearrange("p (i c) -> p i c", i=4),
                        ps[b][:, 0:256].rearrange("p (i c) -> p i c", i=4), BB[:, h, i0:i0 + 4, :], ALU.add),
                        m, tm["bb"], sr_free[n % 6])
                    m2 = copy(DV, z[:, 256:512], ps[b][:, 256:512], m)
                    bb_free[0] = m1
                    pfree[b] = m2
                    src = z
                else:
                    src, m2 = ps[b][:, 0:N], m
                mx, nm, den = col(), col(), col()
                m = red(mx, src, ALU.max, m2)
                m = ts(DV, nm, mx, -1.0, ALU.mult, None, None, m)
                m = act(z, src, ACT.Exp, m, sr_free[n % 6], bias=nm, accum_out=den)
                if qt >= 2:
                    pfree[b] = m
                st[n] = (z, den, m)

            def divide(n):
                z, den, m = st[n]
                rd = col()
                m = recip(rd, den, m)
                st[n] = ts(DV, z, z, rd, ALU.mult, None, None, m)

            def turns(n):
                h, qt = items[n]
                nb = 4 if qt < 2 else 2
                z = SR[n % 6]
                b = bank()
                for k in range(nb):
                    m = tr(ps[b][:, 128 * k:128 * k + 128], z[:, 128 * k:128 * k + 128], k == nb - 1, st[n])
                sr_free[n % 6] = m
                g = n // 2 % 2
                m = copy(AC, PT[g][:, 0:nb, 128 * (qt % 2):128 * (qt % 2) + 128],
                         ps[b][:, 0:128 * nb].rearrange("p (k t) -> p k t", k=nb), m, pt_free[g])
                pfree[b] = m
                st[n] = m

            def values(n):
                h, qt = items[n]
                if qt % 2 == 0:
                    return
                g = n // 2 % 2
                s = qt // 2
                p0 = 64 * (h % 2)
                if h % 2 == 0:
                    pair[s] = bank()
                b = pair[s]
                kb = range(4) if s == 0 else range(2, 4)
                for k in kb:
                    m = mm(ps[b][p0:p0 + 64, 0:256], V[:, k, 64 * h:64 * h + 64], PT[g][:, k - kb[0], :],
                           k == kb[0], k == 3, k == 3, st[n], tm["v"])
                pt_free[g] = m
                if h % 2:
                    o = 256 * s
                    hi, lo = Hhi[:, h // 2, o:o + 256], Hlo[:, h // 2, o:o + 256]
                    m = two_parts(hi, lo, ps[b][:, 0:256], m, h_free[0])
                    pfree[b] = m
                    tm["mix"] = m

            for n in range(len(items) + 5):
                if n < len(items):
                    scores(n)
                if 0 <= n - 1 < len(items):
                    divide(n - 1)
                if 0 <= n - 3 < len(items):
                    turns(n - 3)
                if 0 <= n - 5 < len(items):
                    values(n - 5)
            s_free[0], s_free[1] = sr_free[0], sr_free[1]
            xn_free[0], xn_free[1] = sr_free[2:4], sr_free[4:6]

            T = 512 if ctx_out else 256
            if ctx_out:
                o, n_ = CST["pool_c"]
                m_pc = load("pc", at(PT_AT, 2048), a["cst"][:, o:o + n_], list(pt_free), st[len(items) - 1], line=PO)
                pc = at(PT_AT, 4, 2, 256)
            px = cs("pool_x").rearrange("p (g t) -> p g t", g=4)
            for g in range(4):
                b = bank()
                for t in range(2):
                    m = mm(ps[b][:, 128 * t:128 * t + 128], UU[:, t, 128 * g:128 * g + 128], px[:, g, :],
                           True, True, True, tm["u"], m_cst)
                if ctx_out:
                    for t in range(2):
                        m = mm(ps[b][:, 256:512], UU[:, 2 + t, 128 * g:128 * g + 128], pc[:, g, t, :],
                               t == 0, t == 1, True, m_pc)
                q = g % 2
                z = S[q][:, 0:T]
                m = copy(AC, z, ps[b][:, 0:T], m, s_free[q])
                pfree[b] = m
                b = bank()
                m = mm(ps[b][:, 0:T], WPOOL[:, g, :], z, True, True, True, m, m_wp)
                s_free[q] = m
                wp_free[0] = m
                sc_ = VEC["pool_scale"] + 4 * l + g
                y = XN[q][:, 0:T]
                m = act(y, ps[b][:, 0:T], ACT.Copy, m, xn_free[q], scale=vec[:, sc_:sc_ + 1])
                pfree[b] = m
                m = two_parts(Hhi[:, 4 + g, 0:T], Hlo[:, 4 + g, 0:T], y, m, h_free[0])
                xn_free[q] = m
            return [m, tm["mix"]]

        WPOOL = at(PT_AT + 2048 + 3072, 4, 128)
        wp_free = [None]

        def xs(m0=None):
            return [(X[:, t, :], m0) for t in range(2)]

        tiles_x = xs(m_x)
        tiles_c = [(C[:, t, :], m_c) for t in range(2)]

        def ab(l, v):
            def f(i):
                s, n = 0 if i < 2 else 1, 6 * l + v // 3 * 2
                return mods[:, n + 1, :, s], mods[:, n, :, s], [mods_ready[n], mods_ready[n + 1]]
            return f

        PE.wait(m_sc)
        act_free = None
        tiles = tiles_x + tiles_c
        r1 = []
        for h in range(2):
            advance()
            r1 += plain_rows(1)
            side_step((0, 0, h))
            side_summed.clear()
        side_finish()
        ms = [vector_row(0, 1, h, *r1[h]) for h in range(2)]
        vector_turn(0, 1, 0, ms)
        xn_free[:], g_free[:] = [free[5]] * 2, [free[6]] * 2
        PE.wait(m_cst)
        DV.wait(m_cst)
        diag = first_stats(tiles)
        until[0] = 10
        advance()
        for l in range(2):
            m_h = pre(tiles, diag, ab(l, 0), (1, 2, 1) if l else None)
            if l == 0:
                m_rope2 = rope_tables()
                wp_free[0] = m_rope2[-1]
            parts = gate_up(512, m_h, ACT_AT)
            bs, m_y = down(512, parts)
            act_free = [h_free[0], (DV.sem, DV.n)]
            tiles, diag = post(bs, m_y, tiles, [0, 0, 1, 1])
            m_h = pre(tiles, diag, ab(l, 3), (l, 5, 2 - l))
            m_mix = token_mix(l, m_h, act_free)
            if l == 1:
                tiles = tiles[0:2]
            nt = len(tiles)
            bs, m_y = from_H(8, nt, m_mix)
            tiles, diag = post(bs, m_y, tiles, [0, 0, 1, 1])
            m_h = pre(tiles, diag, ab(l, 6), (l, 8, 2))
            parts = gate_up(128 * nt, m_h, ACT_AT)
            bs, m_y = down(128 * nt, parts)
            tiles, diag = post(bs, m_y, tiles, [0, 0, 1, 1])

        def gain(name, n=0):
            v = vec[:, VEC[name] + 8 * n:VEC[name] + 8 * n + 8]
            return lambda i: (v, None, m_vec)

        def ffn2(n, tiles, diag):
            m_h = pre(tiles, diag, gain("ffn_norm", n))
            bs, my = down(256, gate_up(256, m_h, ACT_AT))
            return post(bs, my, tiles, None)

        m_h = pre(tiles, diag, gain("attn_norm"))
        region_free = [h_free[0], (DV.sem, DV.n), g_ready[0], g_ready[1]]
        Q3, K3, V3 = at(U0, 12, 256), at(U0 + 3072, 12, 256), at(U0 + 6144, 6, 512)
        S3 = [at(MROW + 768 * i, 768) for i in range(4)]
        P3 = [at(1152, 3, 384), at(2304, 3, 384)]
        o_, n_ = CST["causal"]
        m_ca = load("ca", at(0, n_), a["cst"][:, o_:o_ + n_], region_free, (PO.sem, PO.n))
        qk3, v3 = [None], [None]
        s3_free, p3_free = [None] * 4, [None, None]
        attended = [region_free]

        def ev_qk(dst, g, scale, t, b, m):
            q = t % 2
            z = XN[q][:, 0:512]
            z4 = z.rearrange("p (h d) -> p h d", h=4)
            t1 = XN[q][:, 512:640].rearrange("p (h d) -> p h d", h=4)
            t2 = XN[q][:, 640:768].rearrange("p (h d) -> p h d", h=4)
            m = copy(AC, z, ps[b][:, :], m, xn_free[q])
            pfree[b] = m
            cc = rope2[:, t, 0, :].unsqueeze(1).to_broadcast([128, 4, 32])
            m1 = tt(DV, t1, z4[:, :, 0:32], cc, ALU.mult, m, m_rope2)
            for f in range(2):
                sn = rope2[:, t, 1, 16 * f:16 * f + 16].unsqueeze(1).to_broadcast([128, 4, 16])
                m2 = tt(DV, t2[:, :, 16 * f:16 * f + 16], z4[:, :, 16 - 16 * f:32 - 16 * f], sn, ALU.mult, m)
            m = tt(DV, z4[:, :, 0:32], t1, t2, ALU.add, m1, m2)

            def turned():
                b2 = bank()
                for k in range(4):
                    mt = tr(ps[b2][:, 128 * k:128 * k + 128], z[:, 128 * k:128 * k + 128], k == 3, m)
                xn_free[q] = mt
                mt = act(dst[:, 4 * g:4 * g + 4, 128 * t:128 * t + 128],
                         ps[b2][:, :].rearrange("p (k t) -> p k t", k=4), ACT.Copy, mt, attended[0], scale=scale)
                pfree[b2] = mt
                qk3[0] = mt
            later.append(turned)

        def ev_v(g, t, b, m):
            m = copy(AC, V3[:, 2 * g + t, :], ps[b][:, :], m, attended[0])
            pfree[b] = m
            v3[0] = m

        def attend(half):
            items = [(h, qt) for h in range(4) for qt in range(2)]
            st = {}
            ca = at(0, 1152)

            def scores(n):
                h, qt = items[n]
                w = 128 * (qt + 1)
                z = S3[n % 4][:, 0:3 * w]
                ms = [s3_free[n % 4], m_ca]
                for gs in ((0, 1, 2),) if qt == 0 else ((0, 1), (2,)):
                    b = bank()
                    for i, g in enumerate(gs):
                        m = mm(ps[b][:, w * i:w * i + w], Q3[:, 4 * g + h, 128 * qt:128 * qt + 128],
                               K3[:, 4 * g + h, 0:w], True, True, True, qk3[0])
                    o = 384 * qt + w * gs[0]
                    m = tt(DV, z[:, w * gs[0]:w * gs[0] + w * len(gs)], ps[b][:, 0:w * len(gs)],
                           ca[:, o:o + w * len(gs)], ALU.add, m, ms)
                    pfree[b] = m
                mx, nm, den = col(), col(), col()
                m = red(mx, z, ALU.max, m)
                m = ts(DV, nm, mx, -1.0, ALU.mult, None, None, m)
                m = act(z, z, ACT.Exp, m, bias=nm, accum_out=den)
                st[n] = (z, den, m)

            def divide(n):
                z, den, m = st[n]
                rd = col()
                m = recip(rd, den, m)
                st[n] = ts(DV, z, z, rd, ALU.mult, None, None, m)

            def turns(n):
                h, qt = items[n]
                z = S3[n % 4]
                pt = P3[n // 2 % 2]
                f = p3_free[n // 2 % 2]
                if qt == 0:
                    b = bank()
                    for g in range(3):
                        m = tr(ps[b][:, 128 * g:128 * g + 128], z[:, 128 * g:128 * g + 128], g == 2, st[n])
                    s3_free[n % 4] = m
                    m = copy(AC, pt[:, :, 0:128], ps[b][:, 0:384].rearrange("p (g t) -> p g t", g=3), m, f)
                    pfree[b] = m
                else:
                    for gs in ((0, 1), (2,)):
                        b = bank()
                        for i, g in enumerate(gs):
                            for k in range(2):
                                o = 256 * i + 128 * k
                                m = tr(ps[b][:, o:o + 128], z[:, 256 * g + 128 * k:256 * g + 128 * k + 128],
                                       True, st[n])
                        s3_free[n % 4] = m
                        m = copy(AC, pt[:, gs[0]:gs[0] + len(gs), 128:384],
                                 ps[b][:, 0:256 * len(gs)].rearrange("p (g t) -> p g t", g=len(gs)), m, f)
                        pfree[b] = m
                st[n] = m

            def values(n):
                h, qt = items[n]
                if qt == 0:
                    return
                pt = P3[n // 2 % 2]
                b = bank()
                o = ps[b][:, 0:256]
                for g in range(3):
                    mm(o, V3[:, 2 * g, 128 * h:128 * h + 128], pt[:, g, 0:256], g == 0, False, False, st[n], v3[0])
                    m = mm(ps[b][:, 128:256], V3[:, 2 * g + 1, 128 * h:128 * h + 128], pt[:, g, 256:384],
                           False, g == 2, g == 2)
                p3_free[n // 2 % 2] = m
                hh = 4 * half + h
                mo = two_parts(Hhi[:, hh, 256:512], Hlo[:, hh, 256:512], o, m, h_free[0])
                pfree[b] = mo
                return mo, m

            for n in range(len(items) + 4):
                if n < len(items):
                    scores(n)
                if 0 <= n - 1 < len(items):
                    divide(n - 1)
                if 0 <= n - 2 < len(items):
                    turns(n - 2)
                if 0 <= n - 4 < len(items):
                    r_ = values(n - 4)
                    if r_:
                        mo, m_ = r_
            attended[0] = m_
            return mo

        for half in range(2):
            for g in range(3):
                project([0, 1], lambda t, b, m: ev_qk(Q3, g, 128.0 ** -0.5, t, b, m), m_h)
                project([0, 1], lambda t, b, m: ev_qk(K3, g, 1.0, t, b, m))
                project([0, 1], lambda t, b, m: ev_v(g, t, b, m))
            flush()
            m_o = attend(half)
        bs, m_y = from_H(8, 2, m_o, 256)
        tiles, diag = post(bs, m_y, tiles, None)
        tiles, diag = ffn2(0, tiles, diag)

        QK = at(U0, 8, 256)
        VM, OG, HO = at(U0 + 2048, 2, D), at(U0 + 4096, 2, D), at(U0 + 6144, 2, D)
        XP = [at(U0 + 8192, 260), at(U0 + 8452, 260)]
        CV = [at(U0 + 8712, 256), at(U0 + 8968, 256)]
        R0, R1 = [at(U0 + 9224 + 384 * i, 128) for i in range(2)], [at(U0 + 9352 + 384 * i, 256) for i in range(2)]
        DW = [at(U0 + 9992 + 384 * i, 384) for i in range(8)]
        assert U0 + 9992 + 8 * 384 <= AR
        SS = [at(768 + 384 * i, 384) for i in range(2)]
        ST = [at(1536 + 384 * i, 384) for i in range(2)]
        SQ = at(2304, D)
        GT = at(3328, 16, 2, 8)
        GB = at(3584, 16)
        Fs = at(3600, 2, 8)
        m_free = [h_free[0], (DV.sem, DV.n), (AC.sem, AC.n)]
        m_gb = [load("gb0", GB[:, 0:8], bass.AP(a["mlstm_ig_bias_2"].tensor, 0, [[0, 128], [1, 8]]), m_free),
                load("gb1", GB[:, 8:16], bass.AP(a["mlstm_fg_bias_2"].tensor, 0, [[0, 128], [1, 8]]), m_free)]
        m_h = pre(tiles, diag, gain("mlstm_norm"))
        m_z = [ts(DV, XP[i][:, 0:3], vec[:, 0:3], 0.0, ALU.mult, None, None, m_free) for i in range(2)]
        AC.wait(m_free)
        xp_free, cv_free = [None, None], [None, None]
        PE.wait(m_h)
        hi, lo = unit(8, 16)
        b = bank()
        for t in range(2):
            for k in range(8):
                m = mm3(ps[b][:, 16 * t:16 * t + 16], (Hhi[:, k, 128 * t:128 * t + 128],
                                                      Hlo[:, k, 128 * t:128 * t + 128]),
                        (hi[:, k, :], lo[:, k, :]), k == 0, k == 7, mark=(k == 7))
        unit_done(m)
        gv = ps[b][:, 0:32].rearrange("p (t g) -> p t g", t=2)
        IG, FG, NFG, AF, E, UE, DE, RU, LN, CO, MF, LF = [GT[:, i, :, :] for i in range(12)]
        gbb = lambda c0: GB[:, c0:c0 + 8].unsqueeze(1).to_broadcast([128, 2, 8])
        m_ig = tt(DV, IG, gv[:, :, 0:8], gbb(0), ALU.add, m, m_gb, m_free)
        m = tt(DV, FG, gv[:, :, 8:16], gbb(8), ALU.add)
        pfree[b] = m
        m = ts(DV, NFG, FG, -1.0, ALU.mult, None, None, m)
        m = tt(DV, AF, FG, NFG, ALU.max, m)
        m_f = ts(DV, MF, FG, 0.0, ALU.min, None, None)
        m = act(E, AF, ACT.Exp, m, scale=-1.0)
        m = ts(DV, UE, E, 1.0, ALU.add, None, None, m)
        m_l = act(LN, UE, ACT.Ln, m)
        m = ts(DV, DE, UE, -1.0, ALU.add, None, None, m)
        m = tt(DV, CO, E, DE, ALU.subtract, m)
        m1 = recip(RU, UE)
        m = tt(DV, CO, CO, RU, ALU.mult, m, m1)
        m = tt(DV, LN, LN, CO, ALU.add, m, m_l)
        m_lf = tt(DV, LF, MF, LN, ALU.subtract, m, m_f)
        for j in range(4):
            hi, lo = unit(8, 256)
            b2 = []
            for s in range(2):
                b = bank()
                for k in range(8):
                    m = mm3(ps[b][:, 0:256], (hi[:, k, 128 * s:128 * s + 128], lo[:, k, 128 * s:128 * s + 128]),
                            (Hhi[:, k, 0:256], Hlo[:, k, 0:256]), k == 0, k == 7, mark=(k == 7))
                b2.append((b, m))
            for s, (b, mb) in enumerate(b2):
                c_ = 2 * j + s
                xp, cv = XP[s], CV[s]
                mc = copy(AC, xp[:, 3:259], ps[b][:, 0:256], mb, xp_free[s])
                pfree[b] = mc
                w = lambda i: vec[:, VEC["conv_w"] + 8 * i + c_:VEC["conv_w"] + 8 * i + c_ + 1]
                bi = vec[:, VEC["conv_b"] + c_:VEC["conv_b"] + c_ + 1]
                mc = ts(DV, cv, xp[:, 3:259], w(3), ALU.mult, bi, ALU.add, mc, m_z, cv_free[s])
                for i in range(3):
                    mc = stt(cv, xp[:, i:i + 256], w(i), cv, ALU.mult, ALU.add, mc)
                xp_free[s] = mc
                m_qk = act(QK[:, c_, :], cv, ACT.Silu, mc)
                cv_free[s] = m_qk
            unit_done(m)
        def ev_vo(dst, f, j, t, b, m):
            m = act(dst[:, t, 512 * j:512 * j + 512], ps[b][:, :], f, m)
            pfree[b] = m
            return m

        b = bank()
        mm(ps[b][:, 0:8], cs("upto"), LF[:, 0, :], True, True, True, m_lf, m_cst)
        mm(ps[b][:, 8:16], cs("upto"), LF[:, 1, :], True, False)
        m = mm(ps[b][:, 8:16], cs("ones"), LF[:, 0, :], False, True)
        m_F = copy(DV, Fs, ps[b][:, 0:16].rearrange("p (t h) -> p t h", t=2), m)
        pfree[b] = m_F
        r_free, ss_free, stt_free = [None, None], [None, None], [None, None]
        ssq = col(16)
        decay, st = {}, {}

        def rows_of(h):
            q = h % 2
            rf = r_free[q]
            lf, ig = (lambda t: LF[:, t, h:h + 1]), (lambda t: IG[:, t, h:h + 1])
            m = ts(DV, R0[q], cs("after"), lf(0), ALU.mult, None, None, m_lf, rf)
            m = stt(R0[q], ident(), ig(0), R0[q], ALU.mult, ALU.add, m, m_ig)
            ma = ts(DV, R1[q][:, 0:128], cs("ones"), lf(1), ALU.mult, None, None)
            mb = ts(DV, R1[q][:, 128:256], cs("after"), lf(1), ALU.mult, None, None)
            mb = stt(R1[q][:, 128:256], ident(), ig(1), R1[q][:, 128:256], ALU.mult, ALU.add, mb)
            decay[h] = [m, ma, mb]

        def weights(h):
            q = h % 2
            b = bank()
            mm(ps[b][:, 0:128], cs("upto"), R0[q], True, True, True, decay[h])
            mm(ps[b][:, 128:384], cs("upto"), R1[q], True, False)
            m = mm(ps[b][:, 128:256], cs("ones"), R0[q], False, True)
            r_free[q] = m
            d = DW[h]
            nv = cs("never")
            m1 = tt(DV, d[:, 0:128], ps[b][:, 0:128], nv, ALU.add, m)
            m2 = copy(DV, d[:, 128:256], ps[b][:, 128:256])
            m3 = tt(DV, d[:, 256:384], ps[b][:, 256:384], nv, ALU.add)
            pfree[b] = m3
            mx, nm, en = col(2), col(2), col(2)
            ma = red(mx[:, 0:1], d[:, 0:128], ALU.max, m1)
            mb = red(mx[:, 1:2], d[:, 128:384], ALU.max, m2, m3)
            m = tt(DV, mx, mx, Fs[:, :, h], ALU.max, ma, mb, m_F)
            m = ts(DV, nm, mx, -1.0, ALU.mult, None, None, m)
            act(d[:, 0:128], d[:, 0:128], ACT.Exp, m, bias=nm[:, 0:1])
            act(d[:, 128:384], d[:, 128:384], ACT.Exp, bias=nm[:, 1:2])
            decay[h] = (en, act(en, nm, ACT.Exp))

        def scored(h):
            q = h % 2
            d = DW[h]
            en, m_w = decay[h]
            b = bank()
            p0, c_ = 64 * (h % 2), h // 2
            mm(ps[b][:, 0:128], QK[p0:p0 + 64, c_, 0:128], QK[p0:p0 + 64, 4 + c_, 0:128], True, True, True, m_qk)
            m = mm(ps[b][:, 128:384], QK[p0:p0 + 64, c_, 128:256], QK[p0:p0 + 64, 4 + c_, 0:256])
            den, nd, rd = col(2), col(2), col(2)
            s_ = SS[q]
            m1 = stt(s_[:, 0:128], ps[b][:, 0:128], 0.125, d[:, 0:128], ALU.mult, ALU.mult, m, m_w, ss_free[q],
                     acc=den[:, 0:1])
            m2 = stt(s_[:, 128:384], ps[b][:, 128:384], 0.125, d[:, 128:384], ALU.mult, ALU.mult,
                     acc=den[:, 1:2])
            pfree[b] = m2
            m = ts(DV, nd, den, -1.0, ALU.mult, None, None, m1, m2)
            m = tt(DV, den, den, nd, ALU.max, m)
            m = tt(DV, den, den, en, ALU.max, m)
            m_rd = recip(rd, den, m)
            st[h] = (m2, rd, m_rd)

        def turned_scores(h):
            q = h % 2
            m2, rd, m_rd = st[h]
            b = bank()
            for k in range(3):
                m = tr(ps[b][:, 128 * k:128 * k + 128], SS[q][:, 128 * k:128 * k + 128], k == 2, m2)
            ss_free[q] = m
            m = copy(AC, ST[q], ps[b][:, 0:384], m, stt_free[q])
            pfree[b] = m
            st[h] = (m, rd, m_rd)

        def outs(h):
            q = h % 2
            m, rd, m_rd = st[h]
            b = bank()
            c_ = slice(128 * h, 128 * h + 128)
            mm(ps[b][:, 0:128], ST[q][:, 0:128], VM[:, 0, c_], True, True, True, m, mv)
            mm(ps[b][:, 128:256], ST[q][:, 256:384], VM[:, 1, c_], True, False)
            m = mm(ps[b][:, 128:256], ST[q][:, 128:256], VM[:, 0, c_], False, True)
            stt_free[q] = m
            for t in range(2):
                m1 = ts(DV, HO[:, t, c_], ps[b][:, 128 * t:128 * t + 128], rd[:, t:t + 1], ALU.mult, None, None,
                        m, m_rd)
                m2 = act(SQ[:, 128 * t:128 * t + 128], HO[:, t, c_], ACT.Square, m1, sq_free[t],
                         accum_out=ssq[:, 8 * t + h:8 * t + h + 1])
                sq_free[t] = m2
            pfree[b] = m1
            return m1, m2

        sq_free = [None, None]
        mv = []
        rows_of(0)
        rows_of(1)
        for j in range(4):
            dst, f, half = (VM, ACT.Copy, j) if j < 2 else (OG, ACT.Sigmoid, j - 2)
            m_pe = project([0, 1], lambda t, b, m: mv.append(ev_vo(dst, f, half, t, b, m)))
            for h in (2 * j, 2 * j + 1):
                weights(h)
            for h in (2 * j + 2, 2 * j + 3):
                if h < 8:
                    rows_of(h)
        h_free[0] = m_pe
        for h in range(10):
            if h < 8:
                scored(h)
            if 0 <= h - 1 < 8:
                turned_scores(h - 1)
            if 0 <= h - 2 < 8:
                m_ho, m_sq = outs(h - 2)
        r, m_r = rstd(ssq, 16, 1.0 / 128, m_sq)
        for t in range(2):
            for h in range(8):
                ho = HO[:, t, 128 * h:128 * h + 128]
                m = stt(ho, ho, r[:, 8 * t + h:8 * t + h + 1], OG[:, t, 128 * h:128 * h + 128], ALU.mult, ALU.mult,
                        m_r, m_ho, mv)
            g_, _, mg_ = gain("head_gain")(0)
            turn(t, HO[:, t, :], m, 128 * t, g_, None, mg_)
        m_h = turn_end()
        bs, m_y = from_H(8, 2, m_h)
        tiles, diag = post(bs, m_y, tiles, None)
        tiles, diag = ffn2(1, tiles, diag)
        m_fn = load("fn", G[0], bass.AP(a["final_norm_2"].tensor, 0, [[0, 128], [1, D]]), g_free[0])
        for t, (x_, m_) in enumerate(tiles):
            m = stt(XN[t], x_, diag[t][0], G[0], ALU.mult, ALU.mult, diag[t][1], m_fn, xn_free[t])
            load(f"out{t}", out[0, 128 * t:128 * t + 128, :], XN[t], m)

        for s, n in dsems.values():
            SP.wait((s, n))
        for ln in (PE, DV, AC, PO):
            SP.wait((ln.sem, ln.n))
        block = ctx.enter_context(nc.Block())

        @block.sync
        def _(e):
            SP.emit(e)

        @block.tensor
        def _(e):
            PE.emit(e)

        @block.vector
        def _(e):
            DV.emit(e)

        @block.scalar
        def _(e):
            AC.emit(e)

        @block.gpsimd
        def _(e):
            PO.emit(e)


def tables():
    f = np.float32
    c = np.zeros((128, NCST), f)

    def put(name, v):
        o, n = CST[name]
        c[:v.shape[0], o:o + n] = v.reshape(v.shape[0], n)

    put("ident", np.eye(128, dtype=f))
    tok = np.arange(256)
    inv = f(10000.0) ** (-np.arange(16, dtype=f) / f(16))
    t = np.zeros((256, 2, 2, 2, 16), f)
    for i, pos in enumerate((tok // 64, tok % 64)):
        ang = pos.astype(f)[:, None] * inv
        t[:, 0, i, 0], t[:, 0, i, 1] = np.cos(ang), np.cos(ang)
        t[:, 1, i, 0], t[:, 1, i, 1] = -np.sin(ang), np.sin(ang)
    put("rope", t.reshape(2, 128, 128).transpose(1, 0, 2).copy())
    j = np.arange(64)
    start = np.clip(j - 8, 0, 48)
    ok = (j[None] >= start[:, None]) & (j[None] < start[:, None] + 16)
    put("colmask", np.tile(np.where(ok, f(0), f(NEG)), (2, 1)).astype(f))

    def window(n, w):
        q = np.arange(n)
        lo, hi = np.clip(q - w // 2, 0, n), np.clip(q - w // 2 + w, 0, n)
        m = ((q[:, None] >= lo[None]) & (q[:, None] < hi[None])) / (hi - lo)[None]
        return (m - np.eye(n)).astype(f)

    px = np.zeros((128, 4, 128), f)
    pc = np.zeros((128, 4, 2, 256), f)
    for g, w in enumerate((2, 4, 8, 16)):
        for r in range(2):
            px[64 * r:64 * r + 64, g, 64 * r:64 * r + 64] = window(64, w)
        pc[:, g] = window(256, w).reshape(2, 128, 256).transpose(1, 0, 2)
    put("pool_x", px)
    put("pool_c", pc)
    i, k = np.arange(256)[:, None], np.arange(256)[None]
    ca = np.zeros((128, 1152), f)
    for g, (window_, dil) in enumerate(((128, 1), (512, 4), (2048, 16))):
        ok = (k <= i) & ((i - k) % dil == 0) & ((i - k) // dil <= window_ // dil)
        m = np.where(ok, f(0), f(NEG))
        ca[:, 128 * g:128 * g + 128] = m[0:128, 0:128]
        ca[:, 384 + 256 * g:384 + 256 * g + 256] = m[128:256]
    put("causal", ca)
    u, v = np.arange(128)[:, None], np.arange(128)[None]
    put("upto", (u <= v).astype(f))
    put("after", (u > v).astype(f))
    put("ones", np.ones((128, 128), f))
    put("never", np.where(v > u, f(NEG), f(0)).astype(f))
    sel = np.zeros((2, 2, 128), f)
    sel[0, 0], sel[1, 1] = 1, 1
    put("sel", sel)
    pick = np.zeros((128, 2, 2), f)
    pick[:, 0, 0], pick[:, 1, 1] = 1, 1
    put("pick", pick)
    put("freq", np.tile(f(500000.0) ** (-np.arange(16, dtype=f) * f(2.0) / f(32)), (128, 1)))
    return c


def lay_out(inputs):
    x = {k: np.ascontiguousarray(np.asarray(v)) for k, v in inputs.items()}

    def cols(v):
        return v.reshape(-1, 128).T

    parts = [x["c"], x["c_ctx"], x["norm_g"], x["b_mod"], x["pool_scale"], x["attn_norm_2"], x["mlstm_norm_2"],
             x["ffn_norm_2"], x["mlstm_head_gain_2"], x["mlstm_conv_b_2"], x["mlstm_conv_w_2"]]
    arrays = {n: x[n] for n in BIG}
    arrays["vec"] = np.ascontiguousarray(np.concatenate([cols(p) for p in parts], axis=1))
    arrays["cst"] = tables()
    return arrays


BIG = ["x", "ctx", "w_mod", "b_mod", "norm_g", "w_ffn_gate_up", "w_ffn_down", "w_in", "w_out", "na_rpb", "w_pool",
       "positions_2", "attn_w_in_2", "attn_w_out_2", "mlstm_w_in_2", "mlstm_ig_bias_2", "mlstm_fg_bias_2",
       "mlstm_w_out_2", "ffn_w_in_2", "ffn_w_out_2", "final_norm_2"]


def kernel(**inputs):
    import concourse.bacc as bacc
    from concourse.bass_utils import run_bass_kernel_spmd

    nc = bacc.Bacc("TRN2", target_bir_lowering=False, num_devices=1)
    arrays = lay_out(inputs)
    args = {n: nc.dram_tensor(f"in_{n}", v.shape, mybir.dt.from_np(v.dtype), kind="ExternalInput").ap()
            for n, v in arrays.items()}
    out = nc.dram_tensor("out_0", (1, 256, D), F32, kind="ExternalOutput").ap()
    build(nc, args, out)
    r = run_bass_kernel_spmd(nc, [{f"in_{n}": v for n, v in arrays.items()}], core_ids=[0])
    return r.results[0]["out_0"]
```
